# Optimizing a Trainium2 kernel written in Bass

```python
import jax, jax.numpy as jnp
from jax import lax
import numpy as np

D_MODEL = 2048
BATCH = 1
SEQ = 256
DEPTH = 1

GRID_W = 64
CTX_LEN = 256

D_MIX = D_MODEL
HEAD_DIM = 128
D_ATTN = D_MIX // 2
N_Q_HEADS = D_ATTN // HEAD_DIM
N_KV_HEADS = 2
Q_PER_KV = N_Q_HEADS // N_KV_HEADS
D_KV = N_KV_HEADS * HEAD_DIM
WINDOW = 128
BLOCK = 128
D_GMLP = D_MIX // 4
N_GMLP_HEADS = D_GMLP // HEAD_DIM
GMLP_CHUNK = 128
D_CONV = D_MIX - D_ATTN - D_GMLP
CONV_WIDTH = 31
Q_END = D_ATTN
K_END = Q_END + D_KV
V_END = K_END + D_KV
G_END = V_END + 2 * D_GMLP
D_IN = G_END + 2 * D_CONV

N_EXPERTS = 16
N_EXPERT_GROUPS = 4
EXPERTS_PER_GROUP = N_EXPERTS // N_EXPERT_GROUPS
TOP_K = 2
D_EXPERT = 1024

ROPE_THETA = 10000.0
EPS = 1e-6
NEG_INF = -1e30

kernel_name = 'hybrid_parallel_heads_dit_block'

def rmsnorm(x, g):
    xf = x.astype(jnp.float32)
    y = xf * lax.rsqrt(jnp.mean(xf * xf, axis=-1, keepdims=True) + EPS)
    return (y * g.astype(jnp.float32)).astype(x.dtype)

def layernorm(x, g, b):
    xf = x.astype(jnp.float32)
    mu = jnp.mean(xf, axis=-1, keepdims=True)
    xc = xf - mu
    var = jnp.mean(xc * xc, axis=-1, keepdims=True)
    y = xc * lax.rsqrt(var + EPS) * g.astype(jnp.float32) + b.astype(jnp.float32)
    return y.astype(x.dtype)

def modulate(x, shift, scale):
    return x * (1 + scale) + shift

def axial_rope_tables(n_tokens):
    rows = n_tokens // GRID_W
    row = jnp.repeat(jnp.arange(rows, dtype=jnp.float32), GRID_W)
    col = jnp.tile(jnp.arange(GRID_W, dtype=jnp.float32), rows)
    n_freq = HEAD_DIM // 4
    inv_freq = ROPE_THETA ** (-jnp.arange(n_freq, dtype=jnp.float32) / n_freq)
    ang = jnp.concatenate([row[:, None] * inv_freq, col[:, None] * inv_freq], axis=-1)
    return jnp.cos(ang)[None, :, None, :], jnp.sin(ang)[None, :, None, :]

def apply_rope(x, cos, sin):
    cos = cos.astype(x.dtype)
    sin = sin.astype(x.dtype)
    x1, x2 = x[..., :HEAD_DIM // 2], x[..., HEAD_DIM // 2:]
    return jnp.concatenate([x1 * cos - x2 * sin, x1 * sin + x2 * cos], axis=-1)

def split_heads(z, n_heads):
    return z.reshape(z.shape[0], z.shape[1], n_heads, HEAD_DIM)

def kv_heads(z_kv, k_g):
    k = rmsnorm(split_heads(z_kv[..., :D_KV], N_KV_HEADS), k_g)
    v = split_heads(z_kv[..., D_KV:], N_KV_HEADS)
    return k, v

def window_attention(q, k, v, k_c, v_c, sink):
    B, S = q.shape[0], q.shape[1]
    nb = S // BLOCK
    scale = HEAD_DIM ** -0.5
    qb = q.reshape(B, nb, BLOCK, N_KV_HEADS, Q_PER_KV, HEAD_DIM)
    pad = ((0, 0), (BLOCK, BLOCK), (0, 0), (0, 0))
    kp = jnp.pad(k, pad).reshape(B, nb + 2, BLOCK, N_KV_HEADS, HEAD_DIM)
    vp = jnp.pad(v, pad).reshape(B, nb + 2, BLOCK, N_KV_HEADS, HEAD_DIM)
    kb = jnp.concatenate([kp[:, :-2], kp[:, 1:-1], kp[:, 2:]], axis=2)
    vb = jnp.concatenate([vp[:, :-2], vp[:, 1:-1], vp[:, 2:]], axis=2)
    s_loc = jnp.einsum('bnqhgd,bnkhd->bhgnqk', qb, kb).astype(jnp.float32) * scale
    qpos = jnp.arange(nb)[:, None] * BLOCK + jnp.arange(BLOCK)[None, :]
    kpos = (jnp.arange(nb)[:, None] - 1) * BLOCK + jnp.arange(3 * BLOCK)[None, :]
    valid = ((jnp.abs(kpos[:, None, :] - qpos[:, :, None]) <= WINDOW)
             & (kpos[:, None, :] >= 0) & (kpos[:, None, :] < S))
    s_loc = jnp.where(valid, s_loc, NEG_INF)
    s_ctx = jnp.einsum('bnqhgd,blhd->bhgnql', qb, k_c).astype(jnp.float32) * scale
    s_sink = jnp.broadcast_to(sink.astype(jnp.float32).reshape(N_KV_HEADS, Q_PER_KV)[None, :, :, None, None, None],
                              s_loc.shape[:-1] + (1,))
    p = jax.nn.softmax(jnp.concatenate([s_loc, s_ctx, s_sink], axis=-1), axis=-1)
    n_loc = 3 * BLOCK
    n_ctx = k_c.shape[1]
    p_loc = p[..., :n_loc].astype(v.dtype)
    p_ctx = p[..., n_loc:n_loc + n_ctx].astype(v.dtype)
    o = (jnp.einsum('bhgnqk,bnkhd->bnqhgd', p_loc, vb)
         + jnp.einsum('bhgnql,blhd->bnqhgd', p_ctx, v_c))
    return o.reshape(B, S, N_Q_HEADS * HEAD_DIM)

def context_attention(q_c, k_c, v_c, sink):
    B, L = q_c.shape[0], q_c.shape[1]
    scale = HEAD_DIM ** -0.5
    qg = q_c.reshape(B, L, N_KV_HEADS, Q_PER_KV, HEAD_DIM)
    s = jnp.einsum('blhgd,bmhd->bhglm', qg, k_c).astype(jnp.float32) * scale
    s_sink = jnp.broadcast_to(sink.astype(jnp.float32).reshape(N_KV_HEADS, Q_PER_KV)[None, :, :, None, None],
                              s.shape[:-1] + (1,))
    p = jax.nn.softmax(jnp.concatenate([s, s_sink], axis=-1), axis=-1)
    o = jnp.einsum('bhglm,bmhd->blhgd', p[..., :L].astype(v_c.dtype), v_c)
    return o.reshape(B, L, N_Q_HEADS * HEAD_DIM)

def chunk_gmlp(z, ln_g, ln_b, w_s, b_s):
    B, T = z.shape[0], z.shape[1]
    z = jax.nn.gelu(z)
    u, v = z[..., :D_GMLP], z[..., D_GMLP:]
    v = layernorm(v, ln_g, ln_b)
    vc = v.reshape(B, T // GMLP_CHUNK, GMLP_CHUNK, N_GMLP_HEADS, HEAD_DIM)
    mixed = jnp.einsum('hpq,bnqhd->bnphd', w_s, vc) + b_s.T[:, :, None]
    return u * mixed.reshape(B, T, D_GMLP)

def conformer_conv(z, w_dw, b_dw, ln_g, ln_b):
    a, g = z[..., :D_CONV], z[..., D_CONV:]
    y = a * jax.nn.sigmoid(g)
    y = lax.conv_general_dilated(y, w_dw[:, None, :].astype(y.dtype), window_strides=(1,),
                                 padding=((CONV_WIDTH // 2, CONV_WIDTH // 2),),
                                 dimension_numbers=('NWC', 'WIO', 'NWC'),
                                 feature_group_count=D_CONV) + b_dw
    return jax.nn.silu(layernorm(y, ln_g, ln_b))

def grouped_moe(x, w_router, router_bias, w_gate, w_up, w_down):
    B, T = x.shape[0], x.shape[1]
    scores = jax.nn.sigmoid((x @ w_router).astype(jnp.float32))
    sel = scores + router_bias.astype(jnp.float32)
    grp = sel.reshape(B, T, N_EXPERT_GROUPS, EXPERTS_PER_GROUP)
    grp_score = lax.top_k(grp, 2)[0].sum(axis=-1)
    gmask = jax.nn.one_hot(jnp.argmax(grp_score, axis=-1), N_EXPERT_GROUPS, dtype=jnp.bool_)
    masked = jnp.where(jnp.repeat(gmask, EXPERTS_PER_GROUP, axis=-1), sel, NEG_INF)
    _, idx = lax.top_k(masked, TOP_K)
    chosen = jnp.take_along_axis(scores, idx, axis=-1)
    gates = chosen / jnp.sum(chosen, axis=-1, keepdims=True)
    combine = jnp.einsum('btk,btke->bte', gates, jax.nn.one_hot(idx, N_EXPERTS, dtype=jnp.float32)).astype(x.dtype)
    y = jnp.zeros_like(x)
    for e in range(N_EXPERTS):
        h = jax.nn.silu(x @ w_gate[e]) * (x @ w_up[e])
        y = y + combine[..., e:e + 1] * (h @ w_down[e])
    return y

def setup_inputs(seed: int = 0) -> dict:
    key = jax.random.key(seed)
    ks = jax.random.split(key, 26)
    f32 = jnp.float32
    D = D_MODEL

    def nrm(k, shape, s):
        return jax.random.normal(k, shape, f32) * s

    return {
        'x': nrm(ks[0], (BATCH, SEQ, D), 1.0),
        'c': nrm(ks[1], (BATCH, D), 1.0),
        'ctx': nrm(ks[2], (BATCH, CTX_LEN, D), 1.0),
        'c_ctx': nrm(ks[3], (D,), 1.0),
        'w_mod': nrm(ks[4], (DEPTH, D, 6 * D), 0.5 * D ** -0.5),
        'b_mod': nrm(ks[5], (DEPTH, 6 * D), 0.02),
        'norm_mix_g': 1.0 + nrm(ks[6], (DEPTH, D), 0.02),
        'norm_ffn_g': 1.0 + nrm(ks[7], (DEPTH, D), 0.02),
        'w_in': nrm(ks[8], (DEPTH, D, D_IN), D ** -0.5),
        'w_out': nrm(ks[9], (DEPTH, D_MIX, D), D_MIX ** -0.5),
        'q_norm_g': 1.0 + nrm(ks[10], (DEPTH, HEAD_DIM), 0.02),
        'k_norm_g': 1.0 + nrm(ks[11], (DEPTH, HEAD_DIM), 0.02),
        'attn_sink': nrm(ks[12], (DEPTH, N_Q_HEADS), 0.5),
        'gmlp_ln_g': 1.0 + nrm(ks[13], (DEPTH, D_GMLP), 0.02),
        'gmlp_ln_b': nrm(ks[14], (DEPTH, D_GMLP), 0.02),
        'gmlp_w_s': nrm(ks[15], (DEPTH, N_GMLP_HEADS, GMLP_CHUNK, GMLP_CHUNK), GMLP_CHUNK ** -0.5),
        'gmlp_b_s': 1.0 + nrm(ks[16], (DEPTH, N_GMLP_HEADS, GMLP_CHUNK), 0.02),
        'conv_w': nrm(ks[17], (DEPTH, CONV_WIDTH, D_CONV), CONV_WIDTH ** -0.5),
        'conv_b': nrm(ks[18], (DEPTH, D_CONV), 0.02),
        'conv_ln_g': 1.0 + nrm(ks[19], (DEPTH, D_CONV), 0.02),
        'conv_ln_b': nrm(ks[20], (DEPTH, D_CONV), 0.02),
        'w_router': nrm(ks[21], (D, N_EXPERTS), D ** -0.5),
        'router_bias': nrm(ks[22], (N_EXPERTS,), 0.01),
        'w_gate': nrm(ks[23], (DEPTH, N_EXPERTS, D, D_EXPERT), D ** -0.5),
        'w_up': nrm(ks[24], (DEPTH, N_EXPERTS, D, D_EXPERT), D ** -0.5),
        'w_down': nrm(ks[25], (DEPTH, N_EXPERTS, D_EXPERT, D), D_EXPERT ** -0.5),
    }

def reference(x, c, ctx, c_ctx, w_mod, b_mod, norm_mix_g, norm_ffn_g, w_in, w_out, q_norm_g, k_norm_g,
              attn_sink, gmlp_ln_g, gmlp_ln_b, gmlp_w_s, gmlp_b_s, conv_w, conv_b, conv_ln_g, conv_ln_b,
              w_router, router_bias, w_gate, w_up, w_down):
    L = ctx.shape[1]
    cos, sin = axial_rope_tables(x.shape[1])
    silu_c = jax.nn.silu(c)
    silu_cc = jax.nn.silu(c_ctx)
    h_l, h_c = x, ctx
    for layer in range(DEPTH):
        last = layer == DEPTH - 1
        w_in_l = w_in[layer]
        mod_l = jnp.split((silu_c @ w_mod[layer] + b_mod[layer])[:, None, :], 6, axis=-1)
        mod_c = jnp.split(silu_cc @ w_mod[layer] + b_mod[layer], 6, axis=-1)

        n_l = modulate(rmsnorm(h_l, norm_mix_g[layer]), mod_l[0], mod_l[1])
        n_c = modulate(rmsnorm(h_c, norm_mix_g[layer]), mod_c[0], mod_c[1])
        z_l = n_l @ w_in_l
        if last:
            z_c = n_c @ w_in_l[:, Q_END:V_END]
            kv_c = z_c
        else:
            z_c = n_c @ w_in_l
            kv_c = z_c[..., Q_END:V_END]
        k_c, v_c = kv_heads(kv_c, k_norm_g[layer])

        q_l = apply_rope(rmsnorm(split_heads(z_l[..., :Q_END], N_Q_HEADS), q_norm_g[layer]), cos, sin)
        k_l, v_l = kv_heads(z_l[..., Q_END:V_END], k_norm_g[layer])
        k_l = apply_rope(k_l, cos, sin)
        attn_l = window_attention(q_l, k_l, v_l, k_c, v_c, attn_sink[layer])
        gm_l = chunk_gmlp(z_l[..., V_END:G_END], gmlp_ln_g[layer], gmlp_ln_b[layer], gmlp_w_s[layer], gmlp_b_s[layer])
        cv_l = conformer_conv(z_l[..., G_END:], conv_w[layer], conv_b[layer], conv_ln_g[layer], conv_ln_b[layer])
        out_l = jnp.concatenate([attn_l, gm_l, cv_l], axis=-1) @ w_out[layer]

        if not last:
            q_c = rmsnorm(split_heads(z_c[..., :Q_END], N_Q_HEADS), q_norm_g[layer])
            attn_c = context_attention(q_c, k_c, v_c, attn_sink[layer])
            gm_c = chunk_gmlp(z_c[..., V_END:G_END], gmlp_ln_g[layer], gmlp_ln_b[layer], gmlp_w_s[layer], gmlp_b_s[layer])
            cv_c = conformer_conv(z_c[..., G_END:], conv_w[layer], conv_b[layer], conv_ln_g[layer], conv_ln_b[layer])
            out_c = jnp.concatenate([attn_c, gm_c, cv_c], axis=-1) @ w_out[layer]
            h_c = h_c + mod_c[2] * out_c
        h_l = h_l + mod_l[2] * out_l

        m_l = modulate(rmsnorm(h_l, norm_ffn_g[layer]), mod_l[3], mod_l[4])
        if last:
            h_l = h_l + mod_l[5] * grouped_moe(m_l, w_router, router_bias, w_gate[layer], w_up[layer], w_down[layer])
        else:
            m_c = modulate(rmsnorm(h_c, norm_ffn_g[layer]), mod_c[3], mod_c[4])
            y = grouped_moe(jnp.concatenate([m_c, m_l], axis=1), w_router, router_bias,
                            w_gate[layer], w_up[layer], w_down[layer])
            h_c = h_c + mod_c[5] * y[:, :L]
            h_l = h_l + mod_l[5] * y[:, L:]
    return h_l


_drawn_inputs = setup_inputs


def setup_inputs(seed=0):
    import zlib

    import numpy as np

    out = dict(_drawn_inputs(seed))
    spreads = {}
    factors = {'norm_mix_g': 5.218,
     'q_norm_g': 24.207,
     'k_norm_g': 25.789,
     'attn_sink': 8.0,
     'gmlp_ln_g': 33.024,
     'gmlp_ln_b': 34.322,
     'gmlp_b_s': 32.171,
     'conv_b': 64.0,
     'conv_ln_g': 200.0,
     'conv_ln_b': 64.0,
     'norm_ffn_g': 8.0,
     'router_bias': 7.804}
    for name, (base, spread) in spreads.items():
        noise = np.random.default_rng([zlib.crc32(name.encode()), seed]).standard_normal(out[name].shape)
        drawn = base * np.exp(spread * noise) if base else spread * noise
        out[name] = __import__('jax').numpy.asarray(drawn.astype(out[name].dtype))
    for name, factor in factors.items():
        out[name] = (out[name] * factor).astype(out[name].dtype)
    return out
```

```python
from contextlib import ExitStack

import numpy as np

import concourse.bass as bass
from concourse import mybir

F32 = mybir.dt.float32
I32 = mybir.dt.int32
ALU = mybir.AluOpType
ACT = mybir.ActivationFunctionType
AX = mybir.AxisListType

P = 128
D = 2048
KT = D // P
SEQ = 256
TT = SEQ // P
HD = 128
NH, NKV = 8, 2
GRID_W = 64
CW = 31
PAD = CW // 2
NE, NG, EPG = 16, 4, 4
FE = 1024
EPS = 1e-6
BIG = 1e30
N = 512

SLOTS = 8
CH = 2048
BASE, REST = 64, 32
BLK = BASE + REST
NBLK = -(-SEQ // BLK)
CAND = NBLK * NE
JOBS = NE + (2 * SEQ - NE) // BLK + 1
JCH = 24

GROUPS = [("a", 2560), ("g", 3072), ("kv", 1024), ("q0", 0), ("q1", 512), ("v", 2048), ("u", 1536)]
A_, G_, KV_, Q0_, Q1_, V_, U_ = range(7)


def make_schedule():
    mods = [("mod", p, k) for p in (3, 4, 2) for k in range(KT)]
    seq, m, pending = [], 0, []

    def some_mods(upto):
        nonlocal m
        while m < min(upto, len(mods)):
            seq.append(mods[m])
            m += 1
            if mods[m - 1][2] == KT - 1 and mods[m - 1][1] != 2:
                pending.append(("ext", mods[m - 1][1], 0))

    after = {
        (KV_, 3): [("convsum",)], (Q0_, 0): [("convsq",)],
        (Q0_, 1): [("kT",)], (Q1_, 0): [("qT", 0)], (V_, 1): [("qT", 1)],
        (U_, 3): [("spatial",)],
    }
    heads = [("head", h, s) for h in range(NH) for s in range(3)]
    hpos = 0
    for g in range(7):
        for c in range(4):
            seq.append(("win", g, 2 * c))
            while pending:
                seq.append(pending.pop())
            if (g, c) >= (Q1_, 2) and hpos < len(heads):
                seq.append(heads[hpos + 1])
            seq.append(("win", g, 2 * c + 1))
            seq += after.get((g, c), [])
            if (g, c) >= (Q1_, 1) and hpos < len(heads):
                if (g, c) >= (Q1_, 2):
                    seq.append(heads[hpos + 2])
                    hpos += 3
                if hpos < len(heads):
                    seq.append(heads[hpos])
            some_mods((48 * (4 * g + c + 1) + 26) // 27)
    seq += [("bcast", 2, i) for i in range(2)]
    m5 = 0
    for g in range(4):
        for c in range(4):
            seq.append(("wout", g, c))
            if g == 0 and c == 0:
                seq += [("bcast", 2, i) for i in range(2, 4)]
            if g == 0 and c == 1:
                seq.append(("gated",))
            if g and c == 0:
                seq.append(("hT", g - 1))
            if g and c == 2:
                seq += [("mod", 5, m5 + i) for i in range(3)]
                m5 += 3
    seq += [("hT", 3), ("mod", 5, 9), ("mod", 5, 10), ("route", 0), ("mod", 5, 11), ("mod", 5, 12),
            ("route", 1), ("mod", 5, 13), ("mod", 5, 14), ("route", 2), ("route", 3), ("mod", 5, 15)]
    return seq


SCHEDULE = make_schedule()
CHUNK_STEPS = [("mod", p, k) for p in (0, 1) for k in range(KT)] + [
    s for s in SCHEDULE if s[0] in ("mod", "wout") or (s[0] == "win" and s[2] % 2 == 0)]
NPRE = len(CHUNK_STEPS)
NUMBER = {s: n for n, s in enumerate(CHUNK_STEPS)}


def constants():
    p = np.arange(P)[:, None]
    c = np.arange(P)[None, :]
    f = np.float32
    rows = SEQ // GRID_W
    row = np.repeat(np.arange(rows, dtype=f), GRID_W)
    col = np.tile(np.arange(GRID_W, dtype=f), rows)
    nf = HD // 4
    inv = (f(10000.0) ** (-np.arange(nf, dtype=f) / f(nf))).astype(f)
    ang = np.concatenate([row[:, None] * inv, col[:, None] * inv], axis=-1)
    cos, sin = np.cos(ang), np.sin(ang)
    cosd = np.concatenate([cos, cos], 1).reshape(TT, P, HD).transpose(1, 0, 2).reshape(P, -1)
    sind = np.concatenate([-sin, sin], 1).reshape(TT, P, HD).transpose(1, 0, 2).reshape(P, -1)
    cand = np.arange(CAND)
    one = np.ones((P, 1))
    t = {
        "ident": p == c,
        "before": p < c,
        "mask0": np.where(c <= p, 0, -BIG),
        "mask1": np.where(c >= p, 0, -BIG),
        "slots": one * np.arange(BLK)[None],
        "jobno": one * np.arange(JOBS)[None],
        "sel": (p == 32 * (np.arange(8) // 2)[None] + (np.arange(8) % 2)[None]),
        "spread": (p == 32 * (np.arange(N) // P)[None]),
        "blk_lo": (np.arange(P)[:, None] // NE) * BLK,
        "expert": np.arange(P)[:, None] % NE,
        "cand_lo": one * ((cand // NE) * BLK)[None],
        "g4": one * (np.arange(NG) - 2 * NG)[None],
        "e16": one * (np.arange(NE) - 2 * NE)[None],
        "ones": one * np.ones((1, P)),
        "cos": cosd, "sin": sind,
    }
    at, cols = {}, 0
    for k, v in t.items():
        at[k] = (cols, v.shape[1])
        cols += v.shape[1]
    return at, cols, t


CONST_AT, ALL_COLS, _ = constants()
CONST_COLS = CONST_AT["cos"][0]


def build(nc, x, c, ctx, c_ctx, w_mod, b_mod, norm_mix_g, norm_ffn_g, w_in, w_out, q_norm_g, k_norm_g,
          attn_sink, gmlp_ln_g, gmlp_ln_b, gmlp_w_s, gmlp_b_s, conv_w, conv_b, conv_ln_g, conv_ln_b,
          w_router, router_bias, w_gate, w_up, w_down, consts, out):
    with ExitStack() as stack:
        def sb(name, shape, dt=F32):
            return stack.enter_context(nc.sbuf_tensor(name, shape, dt))

        def sem(name):
            return stack.enter_context(nc.semaphore(name))

        ring = sb("ring", [P, SLOTS, CH])
        const = sb("const", [P, CONST_COLS])
        tokens = sb("tokens", [P, 2 * TT, D])
        nT_all = sb("nT_all", [P, KT * 2 * SEQ])
        early = sb("early", [P, 2, D])
        mod_bias = sb("mod_bias", [P, 6, N])
        modrow = sb("modrow", [P, N])
        silu_c = sb("silu_c", [P, KT, 32])
        rows = sb("rows", [76, P])
        cols = sb("cols", [P, 44])
        modcol = sb("modcol", [P, 5, KT, 2])
        scale_mix = sb("scale_mix", [P, KT, 2])
        scale_ffn = sb("scale_ffn", [P, KT])
        qk_gain = sb("qk_gain", [P, 2, HD])
        sink = sb("sink", [P, NH])
        neg_sink = sb("neg_sink", [P, NH])
        rbias = sb("rbias", [P, NE])
        gm_gb = sb("gm_gb", [P, 2, N])
        w_sT = sb("w_sT", [P, 4, P])
        conv_cols = sb("conv_cols", [P, 4, CW + 1])
        wr = sb("wr", [P, KT, NE])
        wr_scaled = sb("wr_scaled", [P, KT, NE])
        stat = sb("stat", [P, 8])
        ss = sb("ss", [P, 8])
        rs_tok = sb("rs_tok", [P, 2 * TT])
        rope = sb("rope", [P, 4, TT, HD])
        work = sb("work", [P, 1024])
        heads = sb("heads", [P, 1024])
        yT = sb("yT", [P, 4, SEQ + 2 * PAD])
        bufA = sb("bufA", [P, 1024])
        bufB = sb("bufB", [P, 1024])
        probs = sb("probs", [P, 2, N])
        small = sb("small", [P, 64])
        n_i = sb("n_i", [1, 2 * JOBS + 1], I32)
        hsq = sb("hsq", [P, TT, 4])
        onehot_j = sb("onehot_j", [CAND, JOBS])
        vcol = sb("vcol", [CAND, 4])
        rrow = sb("rrow", [1, NE])

        def k_(name):
            at, n = CONST_AT[name]
            if at >= CONST_COLS:
                return heads[:, at - CONST_COLS:at - CONST_COLS + n]
            return const[:, at:at + n]

        ident, ones = k_("ident"), k_("ones")
        mixT = tokens[:, TT:2 * TT, :].rearrange("p a d -> p (a d)").rearrange("p (k t) -> p k t", k=KT)
        nT = nT_all[:].rearrange("p (k t) -> p k t", k=KT)
        yacc = nT_all[:, 0:TT * D].rearrange("p (t h n) -> p t h n", t=TT, h=2)
        hrT = nT_all[:, TT * D:].rearrange("p (k t) -> p k t", k=KT)
        tail = TT * D
        def part(buf, at, n):
            return buf[:, at:at + n]

        xg = part(nT_all, tail, KT * BLK).rearrange("p (k s) -> p k s", k=KT)
        outs = part(nT_all, tail + 1536, D)
        spread_T = part(nT_all, tail + 3584, 256).rearrange("p (t n) -> p t n", t=TT)
        hT = [part(bufA, 0, 512), part(nT_all, tail + 3840, 256)]
        silu_g = [part(work, 0, 512), part(bufA, 512, 256)]
        hidden = [part(work, 512, 512), part(bufA, 768, 256)]
        oh_in = part(bufB, 0, TT * BLK).rearrange("p (t s) -> p t s", t=TT)
        oh_out = part(bufB, 256, TT * BLK).rearrange("p (t s) -> p t s", t=TT)
        w_s = work[:, 0:N].rearrange("p (h q) -> p h q", h=4)
        conv_rows = work[0:CW + 1, N:2 * N]
        bc = probs[:].rearrange("p t n -> p (t n)")[:, 0:3 * SEQ].rearrange("p (i t) -> p i t", i=3)
        rt = heads[:, 0:24 * TT * NE].rearrange("p (i t e) -> p i t e", i=24, t=TT)
        yT_flat = yT[:].rearrange("p c t -> p (c t)")
        probsT = yT_flat[:, 0:4 * SEQ].rearrange("p (k t) -> p k t", k=4)
        cand = yT_flat[:, 0:4 * CAND].rearrange("p (t i c) -> p t i c", t=TT, i=2)
        candT = yT_flat[0:CAND, 256:768].rearrange("c (t i p) -> c t i p", t=TT, i=2)
        job = yT_flat[:, 768:768 + 4 * JOBS].rearrange("p (i t j) -> p i t j", i=2, t=TT)
        qT = early[:, 0, :].rearrange("p (h t) -> p h t", h=NH)
        kT = early[:, 1, 0:1024].rearrange("p (h t) -> p h t", h=NKV)
        vtok = early[:, 1, 1024:2048].rearrange("p (t n) -> p t n", t=2 * TT)
        gate_b = early[:, 0, :]
        acc = bufB[:].rearrange("p (c t) -> p c t", c=4)
        aT = bufA[:].rearrange("p (c t) -> p c t", c=4)
        vbuf = bufA[:].rearrange("p (t n) -> p t n", t=TT)
        ubuf = bufB[:].rearrange("p (t n) -> p t n", t=TT)
        mix_g, ffn_g = cols[:, 0:16], cols[:, 16:32]
        b_s, cv_g, cv_b = cols[:, 32:36], cols[:, 36:40], cols[:, 40:44]

        ps = stack.enter_context(nc.psum_tensor("ps", [P, 8, N], F32))
        Z = [ps[:, i, :] for i in range(4)]
        S = [ps[:, 4, :], ps[:, 5, :]]
        T, M = ps[:, 6, :], ps[:, 7, :]
        Gb, Ub, Db = [ps[:, 0, :], ps[:, 1, 0:256]], [ps[:, 2, :], ps[:, 3, 0:256]], [ps[:, 0:2, :], ps[:, 2, :]]
        Xb = Yb = ps[:, 4:8, :]
        pair = {A_: 0, G_: 2, KV_: 0, Q0_: 2, Q1_: 0, V_: 2, U_: 0}

        rows_in, const_in, tok_in, bias_in, misc_in = (sem(s) for s in (
            "rows_in", "const_in", "tok_in", "bias_in", "misc_in"))
        landed = [sem(f"landed{i}") for i in range(SLOTS)]
        slot_free = sem("slot_free")
        zeroed = sem("zeroed")
        rowsT_done, cols_saved, silu_done = sem("rowsT_done"), sem("cols_saved"), sem("silu_done")
        setupT_done, wsT_saved, convc_saved = sem("setupT_done"), sem("wsT_saved"), sem("convc_saved")
        sumsq_done, scaled, tokT_done = sem("sumsq_done"), sem("scaled"), sem("tokT_done")
        tokT_act, tokT_dve = sem("tokT_act"), sem("tokT_dve")
        mod_done, mod_saved, ext_done, modcol_saved = (sem(s) for s in (
            "mod_done", "mod_saved", "ext_done", "modcol_saved"))
        scale_done, nT_ready, nC_ready = sem("scale_done"), sem("nT_ready"), sem("nC_ready")
        a_saved, g_saved, conv_done = (sem(s) for s in ("a_saved", "g_saved", "conv_done"))
        csum_done, centred, csq_saved, csq_done, cnorm = (sem(s) for s in (
            "csum_done", "centred", "csq_saved", "csq_done", "cnorm"))
        conv_saved = sem("conv_saved")
        sq_saved, qk_read, v_saved, rope_done, headT_done, headT_saved = (sem(s) for s in (
            "sq_saved", "qk_read", "v_saved", "rope_done", "headT_done", "headT_saved"))
        score_done, neg_max, exp_done, den_done, probs_done, pT_done, pT0_saved, pT1_saved, pv_done, pv_saved = (
            sem(s) for s in ("score_done", "neg_max", "exp_done", "den_done", "probs_done", "pT_done",
                             "pT0_saved", "pT1_saved", "pv_done", "pv_saved"))
        gelu_v, v_ready, spatial_done, mixed_saved, gelu_u, gated, gatedT_done, gatedT_saved = (
            sem(s) for s in ("gelu_v", "v_ready", "spatial_done", "mixed_saved", "gelu_u", "gated",
                             "gatedT_done", "gatedT_saved"))
        bcast_done, bcast_saved = sem("bcast_done"), sem("bcast_saved")
        h_ready, hT_done, hT_saved, hsq_done, wr_ready = (sem(s) for s in (
            "h_ready", "hT_done", "hT_saved", "hsq_done", "wr_ready"))
        logit_done, logit_saved, score_saved, rbias_row, mask_ready, pos_done, cand_ready, candT_done = (
            sem(s) for s in ("logit_done", "logit_saved", "score_saved", "rbias_row", "mask_ready",
                             "pos_done", "cand_ready", "candT_done"))
        count_saved, order_done, table_oh, table_done, table_ready, y_zeroed = (sem(s) for s in (
            "count_saved", "order_done", "table_oh", "table_done", "table_ready", "y_zeroed"))
        oh_ready, gathered, xg_ready, silu_saved, hidden_ready = (sem(s) for s in (
            "oh_ready", "gathered", "xg_ready", "silu_saved", "hidden_ready"))
        ehT_done, ehT_saved, o_act, o_dve, scattered, summed = (sem(s) for s in (
            "ehT_done", "ehT_saved", "o_act", "o_dve", "scattered", "summed"))
        out_ready, out_sent = sem("out_ready"), sem("out_sent")
        dve_step, spread_saved = sem("dve_step"), sem("spread_saved")

        def save_outputs(eng, copy, odd, wide):
            for q in (odd, 2 + odd):
                if wide:
                    copy(outs[BASE:BLK, q * N:(q + 1) * N], Db[1][REST * q:REST * (q + 1), :])
                copy(outs[0:BASE, q * N:(q + 1) * N], Db[0][BASE * (q // 2):BASE * (q // 2 + 1), odd, :]) \
                    .then_inc(o_dve if odd else o_act, 1)

        block = stack.enter_context(nc.Block())

        def slot(n):
            return ring[:, n % SLOTS, :]

        def used_chunk(n):
            return SLOTS + n + 1

        def used(g):
            return used_chunk(NUMBER["win", g, 6])

        def used_out(g):
            return used_chunk(NUMBER["wout", g, 3])

        dve_count = [0]

        def link(ins):
            dve_count[0] += 1
            ins.then_inc(dve_step, 1)
            nc.vector.wait_ge(dve_step, dve_count[0])

        @block.sync
        def _(sp):
            for n, (kind, a, b) in enumerate(CHUNK_STEPS):
                sp.wait_ge(slot_free, n + 1)
                if kind == "mod":
                    dst, src = slot(n), w_mod[b * P:(b + 1) * P, a * D:(a + 1) * D]
                else:
                    w, col = (w_in, GROUPS[a][1]) if kind == "win" else (w_out, a * N)
                    q = b // 2 if kind == "win" else b
                    dst = slot(n).rearrange("p (k n) -> p k n", k=4)
                    src = w[q * 4 * P:(q + 1) * 4 * P, col:col + N].rearrange("(k p) n -> p k n", p=P)
                sp.dma_start(dst, src).then_inc(landed[n % SLOTS], 16)
            sp.wait_ge(table_ready, 1)
            jobs = sp.value_load(n_i[0:1, 2 * JOBS:2 * JOBS + 1], min_val=1, max_val=JOBS - 1)
            with sp.Fori(0, jobs) as j:
                e = sp.value_load(n_i[0:1, bass.ds(j, 1)], min_val=0, max_val=NE - 1)
                for i in range(JCH):
                    n = NPRE + i
                    sp.wait_ge(slot_free, j * JCH + (n + 1))
                    if i < 16:
                        w = (w_gate if i < 8 else w_up)[bass.ds(e, 1)].rearrange("e k f -> (e k) f")
                        src = w[(i % 8) * 2 * P:(i % 8 + 1) * 2 * P, :].rearrange("(k p) f -> p k f", p=P)
                        dst = slot(n).rearrange("p (k f) -> p k f", k=2)
                    else:
                        w = w_down[bass.ds(e, 1)].rearrange("e k f -> (e k) f")
                        src, dst = w[(i - 16) * P:(i - 15) * P, :], slot(n)
                    sp.dma_start(dst, src).then_inc(landed[n % SLOTS], 16)
            for q in range(4):
                sp.wait_ge(out_ready, q + 1)
                t, h = q // 2, q % 2
                sp.dma_start(out[t * P:(t + 1) * P, h * 1024:(h + 1) * 1024],
                             tokens[:, t, h * 1024:(h + 1) * 1024]).then_inc(out_sent, 16)
            sp.wait_ge(out_sent, 64)

        @block.gpsimd
        def _(pool):
            pool.memset(silu_c[:], 0.0).then_inc(zeroed, 1)
            pool.memset(mod_bias[:], 0.0).then_inc(zeroed, 1)
            pool.memset(yT[:], 0.0).then_inc(zeroed, 1)
            pool.memset(small[:, 63:64], 0.0).then_inc(slot_free, SLOTS)
            pool.memset(small[:, 62:63], 0.0).then_inc(modcol_saved, 1)
            pool.memset(small[:, 61:62], 0.0).then_inc(summed, 4)
            pool.wait_ge(scale_done, 1)
            for k in range(KT):
                pool.tensor_scalar(nT[:, k, SEQ:2 * SEQ], nT[:, k, SEQ:2 * SEQ], scale_mix[:, k, 1:2],
                                   modcol[:, 0, k, 1:2], ALU.mult, ALU.add).then_inc(nC_ready, 1)
            pool.wait_ge(slot_free, used(U_))
            pool.memset(nT_all[:, 0:TT * D], 0.0).then_inc(y_zeroed, 1)

        @block.tensor
        def _(pe):
            pe.wait_ge(const_in, 16)
            pe.wait_ge(rows_in, 16 * 7)
            pe.transpose(S[0][:, 0:76], rows[:], ident[0:76, 0:76]).then_inc(rowsT_done, 1)
            pe.wait_ge(misc_in, 16 * 11)
            for q in range(4):
                pe.transpose(S[1][:, q * 32:q * 32 + 32], conv_rows[:, q * P:(q + 1) * P], ident[0:32, 0:32])
            for h in range(4):
                mm = pe.transpose(T[:, h * P:(h + 1) * P], w_s[:, h, :], ident)
            mm.then_inc(setupT_done, 1)
            for t in range(2 * TT):
                pe.wait_ge(scaled, t + 1)
                for q in range(4):
                    if t >= 1:
                        pe.wait_ge(tokT_act if q % 2 else tokT_dve, 2 * (t - 1) + q // 2 + 1)
                    for i in range(4):
                        k = 4 * q + i
                        mm = pe.transpose(Z[q][:, i * P:(i + 1) * P], early[:, t % 2, k * P:(k + 1) * P], ident)
                    mm.then_inc(tokT_done, 1)

            def mod_products(n, k):
                for i in range(4):
                    mm = pe.matmul(M[32 * i:32 * i + 32, :], silu_c[:, k, :], slot(n)[:, i * N:(i + 1) * N],
                                   start=(k == 0), stop=(k == KT - 1))
                mm.then_inc(slot_free, 1)

            def add_bias(bias):
                pe.matmul(M, ident, bias, start=False, stop=True, skip_group_check=True).then_inc(mod_done, 1)

            def to_columns():
                for q in range(4):
                    mm = pe.matmul(M[:, 8 * q:8 * q + 8], modrow[:, q * P:(q + 1) * P], k_("sel"),
                                   start=True, stop=True)
                mm.then_inc(ext_done, 1)

            pe.wait_ge(silu_done, 1)
            pe.wait_ge(bias_in, 16 * 8)
            with pe.Fori(0, 2) as piece:
                pe.wait_ge(modcol_saved, piece + 1)
                for k in range(KT):
                    pe.wait_ge(landed[k % SLOTS], piece * 32 + 16 * (k // SLOTS + 1))
                    mod_products(k, k)
                add_bias(mod_bias[:, bass.ds(piece, 1), :].rearrange("p a n -> p (a n)"))
                pe.wait_ge(mod_saved, piece + 1)
                to_columns()

            nmod, nbc = 2, 0
            next_mod = {3: 2, 4: 3, 2: 4, 5: 5}

            for step in SCHEDULE:
                kind = step[0]
                n = NUMBER.get(step if kind != "win" else (kind, step[1], step[2] // 2 * 2))
                if n is not None:
                    pe.wait_ge(landed[n % SLOTS], 16 * (n // SLOTS + 1))
                if kind == "mod":
                    p, k = step[1:]
                    if k == 0:
                        if p in (3, 4, 2):
                            pe.wait_ge(modcol_saved, next_mod[p] + 1)
                        else:
                            pe.wait_ge(bcast_saved, 4)
                    mod_products(n, k)
                    if k == KT - 1:
                        add_bias(mod_bias[:, p, :])
                elif kind == "ext":
                    pe.wait_ge(mod_saved, next_mod[step[1]] + 1)
                    to_columns()
                elif kind == "bcast":
                    p, i = step[1:]
                    if i == 0:
                        pe.wait_ge(mod_saved, 5)
                    else:
                        pe.wait_ge(bcast_saved, i)
                    pe.matmul(M, k_("spread")[:, i * P:(i + 1) * P], modrow[:], start=True, stop=True) \
                        .then_inc(bcast_done, 1)
                elif kind == "win":
                    g, half = step[1:]
                    if half == 0:
                        if g == A_:
                            pe.wait_ge(tokT_act, 8)
                            pe.wait_ge(tokT_dve, 8)
                        elif g == KV_:
                            pe.wait_ge(a_saved, 1)
                            pe.wait_ge(cols_saved, 1)
                            pe.wait_ge(convc_saved, 1)
                            pe.wait_ge(silu_done, 1)
                        elif g == Q0_:
                            pe.wait_ge(g_saved, 1)
                        elif g == Q1_:
                            pe.wait_ge(qk_read, 1)
                            pe.wait_ge(v_saved, 1)
                        elif g == V_:
                            pe.wait_ge(qk_read, 2)
                        elif g == U_:
                            pe.wait_ge(qk_read, 3)
                    b = pair[g]
                    for i in range(2):
                        k = 2 * half + i
                        w = slot(n).rearrange("p (k n) -> p k n", k=4)[:, (half % 2) * 2 + i, :]
                        if g == A_:
                            pe.wait_ge(nT_ready, k + 1)
                        if g in (A_, G_):
                            for q in range(4):
                                mm = pe.matmul(Z[b + q // 2][:, (q % 2) * SEQ:(q % 2 + 1) * SEQ],
                                               w[:, q * P:(q + 1) * P], nT[:, k, 0:SEQ],
                                               start=(k == 0 and q % 2 == 0), stop=(k == KT - 1),
                                               skip_group_check=True)
                        else:
                            for t in range(TT):
                                mm = pe.matmul(Z[b + t], nT[:, k, t * P:(t + 1) * P], w,
                                               start=(k == 0), stop=(k == KT - 1))
                        if g == KV_:
                            pe.wait_ge(nC_ready, k + 1)
                            for t in range(TT):
                                mm = pe.matmul(S[t], nT[:, k, SEQ + t * P:SEQ + (t + 1) * P], w,
                                               start=(k == 0), stop=(k == KT - 1))
                    if half % 2 == 1:
                        mm.then_inc(slot_free, 1)
                elif kind == "convsum":
                    pe.wait_ge(conv_done, 1)
                    pe.wait_ge(wsT_saved, 1)
                    for q in range(4):
                        mm = pe.matmul(T[:, 0:SEQ], ones, acc[:, q, :], start=(q == 0), stop=(q == 3))
                    mm.then_inc(csum_done, 1)
                elif kind == "convsq":
                    pe.wait_ge(csq_saved, 1)
                    for q in range(4):
                        mm = pe.matmul(T[:, SEQ:2 * SEQ], ones, aT[:, q, :], start=(q == 0), stop=(q == 3))
                    mm.then_inc(csq_done, 1)
                elif kind == "kT":
                    pe.wait_ge(rope_done, 1)
                    pe.wait_ge(v_saved, 2)
                    for t in range(2 * TT):
                        for h in range(NKV):
                            mm = pe.transpose(S[t // 2][:, h * SEQ + (t % 2) * P:h * SEQ + (t % 2 + 1) * P],
                                              heads[:, t * SEQ + h * HD:t * SEQ + (h + 1) * HD], ident)
                    mm.then_inc(headT_done, 1)
                elif kind == "qT":
                    g = step[1]
                    pe.wait_ge(rope_done, 2 + g)
                    if g == 0:
                        pe.wait_ge(headT_saved, 1)
                    if g:
                        pe.wait_ge(pT0_saved, 4)
                    for t in range(TT):
                        if g:
                            pe.wait_ge(headT_saved, 2 + t)
                            if t == 0:
                                pe.wait_ge(cnorm, 1)
                        for h in range(4):
                            mm = pe.transpose((T if g else S[t])[:, h * P:(h + 1) * P],
                                              heads[:, t * N + h * HD:t * N + (h + 1) * HD], ident)
                        if g or t:
                            mm.then_inc(headT_done, 1)
                elif kind == "head":
                    h, part = step[1:]
                    kv = h // (NH // NKV)
                    if part == 0:
                        if h == 0:
                            pe.wait_ge(headT_saved, 2)
                        if h == 4:
                            pe.wait_ge(headT_saved, 4)
                        for t in range(TT):
                            if h:
                                pe.wait_ge(pv_saved if t else pT1_saved, h)
                            pe.matmul(S[t], qT[:, h, t * P:(t + 1) * P], kT[:, kv, :], start=True, stop=True)
                            mm = pe.matmul(S[t][:, (1 - t) * P:(2 - t) * P], ident, k_(f"mask{t}"),
                                           start=False, stop=True, skip_group_check=True)
                        mm.then_inc(score_done, 1)
                    elif part == 1:
                        pe.wait_ge(probs_done, h + 1)
                        if h == 0:
                            pe.wait_ge(cnorm, 1)
                        if h:
                            pe.wait_ge(pT0_saved, h)
                        for t in range(TT):
                            for q in range(4):
                                mm = pe.transpose((S[0] if t else T)[:, q * P:(q + 1) * P],
                                                  probs[:, t, q * P:(q + 1) * P], ident)
                            mm.then_inc(pT_done, 1)
                    else:
                        pe.wait_ge(pT0_saved, h + 1)
                        pe.wait_ge(pT1_saved, h + 1)
                        for q in range(4):
                            mm = pe.matmul(S[1][:, 0:SEQ], vtok[:, q, kv * HD:(kv + 1) * HD], probsT[:, q, :],
                                           start=(q == 0), stop=(q == 3))
                        mm.then_inc(pv_done, 1)
                elif kind == "spatial":
                    pe.wait_ge(v_ready, 1)
                    pe.wait_ge(pT0_saved, NH)
                    pe.wait_ge(pT1_saved, NH)
                    pe.wait_ge(headT_saved, 4)
                    for t in range(TT):
                        for h in range(4):
                            mm = pe.matmul((S[0] if t else T)[:, h * P:(h + 1) * P], w_sT[:, h, :],
                                           vbuf[:, t, h * HD:(h + 1) * HD], start=True, stop=True)
                    mm.then_inc(spatial_done, 1)
                elif kind == "gated":
                    pe.wait_ge(gated, 1)
                    for t in range(TT):
                        for h in range(4):
                            mm = pe.transpose((S[0] if t else T)[:, h * P:(h + 1) * P],
                                              ubuf[:, t, h * HD:(h + 1) * HD], ident)
                    mm.then_inc(gatedT_done, 1)
                elif kind == "wout":
                    g, c4 = step[1:]
                    b = 2 if g % 2 == 0 else 0
                    if c4 == 0:
                        if g == 0:
                            pe.wait_ge(gelu_v, 1)
                            pe.wait_ge(pv_saved, NH)
                        elif g == 1:
                            pe.wait_ge(gelu_u, 1)
                        else:
                            pe.wait_ge(h_ready, g - 1)
                    if g == 0 and c4 == 2:
                        pe.wait_ge(gatedT_saved, 1)
                    if g == 0 and c4 == 3:
                        pe.wait_ge(conv_saved, 1)
                    for i in range(4):
                        k = 4 * c4 + i
                        w = slot(n).rearrange("p (k n) -> p k n", k=4)[:, i, :]
                        for t in range(TT):
                            mm = pe.matmul(Z[b + t], mixT[:, k, t * P:(t + 1) * P], w,
                                           start=(k == 0), stop=(k == KT - 1))
                    mm.then_inc(slot_free, 1)
                elif kind == "hT":
                    g = step[1]
                    pe.wait_ge(h_ready, g + 1)
                    if g:
                        pe.wait_ge(hT_saved, g)
                    else:
                        pe.wait_ge(gatedT_saved, 1)
                        pe.wait_ge(wr_ready, 1)
                    for t in range(TT):
                        for i in range(4):
                            k = 4 * g + i
                            mm = pe.transpose(S[t][:, i * P:(i + 1) * P], tokens[:, t, k * P:(k + 1) * P], ident)
                    mm.then_inc(hT_done, 1)
                elif kind == "route":
                    part = step[1]
                    if part == 0:
                        pe.wait_ge(hT_saved, 4)
                        for t in range(TT):
                            for k in range(KT):
                                pe.matmul(T[:, t * NE:(t + 1) * NE], hrT[:, k, t * P:(t + 1) * P],
                                          wr_scaled[:, k, :], start=(k == 0), stop=(k == KT - 1))
                        for k in range(KT):
                            mm = pe.matmul(T[0:1, 64:64 + NE], modcol[:, 3, k, 0:1], wr[:, k, :],
                                           start=(k == 0), stop=(k == KT - 1))
                        mm.then_inc(logit_done, 1)
                        pe.wait_ge(rbias_row, 1)
                        pe.matmul(S[0][:, 0:NE], ones[0:1, :], rrow[:], start=True, stop=True) \
                            .then_inc(logit_done, 1)
                    elif part == 1:
                        pe.wait_ge(mask_ready, 1)
                        mask = rt[:, 15]
                        pe.matmul(T[:, 0:NE], k_("before"), mask[:, 0, :], start=True, stop=True)
                        pe.matmul(T[:, NE:2 * NE], ones, mask[:, 0, :], start=True, stop=False)
                        pe.matmul(T[:, NE:2 * NE], k_("before"), mask[:, 1, :], start=False, stop=True)
                        for t in range(TT):
                            mm = pe.matmul(T[0:CAND, 128:129], cand[:, t, 0, :], ones[:, 0:1],
                                           start=(t == 0), stop=(t == TT - 1))
                        mm.then_inc(pos_done, 1)
                    elif part == 2:
                        pe.wait_ge(count_saved, 1)
                        pe.matmul(T[0:CAND, 0:1], k_("before")[0:CAND, 0:CAND], vcol[:, 0:1],
                                  start=True, stop=True)
                        pe.matmul(T[0:1, 2:3], vcol[:, 0:1], ones[0:CAND, 0:1], start=True, stop=True) \
                            .then_inc(order_done, 1)
                        pe.wait_ge(cand_ready, 1)
                        for t in range(TT):
                            for i in range(2):
                                mm = pe.transpose(S[0][0:CAND, (2 * t + i) * P:(2 * t + i + 1) * P],
                                                  cand[:, t, i, :], ident)
                        mm.then_inc(candT_done, 1)
                    else:
                        pe.wait_ge(table_oh, 2)
                        for i in range(2):
                            for t in range(TT):
                                at = (i * TT + t) * JOBS
                                pe.matmul(S[1][:, at:at + JOBS], candT[:, t, i, :], onehot_j[:],
                                          start=True, stop=True)
                        pe.matmul(S[1][0:1, 256:256 + JOBS], k_("expert")[0:CAND, :], onehot_j[:],
                                  start=True, stop=True)
                        pe.matmul(S[1][0:1, 256 + JOBS:256 + 2 * JOBS], vcol[:, 2:3], onehot_j[:],
                                  start=True, stop=True).then_inc(table_done, 1)

            for i in range(4):
                pe.wait_ge(mod_saved, 6) if i == 0 else pe.wait_ge(bcast_saved, 4 + i)
                pe.matmul(M, k_("spread")[:, i * P:(i + 1) * P], modrow[:], start=True, stop=True) \
                    .then_inc(bcast_done, 1)
            pe.wait_ge(bcast_saved, 8)

            def gather(half):
                for k in range(8 * half, 8 * half + 8):
                    for t in range(TT):
                        mm = pe.matmul(Xb[:, k // 4, (k % 4) * BLK:(k % 4 + 1) * BLK],
                                       tokens[:, t, k * P:(k + 1) * P], oh_in[:, t, :],
                                       start=(t == 0), stop=(t == TT - 1))
                mm.then_inc(gathered, 1)

            def experts(j, wide):
                def arrived(i):
                    n = NPRE + i
                    pe.wait_ge(landed[n % SLOTS], j * (16 * JCH // SLOTS) + 16 * (n // SLOTS + 1))
                    return slot(n)

                pe.wait_ge(xg_ready, j + 1)
                for m, out_b in ((0, Gb), (1, Ub)):
                    for i in range(8):
                        w = arrived(8 * m + i).rearrange("p (k f) -> p k f", k=2)
                        for kk in range(2):
                            k = 2 * i + kk
                            for f in range(2):
                                mm = pe.matmul(out_b[0][BASE * f:BASE * (f + 1), :], xg[:, k, 0:BASE],
                                               w[:, kk, f * N:(f + 1) * N], start=(k == 0), stop=(k == KT - 1))
                        for kk in range(2 * wide):
                            k = 2 * i + kk
                            for f in range(4):
                                mm = pe.matmul(out_b[1][REST * f:REST * (f + 1), :], xg[:, k, BASE:BLK],
                                               w[:, kk, f * 256:(f + 1) * 256], start=(k == 0), stop=(k == KT - 1))
                        mm.then_inc(slot_free, 1)
                pe.wait_ge(oh_ready, j + 2)
                pe.wait_ge(summed, j * 4 + 4)
                gather(0)
                pe.wait_ge(hidden_ready, j + 1)
                for i in range(1 + wide):
                    for q in range(4 // (i + 1)):
                        pe.transpose(Gb[i][:, q * P:(q + 1) * P], hidden[i][:, q * P:(q + 1) * P], ident)
                for t in range(TT):
                    mm = pe.transpose(Ub[0][0:BLK, t * P:(t + 1) * P], oh_out[:, t, :], ident)
                mm.then_inc(ehT_done, 1)
                gather(1)
                pe.wait_ge(ehT_saved, j + 1)
                pe.wait_ge(spread_saved, j + 1)
                for i in range(8):
                    w = arrived(16 + i)
                    for q in (0, 2, 1, 3):
                        mm = pe.matmul(Db[0][BASE * (q // 2):BASE * (q // 2 + 1), q % 2, :],
                                       hT[0][:, (i % 4) * P + BASE * (i // 4):(i % 4) * P + BASE * (i // 4 + 1)],
                                       w[:, q * N:(q + 1) * N], start=(i == 0), stop=(i == 7))
                    for q in range(4 * wide):
                        mm = pe.matmul(Db[1][REST * q:REST * (q + 1), :],
                                       hT[1][:, (i % 2) * P + REST * (i // 2):(i % 2) * P + REST * (i // 2 + 1)],
                                       w[:, q * N:(q + 1) * N], start=(i == 0), stop=(i == 7))
                    mm.then_inc(slot_free, 1)
                pe.wait_ge(xg_ready, j + 2)
                rows_used = BLK if wide else BASE
                for t in range(TT):
                    for q in range(4):
                        if t == 0:
                            pe.wait_ge(o_dve if q % 2 else o_act, j * 2 + (q // 2 + 1))
                        elif q % 2 == 0:
                            pe.wait_ge(summed, j * 4 + (5 + q // 2))
                        mm = pe.matmul(Yb[:, q, :], spread_T[0:rows_used, t, :],
                                       outs[0:rows_used, q * N:(q + 1) * N], start=True, stop=True)
                        if q % 2:
                            mm.then_inc(scattered, 1)

            pe.wait_ge(table_ready, 1)
            jobs = pe.value_load(n_i[0:1, 2 * JOBS:2 * JOBS + 1], min_val=1, max_val=JOBS - 1)
            pe.wait_ge(oh_ready, 1)
            gather(0)
            gather(1)
            with pe.Fori(0, jobs) as j:
                wide = pe.value_load(n_i[0:1, bass.ds(j + JOBS, 1)], min_val=0, max_val=1)
                with pe.If(wide):
                    experts(j, True)
                with pe.Else():
                    experts(j, False)

        @block.scalar
        def _(act):
            copy = nc.scalar.copy

            act.dma_start(const[:], consts[:, 0:CONST_COLS]).then_inc(const_in, 16)
            at = 0
            for v, n in ((c, 16), (c_ctx, 16), (norm_mix_g, 16), (norm_ffn_g, 16), (gmlp_b_s, 4),
                         (conv_ln_g, 4), (conv_ln_b, 4)):
                act.dma_start(rows[at:at + n, :], v).then_inc(rows_in, 16)
                at += n
            for t in range(2 * TT):
                act.dma_start(tokens[:, t, :], (x if t < TT else ctx)[(t % TT) * P:(t % TT + 1) * P, :]) \
                    .then_inc(tok_in, 16)
            act.dma_start(heads[:, 0:ALL_COLS - CONST_COLS], consts[:, CONST_COLS:ALL_COLS]).then_inc(misc_in, 16)
            act.dma_start(conv_rows[0:CW, :], conv_w).then_inc(misc_in, 16)
            act.dma_start(conv_rows[CW:CW + 1, :], conv_b).then_inc(misc_in, 16)
            act.dma_start(w_s, gmlp_w_s.rearrange("h p q -> p h q")).then_inc(misc_in, 16)
            for dst, v in ((qk_gain[:, 0, :], q_norm_g), (qk_gain[:, 1, :], k_norm_g), (sink[:], attn_sink),
                           (rbias[:], router_bias), (gm_gb[:, 0, :], gmlp_ln_g), (gm_gb[:, 1, :], gmlp_ln_b)):
                act.dma_start(dst, v.broadcast_to([P, v.shape[1]])).then_inc(misc_in, 16)
            act.dma_start(wr[:], w_router.rearrange("(k p) e -> p k e", p=P)).then_inc(misc_in, 16)
            act.wait_ge(zeroed, 3)
            for i in range(4):
                for r in range(2):
                    act.dma_start(mod_bias[32 * i + r:32 * i + r + 1, :, :],
                                  b_mod.rearrange("o (s i n) -> i o s n", s=6, i=4)[i]).then_inc(bias_in, 16)
            act.wait_ge(rowsT_done, 1)
            act.activation(silu_c[:, :, 0:2], S[0][:, 0:32].rearrange("p (r k) -> p k r", r=2), ACT.Silu) \
                .then_inc(silu_done, 1)
            act.wait_ge(setupT_done, 1)
            copy(w_sT[:].rearrange("p h q -> p (h q)"), T).then_inc(wsT_saved, 1)
            act.wait_ge(tok_in, 16 * 4)
            for t in range(2 * TT):
                act.activation(nT_all[:, t * D:(t + 1) * D], tokens[:, t, :], ACT.Square,
                               accum_out=ss[:, t:t + 1]).then_inc(sumsq_done, 1)
            for t in range(2 * TT):
                for q in (1, 3):
                    act.wait_ge(tokT_done, 4 * t + q + 1)
                    copy(nT[:, 4 * q:4 * q + 4, t * P:(t + 1) * P], Z[q].rearrange("p (k t) -> p k t", k=4)) \
                        .then_inc(tokT_act, 1)

            def save_mod(idx):
                act.wait_ge(mod_done, idx + 1)
                copy(modrow[:], M).then_inc(mod_saved, 1)

            def save_columns(idx, p):
                act.wait_ge(ext_done, idx + 1)
                copy(modcol[:, p, :, :].rearrange("p (i q) r -> p q i r", i=4),
                     M[:, 0:32].rearrange("p (q i r) -> p q i r", q=4, i=4)).then_inc(modcol_saved, 1)

            for idx in range(2):
                save_mod(idx)
                save_columns(idx, idx)
            act.wait_ge(slot_free, used(A_))
            copy(bufA[:], ps[:, 0:2, :]).then_inc(a_saved, 1)
            act.wait_ge(slot_free, used(G_))
            act.activation(bufB[:], ps[:, 2:4, :], ACT.Sigmoid).then_inc(g_saved, 1)
            save_mod(2)
            save_columns(2, 3)

            def squares(idx, bank):
                if idx:
                    act.wait_ge(rope_done, idx)
                act.activation(work[:].rearrange("p (t n) -> p t n", t=TT), ps[:, bank:bank + 2, :], ACT.Square) \
                    .then_inc(sq_saved, 1)

            act.wait_ge(slot_free, used(KV_))
            w4 = work[:].rearrange("p (t n) -> p t n", t=2 * TT)
            act.activation(w4[:, 0:2], ps[:, 0:2, 0:SEQ], ACT.Square)
            act.activation(w4[:, 2:4], ps[:, 4:6, 0:SEQ], ACT.Square).then_inc(sq_saved, 1)
            copy(vtok[:, 0:2], ps[:, 0:2, SEQ:N]).then_inc(v_saved, 1)
            copy(vtok[:, 2:4], ps[:, 4:6, SEQ:N]).then_inc(v_saved, 1)
            act.wait_ge(centred, 1)
            act.activation(bufA[:], bufB[:], ACT.Square).then_inc(csq_saved, 1)
            act.wait_ge(headT_done, 1)
            copy(kT[:, :, 0:SEQ], S[0].rearrange("p (h t) -> p h t", h=NKV))
            copy(kT[:, :, SEQ:N], S[1].rearrange("p (h t) -> p h t", h=NKV)).then_inc(headT_saved, 1)
            act.wait_ge(cnorm, 1)
            for q in range(4):
                last = act.activation(mixT[:, 12 + q, :], acc[:, q, :], ACT.Silu, bias=cv_b[:, q:q + 1],
                                      scale=cv_g[:, q:q + 1])
            last.then_inc(conv_saved, 1)
            act.wait_ge(slot_free, used(Q0_))
            squares(1, 2)
            act.wait_ge(headT_done, 2)
            for t in range(TT):
                last = copy(qT[:, 0:4, t * P:(t + 1) * P], S[t].rearrange("p (h t) -> p h t", h=4))
            last.then_inc(headT_saved, 1)

            def exps(h):
                act.wait_ge(neg_max, h + 1)
                if h:
                    act.wait_ge(pT_done, 2 * h)
                for t in range(TT):
                    act.activation(probs[:, t, :], S[t], ACT.Exp, bias=small[:, 2 + t:3 + t], scale=HD ** -0.5,
                                   accum_out=small[:, 4 + t:5 + t]).then_inc(exp_done, 1)
                for t in range(TT):
                    act.activation(small[:, 6 + t:7 + t], sink[:, h:h + 1], ACT.Exp, bias=small[:, 2 + t:3 + t]) \
                        .then_inc(exp_done, 1)

            def save_pT(h):
                if h:
                    act.wait_ge(pv_done, h)
                for t in range(TT):
                    act.wait_ge(pT_done, 2 * h + t + 1)
                    copy(probsT[:, :, t * P:(t + 1) * P], (S[0] if t else T).rearrange("p (k t) -> p k t", k=4)) \
                        .then_inc(pT1_saved if t else pT0_saved, 1)

            def save_pv(h):
                act.wait_ge(pv_done, h + 1)
                copy(mixT[:, h, :], S[1][:, 0:SEQ]).then_inc(pv_saved, 1)

            for h in range(NH):
                if h == 2:
                    act.wait_ge(slot_free, used(Q1_))
                    squares(2, 0)
                exps(h)
                if h == 0:
                    save_mod(3)
                    save_columns(3, 4)
                save_pT(h)
                if h == 3:
                    for t in range(TT):
                        act.wait_ge(headT_done, 3 + t)
                        copy(qT[:, 4:8, t * P:(t + 1) * P], T.rearrange("p (h t) -> p h t", h=4)) \
                            .then_inc(headT_saved, 1)
                save_pv(h)
            act.wait_ge(slot_free, used(V_))
            act.wait_ge(csq_done, 1)
            act.activation(bufA[:], ps[:, 2:4, :], ACT.Gelu_apprx_tanh).then_inc(gelu_v, 1)
            save_mod(4)
            act.wait_ge(slot_free, used(U_))
            act.activation(bufB[:], ps[:, 0:2, :], ACT.Gelu_apprx_tanh).then_inc(gelu_u, 1)
            for i in range(4):
                act.wait_ge(bcast_done, i + 1)
                copy(gate_b[:, i * N:(i + 1) * N], M).then_inc(bcast_saved, 1)
            act.wait_ge(gatedT_done, 1)
            for t in range(TT):
                last = copy(mixT[:, 8:12, t * P:(t + 1) * P], (S[0] if t else T).rearrange("p (h t) -> p h t", h=4))
            last.then_inc(gatedT_saved, 1)
            for g in range(4):
                act.wait_ge(h_ready, g + 1)
                if g:
                    act.wait_ge(hsq_done, 2 * g)
                for t in range(TT):
                    act.activation(probs[:, t, :], tokens[:, t, g * N:(g + 1) * N], ACT.Square,
                                   accum_out=hsq[:, t, g:g + 1]).then_inc(hsq_done, 1)
                act.wait_ge(hT_done, g + 1)
                for t in range(TT):
                    last = copy(hrT[:, 4 * g:4 * g + 4, t * P:(t + 1) * P], S[t].rearrange("p (k t) -> p k t", k=4))
                last.then_inc(hT_saved, 1)
            act.wait_ge(logit_saved, 1)
            act.activation(rt[:, 1], rt[:, 0], ACT.Sigmoid).then_inc(score_saved, 1)
            save_mod(5)
            for i in range(4):
                act.wait_ge(bcast_done, 5 + i)
                copy(gate_b[:, i * N:(i + 1) * N], M).then_inc(bcast_saved, 1)
            act.wait_ge(table_ready, 1)
            jobs = act.value_load(n_i[0:1, 2 * JOBS:2 * JOBS + 1], min_val=1, max_val=JOBS - 1)

            def save_tokens(half):
                for k in range(8 * half, 8 * half + 8):
                    last = act.activation(xg[:, k, :], Xb[:, k // 4, (k % 4) * BLK:(k % 4 + 1) * BLK], ACT.Identity,
                                          bias=modcol[:, 3, k, 0:1], scale=scale_ffn[:, k:k + 1])
                return last

            def job_evac(j, wide):
                act.wait_ge(slot_free, j * JCH + used_chunk(NPRE + 7))
                for i in range(1 + wide):
                    last = act.activation(silu_g[i], Gb[i], ACT.Silu)
                last.then_inc(silu_saved, 1)
                act.wait_ge(ehT_done, j + 1)
                for i in range(1 + wide):
                    last = copy(hT[i], Gb[i])
                last.then_inc(ehT_saved, 1)
                act.wait_ge(gathered, j * 2 + 3)
                save_tokens(0)
                act.wait_ge(gathered, j * 2 + 4)
                save_tokens(1).then_inc(xg_ready, 1)
                act.wait_ge(slot_free, j * JCH + used_chunk(NPRE + 23))
                save_outputs(act, copy, 0, wide)

            act.wait_ge(gathered, 2)
            save_tokens(0)
            save_tokens(1).then_inc(xg_ready, 1)
            with act.Fori(0, jobs) as j:
                wide = act.value_load(n_i[0:1, bass.ds(j + JOBS, 1)], min_val=0, max_val=1)
                with act.If(wide):
                    job_evac(j, True)
                with act.Else():
                    job_evac(j, False)

        @block.vector
        def _(dve):
            tt, ts, stt = nc.vector.tensor_tensor, nc.vector.tensor_scalar, nc.vector.scalar_tensor_tensor

            def rsqrt(y, v, tmp):
                link(ts(y.bitcast(I32), v.bitcast(I32), 1, None, ALU.logical_shift_right))
                link(ts(y.bitcast(I32), y.bitcast(I32), -1.0, float(0x5F3759DF), ALU.mult, ALU.add))
                for _ in range(3):
                    link(tt(tmp, y, y, ALU.mult))
                    link(tt(tmp, tmp, v, ALU.mult))
                    link(ts(tmp, tmp, -0.5, 1.5, ALU.mult, ALU.add))
                    link(tt(y, y, tmp, ALU.mult))

            def bcast(ap, shape):
                return ap.broadcast_to(shape)

            dve.wait_ge(silu_done, 1)
            nc.vector.tensor_copy(cols[:], S[0][:, 32:76]).then_inc(cols_saved, 1)
            dve.wait_ge(setupT_done, 1)
            nc.vector.tensor_copy(conv_cols[:], S[1][:, 0:P].rearrange("p (q n) -> p q n", q=4)) \
                .then_inc(convc_saved, 1)
            link(ts(neg_sink[:], sink[:], -1.0, None, ALU.mult))
            for i in range(2):
                for t in range(TT):
                    g = qk_gain[:, i, :]
                    cs, sn = (k_(n)[:, t * HD:(t + 1) * HD] for n in ("cos", "sin"))
                    link(tt(rope[:, 2 * i, t, :], cs, g, ALU.mult))
                    for a, b in ((0, 64), (64, 0)):
                        link(tt(rope[:, 2 * i + 1, t, a:a + 64], sn[:, a:a + 64], g[:, b:b + 64], ALU.mult))
            dve.wait_ge(sumsq_done, 4)
            link(ts(stat[:, 0:4], ss[:, 0:4], 1.0 / D, EPS, ALU.mult, ALU.add))
            rsqrt(rs_tok[:], stat[:, 0:4], stat[:, 4:8])
            for t in range(2 * TT):
                if t >= 2:
                    dve.wait_ge(tokT_done, 4 * (t - 1))
                ts(early[:, t % 2, :], tokens[:, t, :], rs_tok[:, t:t + 1], None, ALU.mult).then_inc(scaled, 1)
                if t:
                    for q in (0, 2):
                        dve.wait_ge(tokT_done, 4 * (t - 1) + q + 1)
                        nc.vector.tensor_copy(nT[:, 4 * q:4 * q + 4, (t - 1) * P:t * P],
                                              Z[q].rearrange("p (k t) -> p k t", k=4)).then_inc(tokT_dve, 1)
            for q in (0, 2):
                dve.wait_ge(tokT_done, 12 + q + 1)
                nc.vector.tensor_copy(nT[:, 4 * q:4 * q + 4, 3 * P:4 * P],
                                      Z[q].rearrange("p (k t) -> p k t", k=4)).then_inc(tokT_dve, 1)
            dve.wait_ge(modcol_saved, 3)
            stt(scale_mix[:], modcol[:, 1], 1.0, mix_g.unsqueeze(2).broadcast_to([P, KT, 2]),
                ALU.add, ALU.mult).then_inc(scale_done, 1)
            dve.wait_ge(scale_done, 1)
            dve.wait_ge(tokT_act, 8)
            dve.wait_ge(tokT_dve, 8)
            for k in range(KT):
                ts(nT[:, k, 0:SEQ], nT[:, k, 0:SEQ], scale_mix[:, k, 0:1], modcol[:, 0, k, 0:1],
                   ALU.mult, ALU.add).then_inc(nT_ready, 1)
            dve.wait_ge(g_saved, 1)
            dve.wait_ge(a_saved, 1)
            dve.wait_ge(zeroed, 3)
            link(tt(yT[:, :, PAD:PAD + SEQ], aT, acc, ALU.mult))
            for tap in range(CW):
                for q in range(4):
                    if tap:
                        dve.wait_ge(dve_step, dve_count[0] - 3)
                        ins = stt(acc[:, q, :], yT[:, q, tap:tap + SEQ], conv_cols[:, q, tap:tap + 1],
                                  acc[:, q, :], ALU.mult, ALU.add)
                    else:
                        ins = ts(acc[:, q, :], yT[:, q, 0:SEQ], conv_cols[:, q, 0:1],
                                 conv_cols[:, q, CW:CW + 1], ALU.mult, ALU.add)
                    ins.then_inc(dve_step, 1)
                    dve_count[0] += 1
            dve.wait_ge(dve_step, dve_count[0])
            ts(small[:, 32:33], small[:, 63:64], 1.0, None, ALU.mult).then_inc(conv_done, 1)
            dve.wait_ge(csum_done, 1)
            link(ts(bc[:, 0, :], T[:, 0:SEQ], 1.0 / N, None, ALU.mult))
            tt(acc, acc, bc[:, 0:1, :].broadcast_to([P, 4, SEQ]), ALU.subtract).then_inc(centred, 1)
            dve.wait_ge(centred, 1)

            def head_norm(idx):
                dve.wait_ge(sq_saved, idx + 1)
                link(nc.vector.tensor_reduce(ss[:], work[:].rearrange("p (h d) -> p h d", h=8), AX.X, ALU.add))
                link(ts(ss[:], ss[:], 1.0 / HD, EPS, ALU.mult, ALU.add))
                rsqrt(stat[:], ss[:], small[:, 8:16])

            def rotate(z, at, n_heads, table, t):
                shape = [P, n_heads, 64]
                zh = z.rearrange("p (h d) -> p h d", d=HD)
                o = heads[:, at:at + n_heads * HD].rearrange("p (h d) -> p h d", d=HD)
                w = work[:, at:at + n_heads * HD].rearrange("p (h d) -> p h d", d=HD)
                last = tt(o, zh, rope[:, table, t:t + 1, :].broadcast_to([P, n_heads, HD]), ALU.mult)
                for a, b in ((0, 64), (64, 0)):
                    last = tt(w[:, :, a:a + 64], zh[:, :, b:b + 64],
                              rope[:, table + 1, t:t + 1, a:a + 64].broadcast_to(shape), ALU.mult)
                return last

            def finish_heads(n):
                link(tt(heads[:, 0:n], heads[:, 0:n], work[:, 0:n], ALU.add))
                tt(heads[:].rearrange("p (h d) -> p h d", d=HD), heads[:].rearrange("p (h d) -> p h d", d=HD),
                   stat[:].unsqueeze(2).broadcast_to([P, 8, HD]), ALU.mult).then_inc(rope_done, 1)

            head_norm(0)
            dve.wait_ge(v_saved, 2)
            for t in range(TT):
                link(rotate(ps[:, t, 0:SEQ], t * SEQ, NKV, 2, t))
            for t in range(TT):
                last = tt(heads[:, N + t * SEQ:N + (t + 1) * SEQ].rearrange("p (h d) -> p h d", d=HD),
                          ps[:, 4 + t, 0:SEQ].rearrange("p (h d) -> p h d", d=HD),
                          qk_gain[:, 1:2, :].broadcast_to([P, NKV, HD]), ALU.mult)
            last.then_inc(qk_read, 1)
            dve.wait_ge(qk_read, 1)
            finish_heads(N)
            dve.wait_ge(csq_done, 1)
            link(ts(bc[:, 0, :], T[:, SEQ:N], 1.0 / N, EPS, ALU.mult, ALU.add))
            rsqrt(bc[:, 1, :], bc[:, 0, :], bc[:, 2, :])
            tt(acc, acc, bc[:, 1:2, :].broadcast_to([P, 4, SEQ]), ALU.mult).then_inc(cnorm, 1)

            def q_heads(idx, bank):
                head_norm(idx)
                dve.wait_ge(headT_done, idx)
                for t in range(TT):
                    last = rotate(ps[:, bank + t, :], t * N, 4, 0, t)
                    if t == 0:
                        link(last)
                last.then_inc(qk_read, 1)
                dve.wait_ge(qk_read, idx + 1)
                finish_heads(1024)

            q_heads(1, 2)
            for h in range(NH):
                if h == 3:
                    q_heads(2, 0)
                dve.wait_ge(score_done, h + 1)
                link(nc.vector.tensor_reduce(small[:, 0:2], ps[:, 4:6, :], AX.X, ALU.max))
                ts(small[:, 2:4], small[:, 0:2], -(HD ** -0.5), neg_sink[:, h:h + 1], ALU.mult, ALU.min) \
                    .then_inc(neg_max, 1)
                dve.wait_ge(exp_done, 4 * h + 4)
                link(tt(small[:, 4:6], small[:, 4:6], small[:, 6:8], ALU.add))
                link(nc.vector.reciprocal(small[:, 4:6], small[:, 4:6]))
                for t in range(TT):
                    last = ts(probs[:, t, :], probs[:, t, :], small[:, 4 + t:5 + t], None, ALU.mult)
                last.then_inc(probs_done, 1)
                dve.wait_ge(probs_done, h + 1)
            dve.wait_ge(gelu_v, 1)
            for t in range(TT):
                link(nc.vector.bn_stats(small[:, 16 + 6 * t:22 + 6 * t], vbuf[:, t, :]))
                link(nc.vector.bn_aggr(small[:, 28 + 2 * t:30 + 2 * t], small[:, 16 + 6 * t:22 + 6 * t]))
                link(ts(stat[:, t:t + 1], small[:, 29 + 2 * t:30 + 2 * t], EPS, None, ALU.add))
            rsqrt(stat[:, 2:4], stat[:, 0:2], stat[:, 4:6])
            for t in range(TT):
                link(ts(vbuf[:, t, :], vbuf[:, t, :], small[:, 28 + 2 * t:29 + 2 * t], stat[:, 2 + t:3 + t],
                        ALU.subtract, ALU.mult))
            link(tt(vbuf, vbuf, gm_gb[:, 0:1, :].broadcast_to([P, TT, N]), ALU.mult))
            tt(vbuf, vbuf, gm_gb[:, 1:2, :].broadcast_to([P, TT, N]), ALU.add).then_inc(v_ready, 1)
            dve.wait_ge(spatial_done, 1)
            for t in range(TT):
                last = tt(vbuf[:, t, :].rearrange("p (h d) -> p h d", h=4),
                          (S[0] if t else T).rearrange("p (h d) -> p h d", h=4),
                          b_s.unsqueeze(2).broadcast_to([P, 4, HD]), ALU.add)
            last.then_inc(mixed_saved, 1)
            dve.wait_ge(mixed_saved, 1)
            dve.wait_ge(gelu_u, 1)
            tt(bufB[:], bufB[:], bufA[:], ALU.mult).then_inc(gated, 1)
            link(stt(scale_ffn[:], modcol[:, 4, :, 0], 1.0, ffn_g, ALU.add, ALU.mult))
            tt(wr_scaled[:], wr[:], scale_ffn[:].unsqueeze(2).broadcast_to([P, KT, NE]), ALU.mult) \
                .then_inc(wr_ready, 1)
            dve.wait_ge(bcast_saved, 4)
            for g in range(4):
                dve.wait_ge(slot_free, used_out(g))
                b = 2 if g % 2 == 0 else 0
                for t in range(TT):
                    last = tt(work[:, t * N:(t + 1) * N], Z[b + t], gate_b[:, g * N:(g + 1) * N], ALU.mult)
                link(last)
                h_g = tokens[:, 0:TT, g * N:(g + 1) * N]
                tt(h_g, h_g, work[:].rearrange("p (t n) -> p t n", t=TT), ALU.add).then_inc(h_ready, 1)
            dve.wait_ge(hsq_done, 8)
            link(nc.vector.tensor_reduce(stat[:, 0:2], hsq[:], AX.X, ALU.add))
            link(ts(stat[:, 0:2], stat[:, 0:2], 1.0 / D, EPS, ALU.mult, ALU.add))
            rsqrt(rs_tok[:, 0:2], stat[:, 0:2], stat[:, 2:4])
            rs2 = rs_tok[:, 0:2].unsqueeze(2).broadcast_to([P, TT, NE])
            dve.wait_ge(logit_done, 1)
            nc.vector.tensor_copy(rrow[:], T[0:1, 64:64 + NE]).then_inc(rbias_row, 1)
            link(tt(rt[:, 0], T[:, 0:2 * NE].rearrange("p (t e) -> p t e", t=TT), rs2, ALU.mult))
            dve.wait_ge(logit_done, 2)
            rb = rt[:, 2, 0:1, :]
            link(nc.vector.tensor_copy(rt[:, 2, 0, :], S[0][:, 0:NE]))
            tt(rt[:, 0], rt[:, 0], rb.broadcast_to([P, TT, NE]), ALU.add).then_inc(logit_saved, 1)
            dve.wait_ge(score_saved, 1)
            scores, sel = rt[:, 1], rt[:, 3]
            link(tt(sel, scores, rbias[:].unsqueeze(1).broadcast_to([P, TT, NE]), ALU.add))
            v = sel.rearrange("p t (g a b) -> p (t g) a b", g=NG, a=2)

            def g8(i):
                return rt[:, i].rearrange("p t e -> p (t e)")[:, 0:16].rearrange("p (g a) -> p g a", a=2)

            def g1(i):
                return rt[:, i].rearrange("p t e -> p (t e)")[:, 0:8]

            hi, lo = g8(4), g8(5)
            link(tt(hi, v[:, :, :, 0], v[:, :, :, 1], ALU.max))
            link(tt(lo, v[:, :, :, 0], v[:, :, :, 1], ALU.min))
            link(tt(g1(6), hi[:, :, 0], hi[:, :, 1], ALU.max))
            link(tt(g1(7), hi[:, :, 0], hi[:, :, 1], ALU.min))
            link(tt(g1(8), lo[:, :, 0], lo[:, :, 1], ALU.max))
            link(tt(g1(7), g1(7), g1(8), ALU.max))
            link(tt(g1(6), g1(6), g1(7), ALU.add))

            def first_max(values, numbers, n, mx, eq, low, hot):
                shape = [P, TT, n]
                link(nc.vector.tensor_reduce(mx, values, AX.X, ALU.max))
                link(tt(eq, values, mx.unsqueeze(2).broadcast_to(shape), ALU.is_equal))
                link(tt(eq, eq, numbers.unsqueeze(1).broadcast_to(shape), ALU.mult))
                link(nc.vector.tensor_reduce(low, eq, AX.X, ALU.min))
                link(tt(hot, numbers.unsqueeze(1).broadcast_to(shape), low.unsqueeze(2).broadcast_to(shape),
                        ALU.is_equal))

            gsc = g1(6).rearrange("p (t g) -> p t g", t=TT)
            geq = g1(8).rearrange("p (t g) -> p t g", t=TT)
            ghot = g1(9).rearrange("p (t g) -> p t g", t=TT)
            first_max(gsc, k_("g4"), NG, small[:, 0:2], geq, small[:, 2:4], ghot)
            masked = rt[:, 10]
            link(ts(geq, ghot, BIG, -BIG, ALU.mult, ALU.add))
            m4 = masked.rearrange("p t (g e) -> p (t g) e", e=EPG)
            link(tt(m4, sel.rearrange("p t (g e) -> p (t g) e", e=EPG),
                    g1(9).unsqueeze(2).broadcast_to([P, 2 * NG, EPG]), ALU.mult))
            link(tt(m4, m4, g1(8).unsqueeze(2).broadcast_to([P, 2 * NG, EPG]), ALU.add))
            first_max(masked, k_("e16"), NE, small[:, 0:2], rt[:, 11], small[:, 2:4], rt[:, 12])
            link(ts(rt[:, 11], rt[:, 12], -3 * BIG, None, ALU.mult))
            link(tt(masked, masked, rt[:, 11], ALU.add))
            first_max(masked, k_("e16"), NE, small[:, 0:2], rt[:, 11], small[:, 2:4], rt[:, 13])
            mask, gates = rt[:, 15], rt[:, 14]
            link(tt(mask, rt[:, 12], rt[:, 13], ALU.add))
            for t in range(TT):
                last = nc.vector.tensor_copy(cand[:, t, 0, :].rearrange("p (b e) -> p b e", b=NBLK),
                                             rt[:, 15, t:t + 1, :].broadcast_to([P, NBLK, NE]))
            last.then_inc(mask_ready, 1)
            link(tt(gates, scores, mask, ALU.mult))
            link(nc.vector.tensor_reduce(small[:, 0:2], gates, AX.X, ALU.add))
            link(nc.vector.reciprocal(small[:, 2:4], small[:, 0:2]))
            link(tt(gates, gates, small[:, 2:4].unsqueeze(2).broadcast_to([P, TT, NE]), ALU.mult))
            dve.wait_ge(pos_done, 1)
            pos = rt[:, 16]
            link(ts(pos, T[:, 0:2 * NE].rearrange("p (t e) -> p t e", t=TT), 1.0, None, ALU.add))
            link(ts(vcol[:, 2:3], T[0:CAND, 128:129], k_("blk_lo")[0:CAND, :], float(BASE),
                    ALU.subtract, ALU.is_gt))
            ts(vcol[:, 0:1], T[0:CAND, 128:129], k_("blk_lo")[0:CAND, :], None, ALU.is_gt).then_inc(count_saved, 1)
            link(tt(pos, pos, mask, ALU.mult))
            link(ts(pos, pos, -1.0, None, ALU.add))
            lows = k_("cand_lo").rearrange("p (b e) -> p b e", b=NBLK)
            for t in range(TT):
                tt(cand[:, t, 0, :].rearrange("p (b e) -> p b e", b=NBLK),
                   rt[:, 16, t:t + 1, :].broadcast_to([P, NBLK, NE]), lows, ALU.subtract)
                last = nc.vector.tensor_copy(cand[:, t, 1, :].rearrange("p (b e) -> p b e", b=NBLK),
                                             rt[:, 14, t:t + 1, :].broadcast_to([P, NBLK, NE]))
            last.then_inc(cand_ready, 1)
            dve.wait_ge(order_done, 1)
            link(nc.vector.tensor_copy(vcol[:, 1:2], T[0:CAND, 0:1]))
            link(nc.vector.tensor_copy(n_i[:, 2 * JOBS:2 * JOBS + 1], T[0:1, 2:3]))
            dve.wait_ge(count_saved, 1)
            ts(onehot_j[:], k_("jobno")[0:CAND, :], vcol[:, 1:2], vcol[:, 0:1], ALU.is_equal, ALU.mult) \
                .then_inc(table_oh, 1)
            dve.wait_ge(candT_done, 1)
            nc.vector.tensor_copy(candT.rearrange("c t i p -> c (t i p)"), S[0][0:CAND, :]).then_inc(table_oh, 1)
            dve.wait_ge(table_done, 1)
            link(nc.vector.tensor_copy(job.rearrange("p i t j -> p (i t j)"), S[1][:, 0:4 * JOBS]))
            nc.vector.tensor_copy(n_i[:, 0:2 * JOBS], S[1][0:1, 256:256 + 2 * JOBS]).then_inc(table_ready, 1)
            dve.wait_ge(table_ready, 1)

            def gather_matrix(j):
                for t in range(TT):
                    last = ts(oh_in[:, t, :], k_("slots"), job[:, 0, t, bass.ds(j, 1)], rs_tok[:, t:t + 1],
                              ALU.is_equal, ALU.mult)
                last.then_inc(oh_ready, 1)

            def spread_matrix(j):
                for t in range(TT):
                    last = ts(oh_out[:, t, :], k_("slots"), job[:, 0, t, bass.ds(j, 1)],
                              job[:, 1, t, bass.ds(j, 1)], ALU.is_equal, ALU.mult)
                return last

            def hidden_product(j, wide):
                dve.wait_ge(silu_saved, j + 1)
                dve.wait_ge(slot_free, j * JCH + used_chunk(NPRE + 15))
                for i in range(1 + wide):
                    last = tt(hidden[i], silu_g[i], Ub[i], ALU.mult)
                last.then_inc(hidden_ready, 1)
                dve.wait_ge(ehT_done, j + 1)
                nc.vector.tensor_copy(spread_T[0:BLK].rearrange("p t n -> p (t n)"), Ub[0][0:BLK, 0:SEQ]) \
                    .then_inc(spread_saved, 1)
                dve.wait_ge(slot_free, j * JCH + used_chunk(NPRE + 23))
                save_outputs(dve, nc.vector.tensor_copy, 1, wide)

            jobs = dve.value_load(n_i[0:1, 2 * JOBS:2 * JOBS + 1], min_val=1, max_val=JOBS - 1)
            gather_matrix(0)
            dve.wait_ge(y_zeroed, 1)
            with dve.Fori(0, jobs) as j:
                wide = dve.value_load(n_i[0:1, bass.ds(j + JOBS, 1)], min_val=0, max_val=1)
                dve.wait_ge(gathered, j * 2 + 2)
                gather_matrix(j + 1)
                spread_matrix(j)
                with dve.If(wide):
                    hidden_product(j, True)
                with dve.Else():
                    hidden_product(j, False)
                for t in range(TT):
                    for h in range(2):
                        dve.wait_ge(scattered, j * 4 + (2 * t + h + 1))
                        y = yacc[:, t, h, :]
                        tt(y, Yb[:, 2 * h:2 * h + 2, :].rearrange("p a n -> p (a n)"), y, ALU.add) \
                            .then_inc(summed, 1)
            dve.wait_ge(summed, jobs * 4 + 4)
            dve.wait_ge(bcast_saved, 8)
            for q in range(4):
                t, h = q // 2, q % 2
                y = yacc[:, t, h, :]
                link(tt(y, y, gate_b[:, h * 1024:(h + 1) * 1024], ALU.mult))
                o = tokens[:, t, h * 1024:(h + 1) * 1024]
                tt(o, o, y, ALU.add).then_inc(out_ready, 1)


INPUTS = ["x", "c", "ctx", "c_ctx", "w_mod", "b_mod", "norm_mix_g", "norm_ffn_g", "w_in", "w_out",
          "q_norm_g", "k_norm_g", "attn_sink", "gmlp_ln_g", "gmlp_ln_b", "gmlp_w_s", "gmlp_b_s", "conv_w",
          "conv_b", "conv_ln_g", "conv_ln_b", "w_router", "router_bias", "w_gate", "w_up", "w_down"]
SHAPES = {"x": (SEQ, D), "ctx": (SEQ, D), "c": (16, P), "c_ctx": (16, P), "norm_mix_g": (16, P),
          "norm_ffn_g": (16, P), "gmlp_b_s": (4, P), "conv_ln_g": (4, P), "conv_ln_b": (4, P),
          "w_mod": (D, 6 * D), "b_mod": (1, 6 * D), "w_in": (D, 3584), "w_out": (D, D),
          "q_norm_g": (1, HD), "k_norm_g": (1, HD), "attn_sink": (1, NH), "gmlp_ln_g": (1, N),
          "gmlp_ln_b": (1, N), "gmlp_w_s": (4, P, P), "conv_w": (CW, N), "conv_b": (1, N),
          "w_router": (D, NE), "router_bias": (1, NE), "w_gate": (NE, D, FE), "w_up": (NE, D, FE),
          "w_down": (NE, FE, D)}


def kernel(**inputs):
    import concourse.bacc as bacc
    from concourse.bass_utils import run_bass_kernel_spmd

    nc = bacc.Bacc("TRN2", target_bir_lowering=False, num_devices=1)
    arrays, args = {}, []
    for name in INPUTS:
        a = np.ascontiguousarray(inputs[name]).reshape(SHAPES[name])
        arrays[name + "_dram"] = a
        args.append(nc.dram_tensor(name + "_dram", a.shape, F32, kind="ExternalInput").ap())
    _, _, tables = constants()
    table = np.concatenate([np.broadcast_to(v, (P, v.shape[1])) for v in tables.values()], 1).astype(np.float32)
    arrays["tables_dram"] = np.ascontiguousarray(table)
    args.append(nc.dram_tensor("tables_dram", table.shape, F32, kind="ExternalInput").ap())
    out = nc.dram_tensor("out_dram", (SEQ, D), F32, kind="ExternalOutput").ap()
    build(nc, *args, out)
    r = run_bass_kernel_spmd(nc, [arrays], core_ids=[0])
    return r.results[0]["out_dram"].reshape(1, SEQ, D)
```

```python
from contextlib import ExitStack

import numpy as np

import concourse.bass as bass
from concourse import mybir

F32 = mybir.dt.float32
I32 = mybir.dt.int32
ALU = mybir.AluOpType
ACT = mybir.ActivationFunctionType
AX = mybir.AxisListType

P = 128
D = 2048
KT = D // P
SEQ = 256
TT = SEQ // P
HD = 128
NH, NKV = 8, 2
GRID_W = 64
CW = 31
PAD = CW // 2
NE, NG, EPG = 16, 4, 4
FE = 1024
EPS = 1e-6
BIG = 1e30
N = 512

SLOTS = 8
PRE_SLOTS = 6
HALF = D // 2
HALF_SLOTS = 4
CH = 2048
BASE, REST = 64, 32
BLK = BASE + REST
NBLK = -(-SEQ // BLK)
CAND = NBLK * NE
JOBS = NE + (2 * SEQ - NE) // BLK + 1
JCH = 24

GROUPS = [("a", 2560), ("g", 3072), ("q0", 0), ("kv", 1024), ("q1", 512), ("v", 2048), ("u", 1536)]
A_, G_, Q0_, KV_, Q1_, V_, U_ = range(7)


def make_schedule():
    seq = [("mod", 0, 0, c) for c in range(4)] + [("tok", 0)]
    seq += [("mod", 0, 1, 0), ("mod", 0, 1, 1), ("tok", 1), ("mod", 0, 1, 2), ("mod", 0, 1, 3),
            ("ext", 0, 0), ("tok", 2), ("ext", 0, 1), ("tok", 3)]
    for b in range(4):
        mods = [("mod", b + 1, p, c) for p in range(2) for c in range(4)] if b < 3 else []
        seq += mods[0:3] + [("win", A_, 2 * b), ("win", A_, 2 * b + 1)]
        seq += mods[3:6] + [("win", G_, 2 * b)] + [("ext", b + 1, 0)] * (b < 3) + [("win", G_, 2 * b + 1)]
        seq += mods[6:8] + [("win", Q0_, 2 * b)] + [("ext", b + 1, 1)] * (b < 3) + [("win", Q0_, 2 * b + 1)]

    after = {
        (KV_, 1): [("qT", 0)], (KV_, 3): [("convsum",)], (Q1_, 0): [("convsq",)],
        (Q1_, 1): [("kT",)], (V_, 2): [("qT", 1)], (U_, 3): [("spatial",)],
    }
    halves = {2: 0, 4: 1, 6: 2}
    heads = [("head", h, s) for h in range(NH) for s in range(3)]
    hpos = 0
    for g in range(KV_, 7):
        for c in range(4):
            seq.append(("win", g, 2 * c))
            busy = (g, c) >= (Q1_, 3) and hpos < len(heads)
            if busy:
                seq.append(heads[hpos + 1])
            seq.append(("win", g, 2 * c + 1))
            seq += after.get((g, c), [])
            if busy:
                seq.append(heads[hpos + 2])
                hpos += 3
            if (g, c) >= (Q1_, 2) and hpos < len(heads):
                seq.append(heads[hpos])
                if heads[hpos][1] in halves:
                    seq.append(("half", halves[heads[hpos][1]]))
    seq += [("bcast", 0), ("bcast", 1)]
    after = {(0, 0): [("bcast", 2), ("bcast", 3)], (0, 1): [("gated",), ("half", 3)],
             (1, 1): [("half", 4)], (2, 1): [("half", 5)], (3, 1): [("half", 6)]}
    for g in range(4):
        for c in range(4):
            seq.append(("wout", g, c))
            if g and c == 0:
                seq.append(("hT", g - 1))
            seq += after.get((g, c), [])
    return seq + [("hT", 3), ("route", 0), ("half", 7), ("route", 1), ("route", 2), ("route", 3)]


SCHEDULE = make_schedule()
CHUNK_STEPS = [s for s in SCHEDULE if s[0] in ("mod", "wout") or (s[0] == "win" and s[2] % 2 == 0)]
NPRE = len(CHUNK_STEPS)
NUMBER = {s: n for n, s in enumerate(CHUNK_STEPS)}


def constants():
    p = np.arange(P)[:, None]
    c = np.arange(P)[None, :]
    f = np.float32
    rows = SEQ // GRID_W
    row = np.repeat(np.arange(rows, dtype=f), GRID_W)
    col = np.tile(np.arange(GRID_W, dtype=f), rows)
    nf = HD // 4
    inv = (f(10000.0) ** (-np.arange(nf, dtype=f) / f(nf))).astype(f)
    ang = np.concatenate([row[:, None] * inv, col[:, None] * inv], axis=-1)
    cos, sin = np.cos(ang), np.sin(ang)
    cosd = np.concatenate([cos, cos], 1).reshape(TT, P, HD).transpose(1, 0, 2).reshape(P, -1)
    sind = np.concatenate([-sin, sin], 1).reshape(TT, P, HD).transpose(1, 0, 2).reshape(P, -1)
    cand = np.arange(CAND)
    one = np.ones((P, 1))
    t = {
        "ident": p == c,
        "before": p < c,
        "mask0": np.where(c <= p, 0, -BIG),
        "mask1": np.where(c >= p, 0, -BIG),
        "slots": one * np.arange(BLK)[None],
        "jobno": one * np.arange(JOBS)[None],
        "sel": (p % 32 == np.arange(2)[None]),
        "spread": (p == 32 * (np.arange(N) // P)[None]),
        "blk_lo": (np.arange(P)[:, None] // NE) * BLK,
        "expert": np.arange(P)[:, None] % NE,
        "cand_lo": one * ((cand // NE) * BLK)[None],
        "g4": one * (np.arange(NG) - 2 * NG)[None],
        "e16": one * (np.arange(NE) - 2 * NE)[None],
        "ones": one * np.ones((1, P)),
        "cos": cosd, "sin": sind,
    }
    at, cols = {}, 0
    for k, v in t.items():
        at[k] = (cols, v.shape[1])
        cols += v.shape[1]
    return at, cols, t


CONST_AT, ALL_COLS, _ = constants()
CONST_COLS = CONST_AT["cos"][0]


def build(nc, x, c, ctx, c_ctx, w_mod, b_mod, norm_mix_g, norm_ffn_g, w_in, w_out, q_norm_g, k_norm_g,
          attn_sink, gmlp_ln_g, gmlp_ln_b, gmlp_w_s, gmlp_b_s, conv_w, conv_b, conv_ln_g, conv_ln_b,
          w_router, router_bias, w_gate, w_up, w_down, consts, out):
    with ExitStack() as stack:
        def sb(name, shape, dt=F32):
            return stack.enter_context(nc.sbuf_tensor(name, shape, dt))

        def sem(name):
            return stack.enter_context(nc.semaphore(name))

        ring = sb("ring", [P, SLOTS, CH])
        const = sb("const", [P, CONST_COLS])
        tokens = sb("tokens", [P, 2 * TT, D])
        nT_all = sb("nT_all", [P, KT * 2 * SEQ])
        early = sb("early", [P, 2, D])
        halves = sb("halves", [P, 2, HALF])
        modrow = sb("modrow", [P, 2, N])
        silu_c = sb("silu_c", [P, KT, 32])
        rows = sb("rows", [108, P])
        cols = sb("cols", [P, 76])
        modcol = sb("modcol", [P, 5, KT, 2])
        scale_mix = sb("scale_mix", [P, KT, 2])
        scale_ffn = sb("scale_ffn", [P, KT])
        qk_gain = sb("qk_gain", [P, 2, HD])
        sink = sb("sink", [P, NH])
        neg_sink = sb("neg_sink", [P, NH])
        rbias = sb("rbias", [P, NE])
        gm_gb = sb("gm_gb", [P, 2, N])
        w_sT = sb("w_sT", [P, 4, P])
        conv_cols = sb("conv_cols", [P, 4, CW + 1])
        wr = sb("wr", [P, KT, NE])
        wr_scaled = sb("wr_scaled", [P, KT, NE])
        stat = sb("stat", [P, 8])
        ss = sb("ss", [P, 8])
        rs_tok = sb("rs_tok", [P, 2 * TT])
        rope = sb("rope", [P, 4, TT, HD])
        work = sb("work", [P, 1024])
        heads = sb("heads", [P, 1024])
        yT = sb("yT", [P, 4, SEQ + 2 * PAD])
        bufA = sb("bufA", [P, 1024])
        bufB = sb("bufB", [P, 1024])
        probs = sb("probs", [P, 2, N])
        small = sb("small", [P, 64])
        n_i = sb("n_i", [1, 2 * JOBS + 1], I32)
        hsq = sb("hsq", [P, TT, 4])
        onehot_j = sb("onehot_j", [CAND, JOBS])
        vcol = sb("vcol", [CAND, 4])
        rrow = sb("rrow", [1, NE])

        def k_(name):
            at, n = CONST_AT[name]
            if at >= CONST_COLS:
                return heads[:, at - CONST_COLS:at - CONST_COLS + n]
            return const[:, at:at + n]

        ident, ones = k_("ident"), k_("ones")
        mixT = tokens[:, TT:2 * TT, :].rearrange("p a d -> p (a d)").rearrange("p (k t) -> p k t", k=KT)
        nT = nT_all[:].rearrange("p (k t) -> p k t", k=KT)
        yacc = nT_all[:, 0:TT * D].rearrange("p (t h n) -> p t h n", t=TT, h=2)
        hrT = nT_all[:, TT * D:].rearrange("p (k t) -> p k t", k=KT)
        tail = TT * D
        def part(buf, at, n):
            return buf[:, at:at + n]

        xg = part(nT_all, tail, KT * BLK).rearrange("p (k s) -> p k s", k=KT)
        outs = part(nT_all, tail + 1536, D)
        spread_T = part(nT_all, tail + 3584, 256).rearrange("p (t n) -> p t n", t=TT)
        hT = [part(bufA, 0, 512), part(nT_all, tail + 3840, 256)]
        silu_g = [part(work, 0, 512), part(bufA, 512, 256)]
        hidden = [part(work, 512, 512), part(bufA, 768, 256)]
        oh_in = part(bufB, 0, TT * BLK).rearrange("p (t s) -> p t s", t=TT)
        oh_out = part(bufB, 256, TT * BLK).rearrange("p (t s) -> p t s", t=TT)
        w_s = work[:, 0:N].rearrange("p (h q) -> p h q", h=4)
        conv_rows = work[0:CW + 1, N:2 * N]
        bc = probs[:].rearrange("p t n -> p (t n)")[:, 0:3 * SEQ].rearrange("p (i t) -> p i t", i=3)
        rt = heads[:, 0:24 * TT * NE].rearrange("p (i t e) -> p i t e", i=24, t=TT)
        yT_flat = yT[:].rearrange("p c t -> p (c t)")
        probsT = yT_flat[:, 0:4 * SEQ].rearrange("p (k t) -> p k t", k=4)
        cand = yT_flat[:, 0:4 * CAND].rearrange("p (t i c) -> p t i c", t=TT, i=2)
        candT = yT_flat[0:CAND, 256:768].rearrange("c (t i p) -> c t i p", t=TT, i=2)
        job = yT_flat[:, 768:768 + 4 * JOBS].rearrange("p (i t j) -> p i t j", i=2, t=TT)
        qT = early[:, 0, :].rearrange("p (h t) -> p h t", h=NH)
        kT = early[:, 1, 0:1024].rearrange("p (h t) -> p h t", h=NKV)
        vtok = early[:, 1, 1024:2048].rearrange("p (t n) -> p t n", t=2 * TT)
        gate_b = early[:, 0, :]
        acc = bufB[:].rearrange("p (c t) -> p c t", c=4)
        aT = bufA[:].rearrange("p (c t) -> p c t", c=4)
        vbuf = bufA[:].rearrange("p (t n) -> p t n", t=TT)
        ubuf = bufB[:].rearrange("p (t n) -> p t n", t=TT)
        mix_g, ffn_g = cols[:, 0:16], cols[:, 16:32]
        b_s, cv_g, cv_b = cols[:, 32:36], cols[:, 36:40], cols[:, 40:44]
        b_mix = cols[:, 44:76].rearrange("p (s k) -> p s k", s=2)
        half_slots = ring[:, PRE_SLOTS:SLOTS, :].rearrange("p s (h n) -> p (s h) n", h=2)

        ps = stack.enter_context(nc.psum_tensor("ps", [P, 8, N], F32))
        Z = [ps[:, i, :] for i in range(4)]
        S = [ps[:, 4, :], ps[:, 5, :]]
        T, M = ps[:, 6, :], ps[:, 7, :]
        Gb, Ub, Db = [ps[:, 0, :], ps[:, 1, 0:256]], [ps[:, 2, :], ps[:, 3, 0:256]], [ps[:, 0:2, :], ps[:, 2, :]]
        Xb = Yb = ps[:, 4:8, :]
        pair = {A_: 0, G_: 2, Q0_: 4, KV_: 0, Q1_: 0, V_: 2, U_: 0}

        rows_in, const_in, tok_in, ctx_in, setup_in, misc_in, wr_in = (sem(s) for s in (
            "rows_in", "const_in", "tok_in", "ctx_in", "setup_in", "misc_in", "wr_in"))
        half_in = [sem(f"half_in{i}") for i in range(HALF_SLOTS)]
        bias_in, half_zero = sem("bias_in"), sem("half_zero")
        half_step, half_done, half_saved = sem("half_step"), sem("half_done"), sem("half_saved")
        half_free = sem("half_free")
        landed = [sem(f"landed{i}") for i in range(SLOTS)]
        slot_free = sem("slot_free")
        zeroed = sem("zeroed")
        rowsT_done, cols_saved, silu_done = sem("rowsT_done"), sem("cols_saved"), sem("silu_done")
        setupT_done, wsT_saved, convc_saved = sem("setupT_done"), sem("wsT_saved"), sem("convc_saved")
        sumsq_done, scaled, tokT_done = sem("sumsq_done"), sem("scaled"), sem("tokT_done")
        tokT_act, tokT_dve = sem("tokT_act"), sem("tokT_dve")
        row_done, row_saved, ext_done, modcol_saved = (sem(s) for s in (
            "row_done", "row_saved", "ext_done", "modcol_saved"))
        scale_done, nT_ready, nC_ready = sem("scale_done"), sem("nT_ready"), sem("nC_ready")
        a_saved, g_saved, conv_done = (sem(s) for s in ("a_saved", "g_saved", "conv_done"))
        csum_done, centred, csq_saved, csq_done, cnorm = (sem(s) for s in (
            "csum_done", "centred", "csq_saved", "csq_done", "cnorm"))
        conv_saved = sem("conv_saved")
        sq_saved, qk_read, v_saved, rope_done, headT_done, headT_saved = (sem(s) for s in (
            "sq_saved", "qk_read", "v_saved", "rope_done", "headT_done", "headT_saved"))
        score_done, neg_max, exp_done, den_done, probs_done, pT_done, pT0_saved, pT1_saved, pv_done, pv_saved = (
            sem(s) for s in ("score_done", "neg_max", "exp_done", "den_done", "probs_done", "pT_done",
                             "pT0_saved", "pT1_saved", "pv_done", "pv_saved"))
        gelu_v, v_ready, spatial_done, mixed_saved, gelu_u, gated, gatedT_done, gatedT_saved = (
            sem(s) for s in ("gelu_v", "v_ready", "spatial_done", "mixed_saved", "gelu_u", "gated",
                             "gatedT_done", "gatedT_saved"))
        bcast_done, bcast_saved = sem("bcast_done"), sem("bcast_saved")
        h_ready, hT_done, hT_saved, hsq_done, wr_ready = (sem(s) for s in (
            "h_ready", "hT_done", "hT_saved", "hsq_done", "wr_ready"))
        logit_done, logit_saved, score_saved, rbias_row, mask_ready, pos_done, cand_ready, candT_done = (
            sem(s) for s in ("logit_done", "logit_saved", "score_saved", "rbias_row", "mask_ready",
                             "pos_done", "cand_ready", "candT_done"))
        count_saved, order_done, table_oh, table_done, table_ready, y_zeroed = (sem(s) for s in (
            "count_saved", "order_done", "table_oh", "table_done", "table_ready", "y_zeroed"))
        oh_ready, gathered, xg_ready, silu_saved, hidden_ready = (sem(s) for s in (
            "oh_ready", "gathered", "xg_ready", "silu_saved", "hidden_ready"))
        ehT_done, ehT_saved, o_act, o_dve, scattered, summed = (sem(s) for s in (
            "ehT_done", "ehT_saved", "o_act", "o_dve", "scattered", "summed"))
        out_ready, out_sent = sem("out_ready"), sem("out_sent")
        dve_step, spread_saved = sem("dve_step"), sem("spread_saved")

        def save_outputs(eng, copy, odd, wide):
            for q in (odd, 2 + odd):
                if wide:
                    copy(outs[BASE:BLK, q * N:(q + 1) * N], Db[1][REST * q:REST * (q + 1), :])
                copy(outs[0:BASE, q * N:(q + 1) * N], Db[0][BASE * (q // 2):BASE * (q // 2 + 1), odd, :]) \
                    .then_inc(o_dve if odd else o_act, 1)

        block = stack.enter_context(nc.Block())

        def slot(n):
            return ring[:, n % PRE_SLOTS, :]

        def used_chunk(n):
            return PRE_SLOTS + n + 1

        def used(g):
            return used_chunk(NUMBER["win", g, 6])

        def used_out(g):
            return used_chunk(NUMBER["wout", g, 3])

        def used_job(i):
            return used_chunk(NPRE + i)

        dve_count = [0]

        def link(ins):
            dve_count[0] += 1
            ins.then_inc(dve_step, 1)
            nc.vector.wait_ge(dve_step, dve_count[0])

        @block.sync
        def _(sp):
            sp.dma_start(conv_rows[0:CW, :], conv_w).then_inc(setup_in, 16)
            sp.dma_start(conv_rows[CW:CW + 1, :], conv_b).then_inc(setup_in, 16)
            sp.dma_start(w_s, gmlp_w_s.rearrange("h p q -> p h q")).then_inc(setup_in, 16)
            for n, (kind, *at) in enumerate(CHUNK_STEPS):
                sp.wait_ge(slot_free, n + 1)
                if kind == "mod":
                    b, p, q = at
                    w, col = w_mod, p * D + b * N
                elif kind == "win":
                    w, col, q = w_in, GROUPS[at[0]][1], at[1] // 2
                else:
                    w, col, q = w_out, at[0] * N, at[1]
                sp.dma_start(slot(n).rearrange("p (k n) -> p k n", k=4),
                             w[q * 4 * P:(q + 1) * 4 * P, col:col + N].rearrange("(k p) n -> p k n", p=P)) \
                    .then_inc(landed[n % PRE_SLOTS], 16)
            sp.wait_ge(table_ready, 1)
            sp.wait_ge(slot_free, used_chunk(NPRE - 1))
            jobs = sp.value_load(n_i[0:1, 2 * JOBS:2 * JOBS + 1], min_val=1, max_val=JOBS - 1)
            with sp.Fori(0, jobs) as j:
                e = sp.value_load(n_i[0:1, bass.ds(j, 1)], min_val=0, max_val=NE - 1)
                for i in range(JCH):
                    if i == PRE_SLOTS:
                        sp.wait_ge(half_step, HALF_SLOTS + 8 * KT)
                    sp.wait_ge(slot_free, j * JCH + used_job(i - SLOTS))
                    dst = ring[:, i % SLOTS, :]
                    if i < 16:
                        w = (w_gate if i < 8 else w_up)[bass.ds(e, 1)].rearrange("e k f -> (e k) f")
                        src = w[(i % 8) * 2 * P:(i % 8 + 1) * 2 * P, :].rearrange("(k p) f -> p k f", p=P)
                        dst = dst.rearrange("p (k f) -> p k f", k=2)
                    else:
                        w = w_down[bass.ds(e, 1)].rearrange("e k f -> (e k) f")
                        src = w[(i - 16) * P:(i - 15) * P, :]
                    sp.dma_start(dst, src).then_inc(landed[i % SLOTS], 16)
            for q in range(4):
                sp.wait_ge(out_ready, q + 1)
                t, h = q // 2, q % 2
                sp.dma_start(out[t * P:(t + 1) * P, h * 1024:(h + 1) * 1024],
                             tokens[:, t, h * 1024:(h + 1) * 1024]).then_inc(out_sent, 16)
            sp.wait_ge(out_sent, 64)

        @block.gpsimd
        def _(pool):
            pool.memset(silu_c[:], 0.0).then_inc(zeroed, 1)
            pool.memset(yT[:], 0.0).then_inc(zeroed, 1)
            pool.memset(small[:, 63:64], 0.0).then_inc(slot_free, PRE_SLOTS)
            pool.memset(small[:, 61:62], 0.0).then_inc(summed, 4)
            pool.dma_start(heads[:, 0:ALL_COLS - CONST_COLS], consts[:, CONST_COLS:ALL_COLS]).then_inc(misc_in, 16)
            for dst, v in ((qk_gain[:, 0, :], q_norm_g), (qk_gain[:, 1, :], k_norm_g), (sink[:], attn_sink)):
                pool.dma_start(dst, v.broadcast_to([P, v.shape[1]])).then_inc(misc_in, 16)
            for b in range(4):
                pool.wait_ge(scale_done, b + 1)
                for k in range(4 * b, 4 * b + 4):
                    pool.tensor_scalar(nT[:, k, SEQ:2 * SEQ], nT[:, k, SEQ:2 * SEQ], scale_mix[:, k, 1:2],
                                       modcol[:, 0, k, 1:2], ALU.mult, ALU.add).then_inc(nC_ready, 1)
            for dst, v in ((rbias[:], router_bias), (gm_gb[:, 0, :], gmlp_ln_g), (gm_gb[:, 1, :], gmlp_ln_b)):
                pool.dma_start(dst, v.broadcast_to([P, v.shape[1]])).then_inc(wr_in, 16)
            pool.dma_start(wr[:], w_router.rearrange("(k p) e -> p k e", p=P)).then_inc(wr_in, 16)

            def load_piece(piece):
                for m in range(2 * KT):
                    h, k = divmod(m, KT)
                    col = (2 + piece) * D + h * HALF
                    if k == 0:
                        pool.wait_ge(half_free, piece * 2 + (h + 1))
                        pool.memset(halves[:, h, :], 0.0).then_inc(half_zero, 1)
                        pool.wait_ge(half_zero, piece * 2 + (h + 1))
                        pool.dma_start(halves[0:1, h, :], b_mod[:, col:col + HALF]) \
                            .then_inc(bias_in, 16)
                    pool.wait_ge(half_step, piece * 2 * KT + (m + 1))
                    pool.dma_start(half_slots[:, m % HALF_SLOTS, :],
                                   w_mod[k * P:(k + 1) * P, col:col + HALF]) \
                        .then_inc(half_in[m % HALF_SLOTS], 16)

            pool.memset(small[:, 60:61], 0.0).then_inc(half_free, 2)
            pool.memset(small[:, 59:60], 0.0).then_inc(half_step, HALF_SLOTS)
            for piece in range(3):
                load_piece(piece)
            pool.wait_ge(slot_free, used(U_))
            pool.memset(nT_all[:, 0:TT * D], 0.0).then_inc(y_zeroed, 1)
            load_piece(3)

        @block.tensor
        def _(pe):
            pe.wait_ge(const_in, 16)
            pe.wait_ge(rows_in, 16 * 8)
            pe.transpose(S[0][:, 0:108], rows[:], ident[0:108, 0:108]).then_inc(rowsT_done, 1)
            pe.wait_ge(setup_in, 16 * 3)
            for q in range(4):
                pe.transpose(S[1][:, q * 32:q * 32 + 32], conv_rows[:, q * P:(q + 1) * P], ident[0:32, 0:32])
            for h in range(4):
                mm = pe.transpose(T[:, h * P:(h + 1) * P], w_s[:, h, :], ident)
            mm.then_inc(setupT_done, 1)
            pe.wait_ge(silu_done, 1)

            for step in SCHEDULE:
                kind = step[0]
                n = NUMBER.get(step if kind != "win" else (kind, step[1], step[2] // 2 * 2))
                if n is not None:
                    pe.wait_ge(landed[n % PRE_SLOTS], 16 * (n // PRE_SLOTS + 1))
                if kind == "mod":
                    b, p, c4 = step[1:]
                    if c4 == 0:
                        if b:
                            pe.wait_ge(modcol_saved, 2 * b + p - 1)
                        elif p:
                            pe.wait_ge(wsT_saved, 1)
                    for i in range(4):
                        mm = pe.matmul((T if p else M)[32 * i:32 * i + 32, :], silu_c[:, 4 * c4 + i, :],
                                       slot(n)[:, i * N:(i + 1) * N], start=(c4 == 0), stop=(c4 == 3))
                    mm.then_inc(slot_free, 1)
                elif kind == "ext":
                    b, p = step[1:]
                    pe.wait_ge(row_saved, 2 * b + p + 1)
                    for q in range(4):
                        mm = pe.matmul((T if p else M)[:, 2 * q:2 * q + 2], modrow[:, p, q * P:(q + 1) * P],
                                       k_("sel"), start=True, stop=True)
                    mm.then_inc(ext_done, 1)
                elif kind == "tok":
                    t = step[1]
                    pe.wait_ge(scaled, t + 1)
                    for q in range(4):
                        if t >= 1:
                            pe.wait_ge(tokT_act if q % 2 else tokT_dve, 2 * (t - 1) + q // 2 + 1)
                        for i in range(4):
                            k = 4 * q + i
                            mm = pe.transpose(Z[q][:, i * P:(i + 1) * P], early[:, t % 2, k * P:(k + 1) * P], ident)
                        mm.then_inc(tokT_done, 1)
                elif kind == "half":
                    i = step[1]
                    pe.wait_ge(half_step, HALF_SLOTS + KT * (i + 1))
                    if i == 0:
                        pe.wait_ge(modcol_saved, 8)
                    else:
                        pe.wait_ge(half_saved, i)
                    if i == 3:
                        pe.wait_ge(bcast_saved, 4)
                    if i in (0, 1, 6, 7):
                        for r in range(2):
                            b = 2 * (i % 2) + r
                            mm = pe.matmul(M[32 * b:32 * b + 32, :], ones[:, 0:32],
                                           halves[:, i % 2, r * N:(r + 1) * N], start=True, stop=True)
                    else:
                        for q in range(8):
                            mm = pe.matmul(M[:, q:q + 1], halves[:, i % 2, q * P:(q + 1) * P], ones[:, 0:1],
                                           start=True, stop=True)
                    mm.then_inc(half_free, 1)
                elif kind == "bcast":
                    i = step[1]
                    if i == 0:
                        pe.wait_ge(half_saved, 3)
                    else:
                        pe.wait_ge(bcast_saved, i)
                    pe.matmul(M, k_("spread")[:, i * P:(i + 1) * P], modrow[:, 0, :], start=True, stop=True) \
                        .then_inc(bcast_done, 1)
                elif kind == "win":
                    g, half = step[1:]
                    if half == 0:
                        if g == A_:
                            pe.wait_ge(tokT_act, 8)
                            pe.wait_ge(tokT_dve, 8)
                        elif g == Q0_:
                            pe.wait_ge(cols_saved, 1)
                            pe.wait_ge(convc_saved, 1)
                            pe.wait_ge(silu_done, 1)
                        elif g == KV_:
                            pe.wait_ge(a_saved, 1)
                            pe.wait_ge(g_saved, 1)
                        elif g == Q1_:
                            pe.wait_ge(qk_read, 2)
                            pe.wait_ge(v_saved, 2)
                        elif g == V_:
                            pe.wait_ge(qk_read, 2)
                        elif g == U_:
                            pe.wait_ge(qk_read, 3)
                    b = pair[g]
                    for i in range(2):
                        k = 2 * half + i
                        w = slot(n).rearrange("p (k n) -> p k n", k=4)[:, (half % 2) * 2 + i, :]
                        if g == A_:
                            pe.wait_ge(nT_ready, k + 1)
                        if g in (A_, G_):
                            for q in range(4):
                                mm = pe.matmul(Z[b + q // 2][:, (q % 2) * SEQ:(q % 2 + 1) * SEQ],
                                               w[:, q * P:(q + 1) * P], nT[:, k, 0:SEQ],
                                               start=(k == 0 and q % 2 == 0), stop=(k == KT - 1),
                                               skip_group_check=True)
                        else:
                            for t in range(TT):
                                mm = pe.matmul(ps[:, b + t, :], nT[:, k, t * P:(t + 1) * P], w,
                                               start=(k == 0), stop=(k == KT - 1))
                        if g == KV_:
                            pe.wait_ge(nC_ready, k + 1)
                            for t in range(TT):
                                mm = pe.matmul(Z[2 + t], nT[:, k, SEQ + t * P:SEQ + (t + 1) * P], w,
                                               start=(k == 0), stop=(k == KT - 1))
                    if half % 2 == 1:
                        mm.then_inc(slot_free, 1)
                elif kind == "convsum":
                    pe.wait_ge(conv_done, 1)
                    pe.wait_ge(modcol_saved, 8)
                    for q in range(4):
                        mm = pe.matmul(T[:, 0:SEQ], ones, acc[:, q, :], start=(q == 0), stop=(q == 3))
                    mm.then_inc(csum_done, 1)
                elif kind == "convsq":
                    pe.wait_ge(csq_saved, 1)
                    for q in range(4):
                        mm = pe.matmul(T[:, SEQ:2 * SEQ], ones, aT[:, q, :], start=(q == 0), stop=(q == 3))
                    mm.then_inc(csq_done, 1)
                elif kind == "kT":
                    pe.wait_ge(rope_done, 2)
                    pe.wait_ge(headT_saved, 1)
                    for t in range(2 * TT):
                        for h in range(NKV):
                            mm = pe.transpose(S[t // 2][:, h * SEQ + (t % 2) * P:h * SEQ + (t % 2 + 1) * P],
                                              heads[:, t * SEQ + h * HD:t * SEQ + (h + 1) * HD], ident)
                    mm.then_inc(headT_done, 1)
                elif kind == "qT":
                    g = step[1]
                    pe.wait_ge(rope_done, 3 if g else 1)
                    if g:
                        pe.wait_ge(pT0_saved, 4)
                    for t in range(TT):
                        if g:
                            pe.wait_ge(headT_saved, 2 + t)
                            if t == 0:
                                pe.wait_ge(cnorm, 1)
                        for h in range(4):
                            mm = pe.transpose((T if g else S[t])[:, h * P:(h + 1) * P],
                                              heads[:, t * N + h * HD:t * N + (h + 1) * HD], ident)
                        if g or t:
                            mm.then_inc(headT_done, 1)
                elif kind == "head":
                    h, part = step[1:]
                    kv = h // (NH // NKV)
                    if part == 0:
                        if h == 0:
                            pe.wait_ge(headT_saved, 2)
                        if h == 4:
                            pe.wait_ge(headT_saved, 4)
                        for t in range(TT):
                            if h:
                                pe.wait_ge(pv_saved if t else pT1_saved, h)
                            pe.matmul(S[t], qT[:, h, t * P:(t + 1) * P], kT[:, kv, :], start=True, stop=True)
                            mm = pe.matmul(S[t][:, (1 - t) * P:(2 - t) * P], ident, k_(f"mask{t}"),
                                           start=False, stop=True, skip_group_check=True)
                        mm.then_inc(score_done, 1)
                    elif part == 1:
                        pe.wait_ge(probs_done, h + 1)
                        if h == 0:
                            pe.wait_ge(cnorm, 1)
                        if h:
                            pe.wait_ge(pT0_saved, h)
                        for t in range(TT):
                            for q in range(4):
                                mm = pe.transpose((S[0] if t else T)[:, q * P:(q + 1) * P],
                                                  probs[:, t, q * P:(q + 1) * P], ident)
                            mm.then_inc(pT_done, 1)
                    else:
                        pe.wait_ge(pT0_saved, h + 1)
                        pe.wait_ge(pT1_saved, h + 1)
                        for q in range(4):
                            mm = pe.matmul(S[1][:, 0:SEQ], vtok[:, q, kv * HD:(kv + 1) * HD], probsT[:, q, :],
                                           start=(q == 0), stop=(q == 3))
                        mm.then_inc(pv_done, 1)
                elif kind == "spatial":
                    pe.wait_ge(v_ready, 1)
                    pe.wait_ge(pT0_saved, NH)
                    pe.wait_ge(pT1_saved, NH)
                    pe.wait_ge(headT_saved, 4)
                    for t in range(TT):
                        for h in range(4):
                            mm = pe.matmul((S[0] if t else T)[:, h * P:(h + 1) * P], w_sT[:, h, :],
                                           vbuf[:, t, h * HD:(h + 1) * HD], start=True, stop=True)
                    mm.then_inc(spatial_done, 1)
                elif kind == "gated":
                    pe.wait_ge(gated, 1)
                    for t in range(TT):
                        for h in range(4):
                            mm = pe.transpose((S[0] if t else T)[:, h * P:(h + 1) * P],
                                              ubuf[:, t, h * HD:(h + 1) * HD], ident)
                    mm.then_inc(gatedT_done, 1)
                elif kind == "wout":
                    g, c4 = step[1:]
                    b = 2 if g % 2 == 0 else 0
                    if c4 == 0:
                        if g == 0:
                            pe.wait_ge(gelu_v, 1)
                            pe.wait_ge(pv_saved, NH)
                        elif g == 1:
                            pe.wait_ge(gelu_u, 1)
                        else:
                            pe.wait_ge(h_ready, g - 1)
                    if g == 0 and c4 == 2:
                        pe.wait_ge(gatedT_saved, 1)
                    if g == 0 and c4 == 3:
                        pe.wait_ge(conv_saved, 1)
                    for i in range(4):
                        k = 4 * c4 + i
                        w = slot(n).rearrange("p (k n) -> p k n", k=4)[:, i, :]
                        for t in range(TT):
                            mm = pe.matmul(Z[b + t], mixT[:, k, t * P:(t + 1) * P], w,
                                           start=(k == 0), stop=(k == KT - 1))
                    mm.then_inc(slot_free, 1)
                elif kind == "hT":
                    g = step[1]
                    pe.wait_ge(h_ready, g + 1)
                    if g:
                        pe.wait_ge(hT_saved, g)
                    else:
                        pe.wait_ge(gatedT_saved, 1)
                    for t in range(TT):
                        for i in range(4):
                            k = 4 * g + i
                            mm = pe.transpose(S[t][:, i * P:(i + 1) * P], tokens[:, t, k * P:(k + 1) * P], ident)
                    mm.then_inc(hT_done, 1)
                elif kind == "route":
                    part = step[1]
                    if part == 0:
                        pe.wait_ge(hT_saved, 4)
                        pe.wait_ge(wr_ready, 1)
                        for t in range(TT):
                            for k in range(KT):
                                pe.matmul(T[:, t * NE:(t + 1) * NE], hrT[:, k, t * P:(t + 1) * P],
                                          wr_scaled[:, k, :], start=(k == 0), stop=(k == KT - 1))
                        for k in range(KT):
                            mm = pe.matmul(T[0:1, 64:64 + NE], modcol[:, 3, k, 0:1], wr[:, k, :],
                                           start=(k == 0), stop=(k == KT - 1))
                        mm.then_inc(logit_done, 1)
                        pe.wait_ge(rbias_row, 1)
                        pe.matmul(S[0][:, 0:NE], ones[0:1, :], rrow[:], start=True, stop=True) \
                            .then_inc(logit_done, 1)
                    elif part == 1:
                        pe.wait_ge(mask_ready, 1)
                        mask = rt[:, 15]
                        pe.matmul(T[:, 0:NE], k_("before"), mask[:, 0, :], start=True, stop=True)
                        pe.matmul(T[:, NE:2 * NE], ones, mask[:, 0, :], start=True, stop=False)
                        pe.matmul(T[:, NE:2 * NE], k_("before"), mask[:, 1, :], start=False, stop=True)
                        for t in range(TT):
                            mm = pe.matmul(T[0:CAND, 128:129], cand[:, t, 0, :], ones[:, 0:1],
                                           start=(t == 0), stop=(t == TT - 1))
                        mm.then_inc(pos_done, 1)
                    elif part == 2:
                        pe.wait_ge(count_saved, 1)
                        pe.matmul(T[0:CAND, 0:1], k_("before")[0:CAND, 0:CAND], vcol[:, 0:1],
                                  start=True, stop=True)
                        pe.matmul(T[0:1, 2:3], vcol[:, 0:1], ones[0:CAND, 0:1], start=True, stop=True) \
                            .then_inc(order_done, 1)
                        pe.wait_ge(cand_ready, 1)
                        for t in range(TT):
                            for i in range(2):
                                mm = pe.transpose(S[0][0:CAND, (2 * t + i) * P:(2 * t + i + 1) * P],
                                                  cand[:, t, i, :], ident)
                        mm.then_inc(candT_done, 1)
                    else:
                        pe.wait_ge(table_oh, 2)
                        for i in range(2):
                            for t in range(TT):
                                at = (i * TT + t) * JOBS
                                pe.matmul(S[1][:, at:at + JOBS], candT[:, t, i, :], onehot_j[:],
                                          start=True, stop=True)
                        pe.matmul(S[1][0:1, 256:256 + JOBS], k_("expert")[0:CAND, :], onehot_j[:],
                                  start=True, stop=True)
                        pe.matmul(S[1][0:1, 256 + JOBS:256 + 2 * JOBS], vcol[:, 2:3], onehot_j[:],
                                  start=True, stop=True).then_inc(table_done, 1)

            for i in range(4):
                if i == 0:
                    pe.wait_ge(half_saved, 8)
                else:
                    pe.wait_ge(bcast_saved, 4 + i)
                pe.matmul(M, k_("spread")[:, i * P:(i + 1) * P], modrow[:, 0, :], start=True, stop=True) \
                    .then_inc(bcast_done, 1)
            pe.wait_ge(bcast_saved, 8)

            def gather(half):
                for k in range(8 * half, 8 * half + 8):
                    for t in range(TT):
                        mm = pe.matmul(Xb[:, k // 4, (k % 4) * BLK:(k % 4 + 1) * BLK],
                                       tokens[:, t, k * P:(k + 1) * P], oh_in[:, t, :],
                                       start=(t == 0), stop=(t == TT - 1))
                mm.then_inc(gathered, 1)

            def experts(j, wide):
                def arrived(i):
                    before = len(range(i % SLOTS, NPRE, PRE_SLOTS)) if i % SLOTS < PRE_SLOTS else 0
                    pe.wait_ge(landed[i % SLOTS], j * (16 * JCH // SLOTS) + 16 * (before + i // SLOTS + 1))
                    return ring[:, i % SLOTS, :]

                pe.wait_ge(xg_ready, j + 1)
                for m, out_b in ((0, Gb), (1, Ub)):
                    for i in range(8):
                        w = arrived(8 * m + i).rearrange("p (k f) -> p k f", k=2)
                        for kk in range(2):
                            k = 2 * i + kk
                            for f in range(2):
                                mm = pe.matmul(out_b[0][BASE * f:BASE * (f + 1), :], xg[:, k, 0:BASE],
                                               w[:, kk, f * N:(f + 1) * N], start=(k == 0), stop=(k == KT - 1))
                        for kk in range(2 * wide):
                            k = 2 * i + kk
                            for f in range(4):
                                mm = pe.matmul(out_b[1][REST * f:REST * (f + 1), :], xg[:, k, BASE:BLK],
                                               w[:, kk, f * 256:(f + 1) * 256], start=(k == 0), stop=(k == KT - 1))
                        mm.then_inc(slot_free, 1)
                pe.wait_ge(oh_ready, j + 2)
                pe.wait_ge(summed, j * 4 + 4)
                gather(0)
                pe.wait_ge(hidden_ready, j + 1)
                for i in range(1 + wide):
                    for q in range(4 // (i + 1)):
                        pe.transpose(Gb[i][:, q * P:(q + 1) * P], hidden[i][:, q * P:(q + 1) * P], ident)
                for t in range(TT):
                    mm = pe.transpose(Ub[0][0:BLK, t * P:(t + 1) * P], oh_out[:, t, :], ident)
                mm.then_inc(ehT_done, 1)
                gather(1)
                pe.wait_ge(ehT_saved, j + 1)
                pe.wait_ge(spread_saved, j + 1)
                for i in range(8):
                    w = arrived(16 + i)
                    for q in (0, 2, 1, 3):
                        mm = pe.matmul(Db[0][BASE * (q // 2):BASE * (q // 2 + 1), q % 2, :],
                                       hT[0][:, (i % 4) * P + BASE * (i // 4):(i % 4) * P + BASE * (i // 4 + 1)],
                                       w[:, q * N:(q + 1) * N], start=(i == 0), stop=(i == 7))
                    for q in range(4 * wide):
                        mm = pe.matmul(Db[1][REST * q:REST * (q + 1), :],
                                       hT[1][:, (i % 2) * P + REST * (i // 2):(i % 2) * P + REST * (i // 2 + 1)],
                                       w[:, q * N:(q + 1) * N], start=(i == 0), stop=(i == 7))
                    mm.then_inc(slot_free, 1)
                pe.wait_ge(xg_ready, j + 2)
                rows_used = BLK if wide else BASE
                for t in range(TT):
                    for q in range(4):
                        if t == 0:
                            pe.wait_ge(o_dve if q % 2 else o_act, j * 2 + (q // 2 + 1))
                        elif q % 2 == 0:
                            pe.wait_ge(summed, j * 4 + (5 + q // 2))
                        mm = pe.matmul(Yb[:, q, :], spread_T[0:rows_used, t, :],
                                       outs[0:rows_used, q * N:(q + 1) * N], start=True, stop=True)
                        if q % 2:
                            mm.then_inc(scattered, 1)

            pe.wait_ge(table_ready, 1)
            jobs = pe.value_load(n_i[0:1, 2 * JOBS:2 * JOBS + 1], min_val=1, max_val=JOBS - 1)
            pe.wait_ge(oh_ready, 1)
            gather(0)
            gather(1)
            with pe.Fori(0, jobs) as j:
                wide = pe.value_load(n_i[0:1, bass.ds(j + JOBS, 1)], min_val=0, max_val=1)
                with pe.If(wide):
                    experts(j, True)
                with pe.Else():
                    experts(j, False)

        @block.scalar
        def _(act):
            copy = nc.scalar.copy

            act.dma_start(const[:], consts[:, 0:CONST_COLS]).then_inc(const_in, 16)
            at = 0
            for v, n in ((c, 16), (c_ctx, 16), (norm_mix_g, 16), (norm_ffn_g, 16), (gmlp_b_s, 4),
                         (conv_ln_g, 4), (conv_ln_b, 4),
                         (b_mod[:, 0:2 * D].rearrange("o (k p) -> (o k) p", p=P), 32)):
                act.dma_start(rows[at:at + n, :], v).then_inc(rows_in, 16)
                at += n
            for t in range(2 * TT):
                act.dma_start(tokens[:, t, :], (x if t < TT else ctx)[(t % TT) * P:(t % TT + 1) * P, :]) \
                    .then_inc(tok_in if t < TT else ctx_in, 16)
            act.wait_ge(zeroed, 1)
            act.wait_ge(rowsT_done, 1)
            act.activation(silu_c[:, :, 0:2], S[0][:, 0:32].rearrange("p (r k) -> p k r", r=2), ACT.Silu) \
                .then_inc(silu_done, 1)
            act.wait_ge(setupT_done, 1)
            copy(w_sT[:].rearrange("p h q -> p (h q)"), T).then_inc(wsT_saved, 1)
            for t in range(2 * TT):
                if t % TT == 0:
                    act.wait_ge(ctx_in if t else tok_in, 16 * TT)
                nowhere = ring[:, PRE_SLOTS + t % TT, :] if t >= TT else nT_all[:, t * D:(t + 1) * D]
                act.activation(nowhere, tokens[:, t, :], ACT.Square,
                               accum_out=ss[:, t:t + 1]).then_inc(sumsq_done, 1)

            def save_tokT(t):
                for q in (1, 3):
                    act.wait_ge(tokT_done, 4 * t + q + 1)
                    copy(nT[:, 4 * q:4 * q + 4, t * P:(t + 1) * P], Z[q].rearrange("p (k t) -> p k t", k=4)) \
                        .then_inc(tokT_act, 1)

            def save_rows(b, p):
                act.wait_ge(slot_free, used_chunk(NUMBER["mod", b, p, 3]))
                copy(modrow[:, p, :], T if p else M).then_inc(row_saved, 1)

            save_rows(0, 0)
            save_tokT(0)
            save_tokT(1)
            save_rows(0, 1)
            save_tokT(2)
            save_tokT(3)
            for b in range(1, 4):
                for p in range(2):
                    act.wait_ge(ext_done, 2 * b - 1 + p)
                    save_rows(b, p)
            act.wait_ge(slot_free, used(A_))
            copy(bufA[:], ps[:, 0:2, :]).then_inc(a_saved, 1)
            act.wait_ge(slot_free, used(G_))
            act.activation(bufB[:], ps[:, 2:4, :], ACT.Sigmoid).then_inc(g_saved, 1)

            def squares(idx, bank):
                if idx:
                    act.wait_ge(rope_done, idx)
                act.activation(work[:].rearrange("p (t n) -> p t n", t=TT), ps[:, bank:bank + 2, :], ACT.Square) \
                    .then_inc(sq_saved, 1)

            def save_half(i):
                act.wait_ge(half_free, i + 3)
                if i in (0, 1, 6, 7):
                    if i == 6:
                        act.wait_ge(bcast_done, 4)
                    at = 64 * (i % 2)
                    copy(modrow[at:at + 64, 0, :], M[at:at + 64, :]).then_inc(half_saved, 1)
                else:
                    at = 8 * (i % 2)
                    copy(modcol[:, 2 + i // 2, at:at + 8, 0], M[:, 0:8]).then_inc(half_saved, 1)

            act.wait_ge(slot_free, used(Q0_))
            act.wait_ge(setupT_done, 1)
            squares(0, 4)
            act.wait_ge(headT_done, 1)
            for t in range(TT):
                last = copy(qT[:, 0:4, t * P:(t + 1) * P], S[t].rearrange("p (h t) -> p h t", h=4))
            last.then_inc(headT_saved, 1)
            act.wait_ge(slot_free, used(KV_))
            act.wait_ge(rope_done, 1)
            w4 = work[:].rearrange("p (t n) -> p t n", t=2 * TT)
            act.activation(w4, ps[:, 0:4, 0:SEQ], ACT.Square).then_inc(sq_saved, 1)
            copy(vtok[:, 0:2], ps[:, 0:2, SEQ:N]).then_inc(v_saved, 1)
            copy(vtok[:, 2:4], ps[:, 2:4, SEQ:N]).then_inc(v_saved, 1)
            act.wait_ge(centred, 1)
            act.activation(bufA[:], bufB[:], ACT.Square).then_inc(csq_saved, 1)
            act.wait_ge(headT_done, 2)
            copy(kT[:, :, 0:SEQ], S[0].rearrange("p (h t) -> p h t", h=NKV))
            copy(kT[:, :, SEQ:N], S[1].rearrange("p (h t) -> p h t", h=NKV)).then_inc(headT_saved, 1)
            act.wait_ge(cnorm, 1)
            for q in range(4):
                last = act.activation(mixT[:, 12 + q, :], acc[:, q, :], ACT.Silu, bias=cv_b[:, q:q + 1],
                                      scale=cv_g[:, q:q + 1])
            last.then_inc(conv_saved, 1)
            def exps(h):
                act.wait_ge(neg_max, h + 1)
                if h:
                    act.wait_ge(pT_done, 2 * h)
                for t in range(TT):
                    act.activation(probs[:, t, :], S[t], ACT.Exp, bias=small[:, 2 + t:3 + t], scale=HD ** -0.5,
                                   accum_out=small[:, 4 + t:5 + t]).then_inc(exp_done, 1)
                for t in range(TT):
                    act.activation(small[:, 6 + t:7 + t], sink[:, h:h + 1], ACT.Exp, bias=small[:, 2 + t:3 + t]) \
                        .then_inc(exp_done, 1)

            def save_pT(h):
                if h:
                    act.wait_ge(pv_done, h)
                for t in range(TT):
                    act.wait_ge(pT_done, 2 * h + t + 1)
                    copy(probsT[:, :, t * P:(t + 1) * P], (S[0] if t else T).rearrange("p (k t) -> p k t", k=4)) \
                        .then_inc(pT1_saved if t else pT0_saved, 1)

            def save_pv(h):
                act.wait_ge(pv_done, h + 1)
                copy(mixT[:, h, :], S[1][:, 0:SEQ]).then_inc(pv_saved, 1)

            for h in range(NH):
                if h == 2:
                    act.wait_ge(slot_free, used(Q1_))
                    squares(2, 0)
                exps(h)
                if h in (2, 4, 6):
                    save_half(h // 2 - 1)
                save_pT(h)
                if h == 3:
                    for t in range(TT):
                        act.wait_ge(headT_done, 3 + t)
                        copy(qT[:, 4:8, t * P:(t + 1) * P], T.rearrange("p (h t) -> p h t", h=4)) \
                            .then_inc(headT_saved, 1)
                save_pv(h)
            act.wait_ge(slot_free, used(V_))
            act.wait_ge(csq_done, 1)
            act.activation(bufA[:], ps[:, 2:4, :], ACT.Gelu_apprx_tanh).then_inc(gelu_v, 1)
            act.wait_ge(slot_free, used(U_))
            act.activation(bufB[:], ps[:, 0:2, :], ACT.Gelu_apprx_tanh).then_inc(gelu_u, 1)
            for i in range(4):
                act.wait_ge(bcast_done, i + 1)
                copy(gate_b[:, i * N:(i + 1) * N], M).then_inc(bcast_saved, 1)
            act.wait_ge(gatedT_done, 1)
            for t in range(TT):
                last = copy(mixT[:, 8:12, t * P:(t + 1) * P], (S[0] if t else T).rearrange("p (h t) -> p h t", h=4))
            last.then_inc(gatedT_saved, 1)
            save_half(3)
            for g in range(4):
                act.wait_ge(h_ready, g + 1)
                if g:
                    act.wait_ge(hsq_done, 2 * g)
                for t in range(TT):
                    act.activation(probs[:, t, :], tokens[:, t, g * N:(g + 1) * N], ACT.Square,
                                   accum_out=hsq[:, t, g:g + 1]).then_inc(hsq_done, 1)
                act.wait_ge(hT_done, g + 1)
                for t in range(TT):
                    last = copy(hrT[:, 4 * g:4 * g + 4, t * P:(t + 1) * P], S[t].rearrange("p (k t) -> p k t", k=4))
                last.then_inc(hT_saved, 1)
                if g < 3:
                    save_half(4 + g)
            act.wait_ge(logit_saved, 1)
            act.activation(rt[:, 1], rt[:, 0], ACT.Sigmoid).then_inc(score_saved, 1)
            save_half(7)
            for i in range(4):
                act.wait_ge(bcast_done, 5 + i)
                copy(gate_b[:, i * N:(i + 1) * N], M).then_inc(bcast_saved, 1)
            act.wait_ge(table_ready, 1)
            jobs = act.value_load(n_i[0:1, 2 * JOBS:2 * JOBS + 1], min_val=1, max_val=JOBS - 1)

            def save_tokens(half):
                for k in range(8 * half, 8 * half + 8):
                    last = act.activation(xg[:, k, :], Xb[:, k // 4, (k % 4) * BLK:(k % 4 + 1) * BLK], ACT.Identity,
                                          bias=modcol[:, 3, k, 0:1], scale=scale_ffn[:, k:k + 1])
                return last

            def job_evac(j, wide):
                act.wait_ge(slot_free, j * JCH + used_job(7))
                for i in range(1 + wide):
                    last = act.activation(silu_g[i], Gb[i], ACT.Silu)
                last.then_inc(silu_saved, 1)
                act.wait_ge(ehT_done, j + 1)
                for i in range(1 + wide):
                    last = copy(hT[i], Gb[i])
                last.then_inc(ehT_saved, 1)
                act.wait_ge(gathered, j * 2 + 3)
                save_tokens(0)
                act.wait_ge(gathered, j * 2 + 4)
                save_tokens(1).then_inc(xg_ready, 1)
                act.wait_ge(slot_free, j * JCH + used_job(23))
                save_outputs(act, copy, 0, wide)

            act.wait_ge(gathered, 2)
            save_tokens(0)
            save_tokens(1).then_inc(xg_ready, 1)
            with act.Fori(0, jobs) as j:
                wide = act.value_load(n_i[0:1, bass.ds(j + JOBS, 1)], min_val=0, max_val=1)
                with act.If(wide):
                    job_evac(j, True)
                with act.Else():
                    job_evac(j, False)

        @block.vector
        def _(dve):
            tt, ts, stt = nc.vector.tensor_tensor, nc.vector.tensor_scalar, nc.vector.scalar_tensor_tensor

            def rsqrt(y, v, tmp):
                link(ts(y.bitcast(I32), v.bitcast(I32), 1, None, ALU.logical_shift_right))
                link(ts(y.bitcast(I32), y.bitcast(I32), -1.0, float(0x5F3759DF), ALU.mult, ALU.add))
                for _ in range(3):
                    link(tt(tmp, y, y, ALU.mult))
                    link(tt(tmp, tmp, v, ALU.mult))
                    link(ts(tmp, tmp, -0.5, 1.5, ALU.mult, ALU.add))
                    link(tt(y, y, tmp, ALU.mult))

            def save_tokT(t):
                for q in (0, 2):
                    dve.wait_ge(tokT_done, 4 * t + q + 1)
                    nc.vector.tensor_copy(nT[:, 4 * q:4 * q + 4, t * P:(t + 1) * P],
                                          Z[q].rearrange("p (k t) -> p k t", k=4)).then_inc(tokT_dve, 1)

            def save_modcol(b, p):
                at = slice(4 * b, 4 * b + 4)
                dve.wait_ge(ext_done, 2 * b + p + 1)
                tt(modcol[:, p, at], (T if p else M)[:, 0:8].rearrange("p (k r) -> p k r", r=2),
                   b_mix[:, p, at].unsqueeze(2).broadcast_to([P, 4, 2]), ALU.add).then_inc(modcol_saved, 1)

            half_count = [0]

            def sum_rows(n):
                for m in range(half_count[0], half_count[0] + n):
                    if m % KT == 0:
                        dve.wait_ge(bias_in, 16 * (m // KT + 1))
                    dve.wait_ge(half_in[m % HALF_SLOTS], 16 * (m // HALF_SLOTS + 1))
                    if m % KT:
                        dve.wait_ge(half_step, HALF_SLOTS + m)
                    total = halves[:, m // KT % 2, :]
                    stt(total, half_slots[:, m % HALF_SLOTS, :], silu_c[:, m % KT, 0:1], total, ALU.mult, ALU.add) \
                        .then_inc(half_step, 1)
                half_count[0] += n

            dve.wait_ge(silu_done, 1)
            nc.vector.tensor_copy(cols[:], S[0][:, 32:108]).then_inc(cols_saved, 1)
            dve.wait_ge(setupT_done, 1)
            nc.vector.tensor_copy(conv_cols[:], S[1][:, 0:P].rearrange("p (q n) -> p q n", q=4)) \
                .then_inc(convc_saved, 1)
            dve.wait_ge(misc_in, 16 * 4)
            link(ts(neg_sink[:], sink[:], -1.0, None, ALU.mult))
            for i in range(2):
                for t in range(TT):
                    g = qk_gain[:, i, :]
                    cs, sn = (k_(n)[:, t * HD:(t + 1) * HD] for n in ("cos", "sin"))
                    link(tt(rope[:, 2 * i, t, :], cs, g, ALU.mult))
                    for a, b in ((0, 64), (64, 0)):
                        link(tt(rope[:, 2 * i + 1, t, a:a + 64], sn[:, a:a + 64], g[:, b:b + 64], ALU.mult))
            for t in range(2 * TT):
                if t % TT == 0:
                    dve.wait_ge(sumsq_done, t + TT)
                    link(ts(stat[:, 0:2], ss[:, t:t + 2], 1.0 / D, EPS, ALU.mult, ALU.add))
                    rsqrt(rs_tok[:, t:t + 2], stat[:, 0:2], stat[:, 4:6])
                if t >= 2:
                    dve.wait_ge(tokT_done, 4 * (t - 1))
                ts(early[:, t % 2, :], tokens[:, t, :], rs_tok[:, t:t + 1], None, ALU.mult).then_inc(scaled, 1)
                if t:
                    save_tokT(t - 1)
                if t == 2:
                    save_modcol(0, 0)
            save_tokT(3)
            save_modcol(0, 1)
            for b in range(4):
                at = slice(4 * b, 4 * b + 4)
                dve.wait_ge(modcol_saved, 2 * b + 2)
                stt(scale_mix[:, at], modcol[:, 1, at], 1.0, mix_g[:, at].unsqueeze(2).broadcast_to([P, 4, 2]),
                    ALU.add, ALU.mult).then_inc(scale_done, 1)
                dve.wait_ge(scale_done, b + 1)
                if b == 0:
                    dve.wait_ge(tokT_act, 8)
                    dve.wait_ge(tokT_dve, 8)
                for k in range(4 * b, 4 * b + 4):
                    ts(nT[:, k, 0:SEQ], nT[:, k, 0:SEQ], scale_mix[:, k, 0:1], modcol[:, 0, k, 0:1],
                       ALU.mult, ALU.add).then_inc(nT_ready, 1)
                if b < 3:
                    save_modcol(b + 1, 0)
                    save_modcol(b + 1, 1)
            def head_norm(idx):
                dve.wait_ge(sq_saved, idx + 1)
                link(nc.vector.tensor_reduce(ss[:], work[:].rearrange("p (h d) -> p h d", h=8), AX.X, ALU.add))
                link(ts(ss[:], ss[:], 1.0 / HD, EPS, ALU.mult, ALU.add))
                rsqrt(stat[:], ss[:], small[:, 8:16])

            def rotate(z, at, n_heads, table, t):
                shape = [P, n_heads, 64]
                zh = z.rearrange("p (h d) -> p h d", d=HD)
                o = heads[:, at:at + n_heads * HD].rearrange("p (h d) -> p h d", d=HD)
                w = work[:, at:at + n_heads * HD].rearrange("p (h d) -> p h d", d=HD)
                last = tt(o, zh, rope[:, table, t:t + 1, :].broadcast_to([P, n_heads, HD]), ALU.mult)
                for a, b in ((0, 64), (64, 0)):
                    last = tt(w[:, :, a:a + 64], zh[:, :, b:b + 64],
                              rope[:, table + 1, t:t + 1, a:a + 64].broadcast_to(shape), ALU.mult)
                return last

            def finish_heads(n):
                link(tt(heads[:, 0:n], heads[:, 0:n], work[:, 0:n], ALU.add))
                tt(heads[:].rearrange("p (h d) -> p h d", d=HD), heads[:].rearrange("p (h d) -> p h d", d=HD),
                   stat[:].unsqueeze(2).broadcast_to([P, 8, HD]), ALU.mult).then_inc(rope_done, 1)

            def q_heads(idx, bank):
                head_norm(idx)
                if idx:
                    dve.wait_ge(headT_done, idx)
                for t in range(TT):
                    last = rotate(ps[:, bank + t, :], t * N, 4, 0, t)
                    if t == 0:
                        link(last)
                last.then_inc(qk_read, 1)
                dve.wait_ge(qk_read, idx + 1)
                finish_heads(1024)

            q_heads(0, 4)
            dve.wait_ge(g_saved, 1)
            dve.wait_ge(a_saved, 1)
            dve.wait_ge(zeroed, 2)
            link(tt(yT[:, :, PAD:PAD + SEQ], aT, acc, ALU.mult))
            for tap in range(CW):
                for q in range(4):
                    if tap:
                        dve.wait_ge(dve_step, dve_count[0] - 3)
                        ins = stt(acc[:, q, :], yT[:, q, tap:tap + SEQ], conv_cols[:, q, tap:tap + 1],
                                  acc[:, q, :], ALU.mult, ALU.add)
                    else:
                        ins = ts(acc[:, q, :], yT[:, q, 0:SEQ], conv_cols[:, q, 0:1],
                                 conv_cols[:, q, CW:CW + 1], ALU.mult, ALU.add)
                    ins.then_inc(dve_step, 1)
                    dve_count[0] += 1
            dve.wait_ge(dve_step, dve_count[0])
            ts(small[:, 32:33], small[:, 63:64], 1.0, None, ALU.mult).then_inc(conv_done, 1)
            dve.wait_ge(csum_done, 1)
            link(ts(bc[:, 0, :], T[:, 0:SEQ], 1.0 / N, None, ALU.mult))
            tt(acc, acc, bc[:, 0:1, :].broadcast_to([P, 4, SEQ]), ALU.subtract).then_inc(centred, 1)
            dve.wait_ge(centred, 1)

            head_norm(1)
            dve.wait_ge(headT_done, 1)
            dve.wait_ge(v_saved, 2)
            for t in range(TT):
                link(rotate(ps[:, t, 0:SEQ], t * SEQ, NKV, 2, t))
            for t in range(TT):
                last = tt(heads[:, N + t * SEQ:N + (t + 1) * SEQ].rearrange("p (h d) -> p h d", d=HD),
                          ps[:, 2 + t, 0:SEQ].rearrange("p (h d) -> p h d", d=HD),
                          qk_gain[:, 1:2, :].broadcast_to([P, NKV, HD]), ALU.mult)
            last.then_inc(qk_read, 1)
            dve.wait_ge(qk_read, 2)
            finish_heads(N)
            dve.wait_ge(csq_done, 1)
            link(ts(bc[:, 0, :], T[:, SEQ:N], 1.0 / N, EPS, ALU.mult, ALU.add))
            rsqrt(bc[:, 1, :], bc[:, 0, :], bc[:, 2, :])
            tt(acc, acc, bc[:, 1:2, :].broadcast_to([P, 4, SEQ]), ALU.mult).then_inc(cnorm, 1)

            for h in range(NH):
                if h == 3:
                    q_heads(2, 0)
                dve.wait_ge(score_done, h + 1)
                link(nc.vector.tensor_reduce(small[:, 0:2], ps[:, 4:6, :], AX.X, ALU.max))
                ts(small[:, 2:4], small[:, 0:2], -(HD ** -0.5), neg_sink[:, h:h + 1], ALU.mult, ALU.min) \
                    .then_inc(neg_max, 1)
                sum_rows(2)
                dve.wait_ge(exp_done, 4 * h + 4)
                link(tt(small[:, 4:6], small[:, 4:6], small[:, 6:8], ALU.add))
                link(nc.vector.reciprocal(small[:, 4:6], small[:, 4:6]))
                for t in range(TT):
                    last = ts(probs[:, t, :], probs[:, t, :], small[:, 4 + t:5 + t], None, ALU.mult)
                last.then_inc(probs_done, 1)
                sum_rows(6)
                dve.wait_ge(probs_done, h + 1)
            dve.wait_ge(wr_in, 16 * 4)
            dve.wait_ge(gelu_v, 1)
            for t in range(TT):
                link(nc.vector.bn_stats(small[:, 16 + 6 * t:22 + 6 * t], vbuf[:, t, :]))
                link(nc.vector.bn_aggr(small[:, 28 + 2 * t:30 + 2 * t], small[:, 16 + 6 * t:22 + 6 * t]))
                link(ts(stat[:, t:t + 1], small[:, 29 + 2 * t:30 + 2 * t], EPS, None, ALU.add))
            rsqrt(stat[:, 2:4], stat[:, 0:2], stat[:, 4:6])
            for t in range(TT):
                link(ts(vbuf[:, t, :], vbuf[:, t, :], small[:, 28 + 2 * t:29 + 2 * t], stat[:, 2 + t:3 + t],
                        ALU.subtract, ALU.mult))
            link(tt(vbuf, vbuf, gm_gb[:, 0:1, :].broadcast_to([P, TT, N]), ALU.mult))
            tt(vbuf, vbuf, gm_gb[:, 1:2, :].broadcast_to([P, TT, N]), ALU.add).then_inc(v_ready, 1)
            dve.wait_ge(spatial_done, 1)
            for t in range(TT):
                last = tt(vbuf[:, t, :].rearrange("p (h d) -> p h d", h=4),
                          (S[0] if t else T).rearrange("p (h d) -> p h d", h=4),
                          b_s.unsqueeze(2).broadcast_to([P, 4, HD]), ALU.add)
            last.then_inc(mixed_saved, 1)
            dve.wait_ge(mixed_saved, 1)
            dve.wait_ge(gelu_u, 1)
            tt(bufB[:], bufB[:], bufA[:], ALU.mult).then_inc(gated, 1)
            for g in range(4):
                sum_rows(16)
                if g == 0:
                    dve.wait_ge(bcast_saved, 4)
                dve.wait_ge(slot_free, used_out(g))
                b = 2 if g % 2 == 0 else 0
                for t in range(TT):
                    last = tt(work[:, t * N:(t + 1) * N], Z[b + t], gate_b[:, g * N:(g + 1) * N], ALU.mult)
                link(last)
                h_g = tokens[:, 0:TT, g * N:(g + 1) * N]
                tt(h_g, h_g, work[:].rearrange("p (t n) -> p t n", t=TT), ALU.add).then_inc(h_ready, 1)
                if g == 2:
                    dve.wait_ge(half_saved, 6)
                    link(stt(scale_ffn[:], modcol[:, 4, :, 0], 1.0, ffn_g, ALU.add, ALU.mult))
                    tt(wr_scaled[:], wr[:], scale_ffn[:].unsqueeze(2).broadcast_to([P, KT, NE]), ALU.mult) \
                        .then_inc(wr_ready, 1)
            dve.wait_ge(hsq_done, 8)
            link(nc.vector.tensor_reduce(stat[:, 0:2], hsq[:], AX.X, ALU.add))
            link(ts(stat[:, 0:2], stat[:, 0:2], 1.0 / D, EPS, ALU.mult, ALU.add))
            rsqrt(rs_tok[:, 0:2], stat[:, 0:2], stat[:, 2:4])
            rs2 = rs_tok[:, 0:2].unsqueeze(2).broadcast_to([P, TT, NE])
            dve.wait_ge(logit_done, 1)
            nc.vector.tensor_copy(rrow[:], T[0:1, 64:64 + NE]).then_inc(rbias_row, 1)
            link(tt(rt[:, 0], T[:, 0:2 * NE].rearrange("p (t e) -> p t e", t=TT), rs2, ALU.mult))
            dve.wait_ge(logit_done, 2)
            rb = rt[:, 2, 0:1, :]
            link(nc.vector.tensor_copy(rt[:, 2, 0, :], S[0][:, 0:NE]))
            tt(rt[:, 0], rt[:, 0], rb.broadcast_to([P, TT, NE]), ALU.add).then_inc(logit_saved, 1)
            dve.wait_ge(score_saved, 1)
            scores, sel = rt[:, 1], rt[:, 3]
            link(tt(sel, scores, rbias[:].unsqueeze(1).broadcast_to([P, TT, NE]), ALU.add))
            v = sel.rearrange("p t (g a b) -> p (t g) a b", g=NG, a=2)

            def g8(i):
                return rt[:, i].rearrange("p t e -> p (t e)")[:, 0:16].rearrange("p (g a) -> p g a", a=2)

            def g1(i):
                return rt[:, i].rearrange("p t e -> p (t e)")[:, 0:8]

            hi, lo = g8(4), g8(5)
            link(tt(hi, v[:, :, :, 0], v[:, :, :, 1], ALU.max))
            link(tt(lo, v[:, :, :, 0], v[:, :, :, 1], ALU.min))
            link(tt(g1(6), hi[:, :, 0], hi[:, :, 1], ALU.max))
            link(tt(g1(7), hi[:, :, 0], hi[:, :, 1], ALU.min))
            link(tt(g1(8), lo[:, :, 0], lo[:, :, 1], ALU.max))
            link(tt(g1(7), g1(7), g1(8), ALU.max))
            link(tt(g1(6), g1(6), g1(7), ALU.add))

            def first_max(values, numbers, n, mx, eq, low, hot):
                shape = [P, TT, n]
                link(nc.vector.tensor_reduce(mx, values, AX.X, ALU.max))
                link(tt(eq, values, mx.unsqueeze(2).broadcast_to(shape), ALU.is_equal))
                link(tt(eq, eq, numbers.unsqueeze(1).broadcast_to(shape), ALU.mult))
                link(nc.vector.tensor_reduce(low, eq, AX.X, ALU.min))
                link(tt(hot, numbers.unsqueeze(1).broadcast_to(shape), low.unsqueeze(2).broadcast_to(shape),
                        ALU.is_equal))

            gsc = g1(6).rearrange("p (t g) -> p t g", t=TT)
            geq = g1(8).rearrange("p (t g) -> p t g", t=TT)
            ghot = g1(9).rearrange("p (t g) -> p t g", t=TT)
            first_max(gsc, k_("g4"), NG, small[:, 0:2], geq, small[:, 2:4], ghot)
            masked = rt[:, 10]
            link(ts(geq, ghot, BIG, -BIG, ALU.mult, ALU.add))
            m4 = masked.rearrange("p t (g e) -> p (t g) e", e=EPG)
            link(tt(m4, sel.rearrange("p t (g e) -> p (t g) e", e=EPG),
                    g1(9).unsqueeze(2).broadcast_to([P, 2 * NG, EPG]), ALU.mult))
            link(tt(m4, m4, g1(8).unsqueeze(2).broadcast_to([P, 2 * NG, EPG]), ALU.add))
            first_max(masked, k_("e16"), NE, small[:, 0:2], rt[:, 11], small[:, 2:4], rt[:, 12])
            link(ts(rt[:, 11], rt[:, 12], -3 * BIG, None, ALU.mult))
            link(tt(masked, masked, rt[:, 11], ALU.add))
            first_max(masked, k_("e16"), NE, small[:, 0:2], rt[:, 11], small[:, 2:4], rt[:, 13])
            mask, gates = rt[:, 15], rt[:, 14]
            link(tt(mask, rt[:, 12], rt[:, 13], ALU.add))
            for t in range(TT):
                last = nc.vector.tensor_copy(cand[:, t, 0, :].rearrange("p (b e) -> p b e", b=NBLK),
                                             rt[:, 15, t:t + 1, :].broadcast_to([P, NBLK, NE]))
            last.then_inc(mask_ready, 1)
            link(tt(gates, scores, mask, ALU.mult))
            link(nc.vector.tensor_reduce(small[:, 0:2], gates, AX.X, ALU.add))
            link(nc.vector.reciprocal(small[:, 2:4], small[:, 0:2]))
            link(tt(gates, gates, small[:, 2:4].unsqueeze(2).broadcast_to([P, TT, NE]), ALU.mult))
            dve.wait_ge(pos_done, 1)
            pos = rt[:, 16]
            link(ts(pos, T[:, 0:2 * NE].rearrange("p (t e) -> p t e", t=TT), 1.0, None, ALU.add))
            link(ts(vcol[:, 2:3], T[0:CAND, 128:129], k_("blk_lo")[0:CAND, :], float(BASE),
                    ALU.subtract, ALU.is_gt))
            ts(vcol[:, 0:1], T[0:CAND, 128:129], k_("blk_lo")[0:CAND, :], None, ALU.is_gt).then_inc(count_saved, 1)
            link(tt(pos, pos, mask, ALU.mult))
            link(ts(pos, pos, -1.0, None, ALU.add))
            lows = k_("cand_lo").rearrange("p (b e) -> p b e", b=NBLK)
            for t in range(TT):
                tt(cand[:, t, 0, :].rearrange("p (b e) -> p b e", b=NBLK),
                   rt[:, 16, t:t + 1, :].broadcast_to([P, NBLK, NE]), lows, ALU.subtract)
                last = nc.vector.tensor_copy(cand[:, t, 1, :].rearrange("p (b e) -> p b e", b=NBLK),
                                             rt[:, 14, t:t + 1, :].broadcast_to([P, NBLK, NE]))
            last.then_inc(cand_ready, 1)
            dve.wait_ge(order_done, 1)
            link(nc.vector.tensor_copy(vcol[:, 1:2], T[0:CAND, 0:1]))
            link(nc.vector.tensor_copy(n_i[:, 2 * JOBS:2 * JOBS + 1], T[0:1, 2:3]))
            dve.wait_ge(count_saved, 1)
            ts(onehot_j[:], k_("jobno")[0:CAND, :], vcol[:, 1:2], vcol[:, 0:1], ALU.is_equal, ALU.mult) \
                .then_inc(table_oh, 1)
            dve.wait_ge(candT_done, 1)
            nc.vector.tensor_copy(candT.rearrange("c t i p -> c (t i p)"), S[0][0:CAND, :]).then_inc(table_oh, 1)
            dve.wait_ge(table_done, 1)
            link(nc.vector.tensor_copy(job.rearrange("p i t j -> p (i t j)"), S[1][:, 0:4 * JOBS]))
            nc.vector.tensor_copy(n_i[:, 0:2 * JOBS], S[1][0:1, 256:256 + 2 * JOBS]).then_inc(table_ready, 1)
            dve.wait_ge(table_ready, 1)

            def gather_matrix(j):
                for t in range(TT):
                    last = ts(oh_in[:, t, :], k_("slots"), job[:, 0, t, bass.ds(j, 1)], rs_tok[:, t:t + 1],
                              ALU.is_equal, ALU.mult)
                last.then_inc(oh_ready, 1)

            def spread_matrix(j):
                for t in range(TT):
                    last = ts(oh_out[:, t, :], k_("slots"), job[:, 0, t, bass.ds(j, 1)],
                              job[:, 1, t, bass.ds(j, 1)], ALU.is_equal, ALU.mult)
                return last

            def hidden_product(j, wide):
                dve.wait_ge(silu_saved, j + 1)
                dve.wait_ge(slot_free, j * JCH + used_job(15))
                for i in range(1 + wide):
                    last = tt(hidden[i], silu_g[i], Ub[i], ALU.mult)
                last.then_inc(hidden_ready, 1)
                dve.wait_ge(ehT_done, j + 1)
                nc.vector.tensor_copy(spread_T[0:BLK].rearrange("p t n -> p (t n)"), Ub[0][0:BLK, 0:SEQ]) \
                    .then_inc(spread_saved, 1)
                dve.wait_ge(slot_free, j * JCH + used_job(23))
                save_outputs(dve, nc.vector.tensor_copy, 1, wide)

            jobs = dve.value_load(n_i[0:1, 2 * JOBS:2 * JOBS + 1], min_val=1, max_val=JOBS - 1)
            gather_matrix(0)
            dve.wait_ge(y_zeroed, 1)
            with dve.Fori(0, jobs) as j:
                wide = dve.value_load(n_i[0:1, bass.ds(j + JOBS, 1)], min_val=0, max_val=1)
                dve.wait_ge(gathered, j * 2 + 2)
                gather_matrix(j + 1)
                spread_matrix(j)
                with dve.If(wide):
                    hidden_product(j, True)
                with dve.Else():
                    hidden_product(j, False)
                for t in range(TT):
                    for h in range(2):
                        dve.wait_ge(scattered, j * 4 + (2 * t + h + 1))
                        y = yacc[:, t, h, :]
                        tt(y, Yb[:, 2 * h:2 * h + 2, :].rearrange("p a n -> p (a n)"), y, ALU.add) \
                            .then_inc(summed, 1)
            dve.wait_ge(summed, jobs * 4 + 4)
            dve.wait_ge(bcast_saved, 8)
            for q in range(4):
                t, h = q // 2, q % 2
                y = yacc[:, t, h, :]
                link(tt(y, y, gate_b[:, h * 1024:(h + 1) * 1024], ALU.mult))
                o = tokens[:, t, h * 1024:(h + 1) * 1024]
                tt(o, o, y, ALU.add).then_inc(out_ready, 1)


INPUTS = ["x", "c", "ctx", "c_ctx", "w_mod", "b_mod", "norm_mix_g", "norm_ffn_g", "w_in", "w_out",
          "q_norm_g", "k_norm_g", "attn_sink", "gmlp_ln_g", "gmlp_ln_b", "gmlp_w_s", "gmlp_b_s", "conv_w",
          "conv_b", "conv_ln_g", "conv_ln_b", "w_router", "router_bias", "w_gate", "w_up", "w_down"]
SHAPES = {"x": (SEQ, D), "ctx": (SEQ, D), "c": (16, P), "c_ctx": (16, P), "norm_mix_g": (16, P),
          "norm_ffn_g": (16, P), "gmlp_b_s": (4, P), "conv_ln_g": (4, P), "conv_ln_b": (4, P),
          "w_mod": (D, 6 * D), "b_mod": (1, 6 * D), "w_in": (D, 3584), "w_out": (D, D),
          "q_norm_g": (1, HD), "k_norm_g": (1, HD), "attn_sink": (1, NH), "gmlp_ln_g": (1, N),
          "gmlp_ln_b": (1, N), "gmlp_w_s": (4, P, P), "conv_w": (CW, N), "conv_b": (1, N),
          "w_router": (D, NE), "router_bias": (1, NE), "w_gate": (NE, D, FE), "w_up": (NE, D, FE),
          "w_down": (NE, FE, D)}


def kernel(**inputs):
    import concourse.bacc as bacc
    from concourse.bass_utils import run_bass_kernel_spmd

    nc = bacc.Bacc("TRN2", target_bir_lowering=False, num_devices=1)
    arrays, args = {}, []
    for name in INPUTS:
        a = np.ascontiguousarray(inputs[name]).reshape(SHAPES[name])
        arrays[name + "_dram"] = a
        args.append(nc.dram_tensor(name + "_dram", a.shape, F32, kind="ExternalInput").ap())
    _, _, tables = constants()
    table = np.concatenate([np.broadcast_to(v, (P, v.shape[1])) for v in tables.values()], 1).astype(np.float32)
    arrays["tables_dram"] = np.ascontiguousarray(table)
    args.append(nc.dram_tensor("tables_dram", table.shape, F32, kind="ExternalInput").ap())
    out = nc.dram_tensor("out_dram", (SEQ, D), F32, kind="ExternalOutput").ap()
    build(nc, *args, out)
    r = run_bass_kernel_spmd(nc, [arrays], core_ids=[0])
    return r.results[0]["out_dram"].reshape(1, SEQ, D)
```

```python
from contextlib import ExitStack

import numpy as np

import concourse.bass as bass
from concourse import mybir

F32 = mybir.dt.float32
I32 = mybir.dt.int32
ALU = mybir.AluOpType
ACT = mybir.ActivationFunctionType
AX = mybir.AxisListType

P = 128
D = 2048
KT = D // P
SEQ = 256
TT = SEQ // P
HD = 128
NH, NKV = 8, 2
GRID_W = 64
CW = 31
PAD = CW // 2
NE, NG, EPG = 16, 4, 4
FE = 1024
EPS = 1e-6
BIG = 1e30
N = 512

SLOTS = 8
PRE_SLOTS = 6
HALF = D // 2
HALF_SLOTS = 4
FIRST = 14
CH = 2048
BASE, REST = 64, 32
BLK = BASE + REST
NBLK = -(-SEQ // BLK)
CAND = NBLK * NE
JOBS = NE + (2 * SEQ - NE) // BLK + 1
EARLY = 2
JCH = 24

GROUPS = [("a", 2560), ("g", 3072), ("q0", 0), ("kv", 1024), ("q1", 512), ("v", 2048), ("u", 1536)]
A_, G_, Q0_, KV_, Q1_, V_, U_ = range(7)


def make_schedule():
    seq = [("setup",), ("tok", 0), ("tok", 1)] + [("mod", 0, 0, c) for c in range(4)]
    seq += [("tok", 2), ("tok", 3), ("ext", 0, 0)] + [("mod", 0, 1, c) for c in range(4)] + [("ext", 0, 1)]
    for b in range(4):
        mods = [("mod", b + 1, p, c) for p in range(2) for c in range(4)] if b < 3 else []
        win = [[("win", g, 4 * b + i) for i in range(4)] for g in (A_, G_, Q0_)]
        seq += mods[0:3] + win[0]
        seq += mods[3:6] + win[1][0:2] + [("ext", b + 1, 0)] * (b < 3) + win[1][2:4]
        seq += mods[6:8] + win[2][0:2] + [("ext", b + 1, 1)] * (b < 3) + win[2][2:4]

    after = {
        (KV_, 3): [("convsum",), ("qT", 0)], (Q1_, 0): [("convsq",), ("half", 0)],
        (Q1_, 1): [("kT",)], (V_, 2): [("qT", 1)],
    }
    halves = {2: 1, 5: 2}
    hpos = 0
    for g in range(KV_, 7):
        for c in range(4):
            busy = (g, c) >= (Q1_, 3) and hpos < NH
            seq += [("win", g, 4 * c + i) for i in range(3)]
            if busy:
                seq.append(("head", hpos, 1))
            seq.append(("win", g, 4 * c + 3))
            seq += after.get((g, c), [])
            if busy:
                seq.append(("head", hpos, 2))
                hpos += 1
            if (g, c) >= (Q1_, 2) and hpos < NH:
                seq.append(("head", hpos, 0))
                if hpos in halves:
                    seq.append(("half", halves[hpos]))
    seq += [("spatial",), ("bcast", 0), ("bcast", 1)]
    gate = [("gate", k) for k in range(KT)]
    after = {(0, 0): [("bcast", 2), ("bcast", 3)], (0, 1): [("gated",), ("half", 3)], (1, 3): [("half", 4)],
             (3, 0): [("half", 5)] + gate[0:2], (3, 1): [("shift",), ("logits", 0)] + gate[2:4],
             (3, 2): [("logits", 1)] + gate[4:6], (3, 3): [("shift_rows",), ("logits", 2)] + gate[6:8]}
    for g in range(4):
        for c in range(4):
            seq.append(("wout", g, c))
            if g and c == 0:
                seq.append(("hT", g - 1))
            seq += after.get((g, c), [])
    seq += [("hT", 3)] + gate[8:9] + [("logits", 3)] + gate[9:13] + [("route", 1)] + gate[13:14]
    return seq + [("route", 2)] + gate[14:15] + [("route", 3)] + gate[15:16]


SCHEDULE = make_schedule()
CHUNK_STEPS = [s for s in SCHEDULE if s[0] in ("mod", "wout", "gate") or (s[0] == "win" and s[2] % 4 == 0)]
NPRE = len(CHUNK_STEPS)
NUMBER = {s: n for n, s in enumerate(CHUNK_STEPS)}


def constants():
    p = np.arange(P)[:, None]
    c = np.arange(P)[None, :]
    f = np.float32
    rows = SEQ // GRID_W
    row = np.repeat(np.arange(rows, dtype=f), GRID_W)
    col = np.tile(np.arange(GRID_W, dtype=f), rows)
    nf = HD // 4
    inv = (f(10000.0) ** (-np.arange(nf, dtype=f) / f(nf))).astype(f)
    ang = np.concatenate([row[:, None] * inv, col[:, None] * inv], axis=-1)
    cos, sin = np.cos(ang), np.sin(ang)
    cosd = np.concatenate([cos, cos], 1).reshape(TT, P, HD).transpose(1, 0, 2).reshape(P, -1)
    sind = np.concatenate([-sin, sin], 1).reshape(TT, P, HD).transpose(1, 0, 2).reshape(P, -1)
    cand = np.arange(CAND)
    one = np.ones((P, 1))
    t = {
        "ident": p == c,
        "before": p < c,
        "mask0": np.where(c <= p, 0, -BIG),
        "mask1": np.where(c >= p, 0, -BIG),
        "slots": one * np.arange(BLK)[None],
        "jobno": one * np.arange(JOBS)[None],
        "sel": (p % 32 == np.arange(2)[None]),
        "spread": (p == 32 * (np.arange(N) // P)[None]),
        "blk_lo": (np.arange(P)[:, None] // NE) * BLK,
        "expert": np.arange(P)[:, None] % NE,
        "cand_lo": one * ((cand // NE) * BLK)[None],
        "g4": one * (np.arange(NG) - 2 * NG)[None],
        "e16": one * (np.arange(NE) - 2 * NE)[None],
        "ones": one * np.ones((1, P)),
        "cos": cosd, "sin": sind,
    }
    at, cols = {}, 0
    for k, v in t.items():
        at[k] = (cols, v.shape[1])
        cols += v.shape[1]
    return at, cols, t


CONST_AT, ALL_COLS, _ = constants()
CONST_COLS = CONST_AT["cos"][0]


def build(nc, x, c, ctx, c_ctx, w_mod, b_mod, norm_mix_g, norm_ffn_g, w_in, w_out, q_norm_g, k_norm_g,
          attn_sink, gmlp_ln_g, gmlp_ln_b, gmlp_w_s, gmlp_b_s, conv_w, conv_b, conv_ln_g, conv_ln_b,
          w_router, router_bias, w_gate, w_up, w_down, consts, out):
    with ExitStack() as stack:
        def sb(name, shape, dt=F32):
            return stack.enter_context(nc.sbuf_tensor(name, shape, dt))

        def sem(name):
            return stack.enter_context(nc.semaphore(name))

        ring = sb("ring", [P, SLOTS, CH])
        const = sb("const", [P, CONST_COLS])
        tokens = sb("tokens", [P, 2 * TT, D])
        nT_all = sb("nT_all", [P, KT * 2 * SEQ])
        early = sb("early", [P, 2, D])
        halves = sb("halves", [P, 2, HALF])
        modrow = sb("modrow", [P, 2, N])
        silu_c = sb("silu_c", [P, KT, 32])
        rows = sb("rows", [108, P])
        cols = sb("cols", [P, 76])
        modcol = sb("modcol", [P, 5, KT, 2])
        scale_mix = sb("scale_mix", [P, KT, 2])
        scale_ffn = sb("scale_ffn", [P, KT])
        qk_gain = sb("qk_gain", [P, 2, HD])
        sink = sb("sink", [P, NH])
        neg_sink = sb("neg_sink", [P, NH])
        rbias = sb("rbias", [P, NE])
        gm_gb = sb("gm_gb", [P, 2, N])
        w_sT = sb("w_sT", [P, 4, P])
        conv_cols = sb("conv_cols", [P, 4, CW + 1])
        wr = sb("wr", [P, KT, NE])
        wr_scaled = sb("wr_scaled", [P, KT, NE])
        stat = sb("stat", [P, 8])
        ss = sb("ss", [P, 8])
        rs_tok = sb("rs_tok", [P, 2 * TT])
        rope = sb("rope", [P, 4, TT, HD])
        work = sb("work", [P, 1024])
        heads = sb("heads", [P, 1024])
        yT = sb("yT", [P, 4, SEQ + 2 * PAD])
        bufA = sb("bufA", [P, 1024])
        bufB = sb("bufB", [P, 1024])
        probs = sb("probs", [P, 2, N])
        small = sb("small", [P, 64])
        n_i = sb("n_i", [1, 2 * JOBS + 1], I32)
        hsq = sb("hsq", [P, TT, 4])
        onehot_j = sb("onehot_j", [CAND, JOBS])
        vcol = sb("vcol", [CAND, 8])
        rrow = sb("rrow", [1, NE])

        def k_(name):
            at, n = CONST_AT[name]
            if at >= CONST_COLS:
                return heads[:, at - CONST_COLS:at - CONST_COLS + n]
            return const[:, at:at + n]

        ident, ones = k_("ident"), k_("ones")
        mixT = tokens[:, TT:2 * TT, :].rearrange("p a d -> p (a d)").rearrange("p (k t) -> p k t", k=KT)
        nT = nT_all[:].rearrange("p (k t) -> p k t", k=KT)
        yacc = nT_all[:, 0:TT * D].rearrange("p (t h n) -> p t h n", t=TT, h=2)
        hrT = nT_all[:, TT * D:].rearrange("p (k t) -> p k t", k=KT)
        tail = TT * D
        def part(buf, at, n):
            return buf[:, at:at + n]

        xg = part(nT_all, tail, KT * BLK).rearrange("p (k s) -> p k s", k=KT)
        outs = part(nT_all, tail + 1536, D)
        spread_T = part(nT_all, tail + 3584, 256).rearrange("p (t n) -> p t n", t=TT)
        hT = [part(bufA, 0, 512), part(nT_all, tail + 3840, 256)]
        silu_g = [part(work, 0, 512), part(bufA, 512, 256)]
        hidden = [part(work, 512, 512), part(bufA, 768, 256)]
        oh_in = part(bufB, 0, TT * BLK).rearrange("p (t s) -> p t s", t=TT)
        oh_out = part(bufB, 256, TT * BLK).rearrange("p (t s) -> p t s", t=TT)
        w_s = work[:, 0:N].rearrange("p (h q) -> p h q", h=4)
        conv_rows = work[0:CW + 1, N:2 * N]
        bc = probs[:].rearrange("p t n -> p (t n)")[:, 0:3 * SEQ].rearrange("p (i t) -> p i t", i=3)
        rt = heads[:, 0:24 * TT * NE].rearrange("p (i t e) -> p i t e", i=24, t=TT)
        yT_flat = yT[:].rearrange("p c t -> p (c t)")
        probsT = yT_flat[:, 0:4 * SEQ].rearrange("p (k t) -> p k t", k=4)
        cand = yT_flat[:, 0:4 * CAND].rearrange("p (t i c) -> p t i c", t=TT, i=2)
        candT = yT_flat[0:CAND, 256:768].rearrange("c (t i p) -> c t i p", t=TT, i=2)
        job = yT_flat[:, 768:768 + 4 * JOBS].rearrange("p (i t j) -> p i t j", i=2, t=TT)
        qT = early[:, 0, :].rearrange("p (h t) -> p h t", h=NH)
        kT = early[:, 1, 0:1024].rearrange("p (h t) -> p h t", h=NKV)
        vtok = early[:, 1, 1024:2048].rearrange("p (t n) -> p t n", t=2 * TT)
        gate_b = early[:, 0, :]
        acc = bufB[:].rearrange("p (c t) -> p c t", c=4)
        aT = bufA[:].rearrange("p (c t) -> p c t", c=4)
        vbuf = bufA[:].rearrange("p (t n) -> p t n", t=TT)
        ubuf = bufB[:].rearrange("p (t n) -> p t n", t=TT)
        mix_g, ffn_g = cols[:, 0:16], cols[:, 16:32]
        b_s, cv_g, cv_b = cols[:, 32:36], cols[:, 36:40], cols[:, 40:44]
        b_mix = cols[:, 44:76].rearrange("p (s k) -> p s k", s=2)
        half_slots = ring[:, PRE_SLOTS:SLOTS, :].rearrange("p s (h n) -> p (s h) n", h=2)

        ps = stack.enter_context(nc.psum_tensor("ps", [P, 8, N], F32))
        Z = [ps[:, i, :] for i in range(4)]
        S = [ps[:, 4, :], ps[:, 5, :]]
        C = [ps[:, 2, :], ps[:, 3, :]]
        T, M = ps[:, 6, :], ps[:, 7, :]
        Gb, Ub, Db = [ps[:, 0, :], ps[:, 1, 0:256]], [ps[:, 2, :], ps[:, 3, 0:256]], [ps[:, 0:2, :], ps[:, 2, :]]
        Xb = Yb = ps[:, 4:8, :]
        pair = {A_: 0, G_: 2, Q0_: 4, KV_: 0, Q1_: 4, V_: 0, U_: 4}

        rows_in, const_in, tok_in, ctx_in, setup_in, misc_in, wr_in = (sem(s) for s in (
            "rows_in", "const_in", "tok_in", "ctx_in", "setup_in", "misc_in", "wr_in"))
        half_in = [sem(f"half_in{i}") for i in range(HALF_SLOTS)]
        bias_in, half_zero = sem("bias_in"), sem("half_zero")
        half_step, half_saved = sem("half_step"), sem("half_saved")
        shift_done = sem("shift_done")
        gate_done, gate_saved = sem("gate_done"), sem("gate_saved")
        half_scaled = sem("half_scaled")
        half_free = sem("half_free")
        landed = [sem(f"landed{i}") for i in range(SLOTS)]
        slot_free = sem("slot_free")
        zeroed = sem("zeroed")
        rowsT_done, cols_saved, silu_done = sem("rowsT_done"), sem("cols_saved"), sem("silu_done")
        setupT_done, wsT_saved, convc_saved = sem("setupT_done"), sem("wsT_saved"), sem("convc_saved")
        sumsq_done, scaled, tokT_done = sem("sumsq_done"), sem("scaled"), sem("tokT_done")
        tokT_act, tokT_dve = sem("tokT_act"), sem("tokT_dve")
        row_saved, ext_done, modcol_saved = sem("row_saved"), sem("ext_done"), sem("modcol_saved")
        scale_done, nT_ready, nC_ready = sem("scale_done"), sem("nT_ready"), sem("nC_ready")
        a_saved, g_saved, conv_done = (sem(s) for s in ("a_saved", "g_saved", "conv_done"))
        csum_done, centred, csq_saved, csq_done, cnorm = (sem(s) for s in (
            "csum_done", "centred", "csq_saved", "csq_done", "cnorm"))
        conv_saved = sem("conv_saved")
        sq_saved, qk_read, v_saved, rope_done, headT_done, headT_saved = (sem(s) for s in (
            "sq_saved", "qk_read", "v_saved", "rope_done", "headT_done", "headT_saved"))
        score_done, neg_max, exp_done, probs_done, pT_done, pT0_saved, pT1_saved, pv_done, pv_saved = (
            sem(s) for s in ("score_done", "neg_max", "exp_done", "probs_done", "pT_done",
                             "pT0_saved", "pT1_saved", "pv_done", "pv_saved"))
        gelu_v, v_ready, spatial_done, mixed_saved, gelu_u, gated, gatedT_done, gatedT_saved = (
            sem(s) for s in ("gelu_v", "v_ready", "spatial_done", "mixed_saved", "gelu_u", "gated",
                             "gatedT_done", "gatedT_saved"))
        bcast_done, bcast_saved = sem("bcast_done"), sem("bcast_saved")
        h_ready, hT_done, hT_saved, hsq_done, wr_ready = (sem(s) for s in (
            "h_ready", "hT_done", "hT_saved", "hsq_done", "wr_ready"))
        logit_done, logit_saved, score_saved, rbias_row, mask_ready, pos_done, cand_ready, candT_done = (
            sem(s) for s in ("logit_done", "logit_saved", "score_saved", "rbias_row", "mask_ready",
                             "pos_done", "cand_ready", "candT_done"))
        count_saved, order_done, table_oh, table_done, table_ready, y_zeroed = (sem(s) for s in (
            "count_saved", "order_done", "table_oh", "table_done", "table_ready", "y_zeroed"))
        oh_ready, gathered, xg_ready, silu_saved, hidden_ready = (sem(s) for s in (
            "oh_ready", "gathered", "xg_ready", "silu_saved", "hidden_ready"))
        ehT_done, ehT_saved, o_act, o_dve, scattered, summed = (sem(s) for s in (
            "ehT_done", "ehT_saved", "o_act", "o_dve", "scattered", "summed"))
        y_done, last_part, out_ready, out_sent = (sem(s) for s in ("y_done", "last_part", "out_ready", "out_sent"))
        dve_step, spread_saved = sem("dve_step"), sem("spread_saved")

        def save_outputs(eng, copy, odd, wide):
            for q in (odd, 2 + odd):
                if wide:
                    copy(outs[BASE:BLK, q * N:(q + 1) * N], Db[1][REST * q:REST * (q + 1), :])
                copy(outs[0:BASE, q * N:(q + 1) * N], Db[0][BASE * (q // 2):BASE * (q // 2 + 1), odd, :]) \
                    .then_inc(o_dve if odd else o_act, 1)

        block = stack.enter_context(nc.Block())

        def place(n):
            return (n - NPRE) % PRE_SLOTS

        def job_place(i):
            return (i + PRE_SLOTS) % SLOTS

        def slot(n):
            return ring[:, place(n), :]

        def used_chunk(n):
            return PRE_SLOTS + n + 1

        def used(g):
            return used_chunk(NUMBER["win", g, 12])

        def used_out(g):
            return used_chunk(NUMBER["wout", g, 3])

        def used_job(i):
            return used_chunk(NPRE + i)

        dve_count = [0]

        def link(ins):
            dve_count[0] += 1
            ins.then_inc(dve_step, 1)
            nc.vector.wait_ge(dve_step, dve_count[0])

        @block.sync
        def _(sp):
            sp.dma_start(const[:], consts[:, 0:CONST_COLS]).then_inc(const_in, 16)
            for at, v in ((64, gmlp_b_s), (68, conv_ln_g), (72, conv_ln_b)):
                sp.dma_start(rows[at:at + 4, :], v).then_inc(rows_in, 16)
            sp.dma_start(rows[76:108, :], b_mod[:, 0:2 * D].rearrange("o (k p) -> (o k) p", p=P)) \
                .then_inc(rows_in, 16)
            sp.dma_start(conv_rows[0:CW, :], conv_w).then_inc(setup_in, 16)
            sp.dma_start(conv_rows[CW:CW + 1, :], conv_b).then_inc(setup_in, 16)
            sp.dma_start(w_s, gmlp_w_s.rearrange("h p q -> p h q")).then_inc(setup_in, 16)
            for n, (kind, *at) in enumerate(CHUNK_STEPS):
                sp.wait_ge(slot_free, n + 1)
                if kind == "mod":
                    b, p, q = at
                    w, col = w_mod, p * D + b * N
                elif kind == "win":
                    w, col, q = w_in, GROUPS[at[0]][1], at[1] // 4
                elif kind == "wout":
                    w, col, q = w_out, at[0] * N, at[1]
                else:
                    sp.dma_start(slot(n), w_mod[at[0] * P:(at[0] + 1) * P, 5 * D:6 * D]) \
                        .then_inc(landed[place(n)], 16)
                    continue
                sp.dma_start(slot(n).rearrange("p (k n) -> p k n", k=4),
                             w[q * 4 * P:(q + 1) * 4 * P, col:col + N].rearrange("(k p) n -> p k n", p=P)) \
                    .then_inc(landed[place(n)], 16)
            sp.wait_ge(table_ready, 1)
            jobs = sp.value_load(n_i[0:1, 2 * JOBS:2 * JOBS + 1], min_val=1, max_val=JOBS - 1)
            with sp.Fori(0, jobs) as j:
                e = sp.value_load(n_i[0:1, bass.ds(j, 1)], min_val=0, max_val=NE - 1)
                for i in range(JCH):
                    if i == 0:
                        sp.wait_ge(half_step, HALF_SLOTS + 6 * KT)
                    sp.wait_ge(slot_free, j * JCH + used_job(i - SLOTS))
                    dst = ring[:, job_place(i), :]
                    if i < 16:
                        w = (w_gate if i < 8 else w_up)[bass.ds(e, 1)].rearrange("e k f -> (e k) f")
                        src = w[(i % 8) * 2 * P:(i % 8 + 1) * 2 * P, :].rearrange("(k p) f -> p k f", p=P)
                        dst = dst.rearrange("p (k f) -> p k f", k=2)
                    else:
                        w = w_down[bass.ds(e, 1)].rearrange("e k f -> (e k) f")
                        src = w[(i - 16) * P:(i - 15) * P, :]
                    sp.dma_start(dst, src).then_inc(landed[job_place(i)], 16)
            for q in (0, 1, 3, 2):
                if q == 3:
                    sp.wait_ge(last_part, 2)
                else:
                    sp.wait_ge(out_ready, q + 1)
                t, h = q // 2, q % 2
                sp.dma_start(out[t * P:(t + 1) * P, h * 1024:(h + 1) * 1024],
                             tokens[:, t, h * 1024:(h + 1) * 1024]).then_inc(out_sent, 16)
            sp.wait_ge(out_sent, 64)

        @block.gpsimd
        def _(pool):
            pool.memset(silu_c[:], 0.0).then_inc(zeroed, 1)
            pool.memset(yT[:], 0.0).then_inc(zeroed, 1)
            pool.memset(small[:, 63:64], 0.0).then_inc(slot_free, PRE_SLOTS)
            pool.memset(small[:, 61:62], 0.0).then_inc(summed, 4)
            pool.dma_start(heads[:, 0:ALL_COLS - CONST_COLS], consts[:, CONST_COLS:ALL_COLS]).then_inc(misc_in, 16)
            for dst, v in ((qk_gain[:, 0, :], q_norm_g), (qk_gain[:, 1, :], k_norm_g), (sink[:], attn_sink)):
                pool.dma_start(dst, v.broadcast_to([P, v.shape[1]])).then_inc(misc_in, 16)
            for b in range(4):
                pool.wait_ge(scale_done, b + 1)
                for k in range(4 * b, 4 * b + 4):
                    pool.tensor_scalar(nT[:, k, SEQ:2 * SEQ], nT[:, k, SEQ:2 * SEQ], scale_mix[:, k, 1:2],
                                       modcol[:, 0, k, 1:2], ALU.mult, ALU.add).then_inc(nC_ready, 1)
            for dst, v in ((rbias[:], router_bias), (gm_gb[:, 0, :], gmlp_ln_g), (gm_gb[:, 1, :], gmlp_ln_b)):
                pool.dma_start(dst, v.broadcast_to([P, v.shape[1]])).then_inc(wr_in, 16)
            pool.dma_start(wr[:], w_router.rearrange("(k p) e -> p k e", p=P)).then_inc(wr_in, 16)

            def start_half(i):
                pool.wait_ge(half_free, i + 1)
                pool.memset(halves[:, i % 2, :], 0.0).then_inc(half_zero, 1)
                pool.wait_ge(half_zero, i + 1)
                col = 2 * D + i * HALF
                pool.dma_start(halves[0:1, i % 2, :], b_mod[:, col:col + HALF]).then_inc(bias_in, 16)

            def load_rows(m):
                if m % KT == 0:
                    start_half(m // KT)
                pool.wait_ge(half_step, m + 1)
                col = 2 * D + m // KT * HALF
                pool.dma_start(half_slots[:, m % HALF_SLOTS, :], w_mod[m % KT * P:(m % KT + 1) * P, col:col + HALF]) \
                    .then_inc(half_in[m % HALF_SLOTS], 16)

            pool.memset(small[:, 60:61], 0.0).then_inc(half_free, 2)
            pool.memset(small[:, 59:60], 0.0).then_inc(half_step, HALF_SLOTS)
            for m in range(HALF_SLOTS):
                load_rows(m)
            for m in range(FIRST):
                if m == 0:
                    pool.wait_ge(bias_in, 16)
                pool.wait_ge(half_scaled, m + 1)
                total = halves[:, 0, :]
                pool.tensor_tensor(total, total, half_slots[:, m % HALF_SLOTS, :], ALU.add).then_inc(half_step, 1)
                pool.wait_ge(half_step, HALF_SLOTS + m + 1)
                load_rows(m + HALF_SLOTS)
            for m in range(FIRST + HALF_SLOTS, 5 * KT):
                load_rows(m)
            pool.wait_ge(slot_free, used(U_))
            pool.memset(nT_all[:, 0:TT * D], 0.0).then_inc(y_zeroed, 1)
            for m in range(5 * KT, 6 * KT):
                load_rows(m)
            for i in (6, 7):
                start_half(i)
            pool.wait_ge(y_done, 1)
            pool.wait_ge(bcast_saved, 8)
            y, o = yacc[:, 1, 1, :], tokens[:, 1, 1024:2048]
            pool.tensor_tensor(y, y, gate_b[:, 1024:2048], ALU.mult).then_inc(last_part, 1)
            pool.wait_ge(last_part, 1)
            pool.tensor_tensor(o, o, y, ALU.add).then_inc(last_part, 1)

        @block.tensor
        def _(pe):
            pe.wait_ge(const_in, 16)
            pe.wait_ge(rows_in, 16 * 8)
            pe.transpose(S[0][:, 0:108], rows[:], ident[0:108, 0:108]).then_inc(rowsT_done, 1)
            pe.wait_ge(silu_done, 1)

            for step in SCHEDULE:
                kind = step[0]
                n = NUMBER.get(step if kind != "win" else (kind, step[1], step[2] // 4 * 4))
                if n is not None:
                    pe.wait_ge(landed[place(n)], 16 * len(range(n, -1, -PRE_SLOTS)))
                if kind == "mod":
                    b, p, c4 = step[1:]
                    if c4 == 0:
                        if b:
                            pe.wait_ge(modcol_saved, 2 * b + p - 1)
                        elif p:
                            pe.wait_ge(wsT_saved, 1)
                    for i in range(4):
                        mm = pe.matmul((T if p else M)[32 * i:32 * i + 32, :], silu_c[:, 4 * c4 + i, :],
                                       slot(n)[:, i * N:(i + 1) * N], start=(c4 == 0), stop=(c4 == 3))
                    mm.then_inc(slot_free, 1)
                elif kind == "ext":
                    b, p = step[1:]
                    pe.wait_ge(row_saved, 2 * b + p + 1)
                    for q in range(4):
                        mm = pe.matmul((T if p else M)[:, 2 * q:2 * q + 2], modrow[:, p, q * P:(q + 1) * P],
                                       k_("sel"), start=True, stop=True)
                    mm.then_inc(ext_done, 1)
                elif kind == "setup":
                    pe.wait_ge(setup_in, 16 * 3)
                    for q in range(4):
                        pe.transpose(S[1][:, q * 32:q * 32 + 32], conv_rows[:, q * P:(q + 1) * P], ident[0:32, 0:32])
                    for h in range(4):
                        mm = pe.transpose(T[:, h * P:(h + 1) * P], w_s[:, h, :], ident)
                    mm.then_inc(setupT_done, 1)
                elif kind == "tok":
                    t = step[1]
                    pe.wait_ge(scaled, t + 1)
                    for q in range(4):
                        if t >= 1:
                            pe.wait_ge(tokT_act if q % 2 else tokT_dve, 2 * (t - 1) + q // 2 + 1)
                        for i in range(4):
                            k = 4 * q + i
                            mm = pe.transpose(Z[q][:, i * P:(i + 1) * P], early[:, t % 2, k * P:(k + 1) * P], ident)
                        mm.then_inc(tokT_done, 1)
                elif kind == "half":
                    i = step[1]
                    pe.wait_ge(half_step, HALF_SLOTS + KT * (i + 1))
                    if i == 0:
                        pe.wait_ge(modcol_saved, 8)
                    else:
                        pe.wait_ge(half_saved, i)
                    if i == 3:
                        pe.wait_ge(bcast_saved, 4)
                    if i < 2:
                        for r in range(2):
                            b = 2 * (i % 2) + r
                            mm = pe.matmul(M[32 * b:32 * b + 32, :], ones[:, 0:32],
                                           halves[:, i % 2, r * N:(r + 1) * N], start=True, stop=True)
                    else:
                        for q in range(8):
                            mm = pe.matmul(M[:, q:q + 1], halves[:, i % 2, q * P:(q + 1) * P], ones[:, 0:1],
                                           start=True, stop=True)
                    mm.then_inc(half_free, 1)
                elif kind == "gate":
                    k = step[1]
                    for i in range(4):
                        mm = pe.matmul(C[1][32 * i:32 * i + 32, :], silu_c[:, k, :], slot(n)[:, i * N:(i + 1) * N],
                                       start=(k == 0), stop=False)
                    mm.then_inc(slot_free, 1)
                    if k == KT - 1:
                        pe.wait_ge(bias_in, 16 * 8)
                        for i in range(4):
                            mm = pe.matmul(C[1][32 * i:32 * i + 32, :], ones[:, 0:32],
                                           halves[:, i // 2, (i % 2) * N:(i % 2 + 1) * N], start=False, stop=True)
                        mm.then_inc(gate_done, 1)
                elif kind == "bcast":
                    i = step[1]
                    if i == 0:
                        pe.wait_ge(half_saved, 3)
                    else:
                        pe.wait_ge(bcast_saved, i)
                    pe.matmul(M, k_("spread")[:, i * P:(i + 1) * P], modrow[:, 0, :], start=True, stop=True) \
                        .then_inc(bcast_done, 1)
                elif kind == "win":
                    g, k = step[1:]
                    if k == 0:
                        if g == A_:
                            pe.wait_ge(tokT_act, 8)
                            pe.wait_ge(tokT_dve, 8)
                        elif g == Q0_:
                            pe.wait_ge(cols_saved, 1)
                            pe.wait_ge(convc_saved, 1)
                            pe.wait_ge(silu_done, 1)
                        elif g == KV_:
                            pe.wait_ge(a_saved, 1)
                            pe.wait_ge(g_saved, 1)
                        elif g == Q1_:
                            pe.wait_ge(headT_saved, 1)
                        elif g == V_:
                            pe.wait_ge(qk_read, 2)
                            pe.wait_ge(v_saved, 2)
                        elif g == U_:
                            pe.wait_ge(headT_saved, 3)
                    b = pair[g]
                    w = slot(n).rearrange("p (k n) -> p k n", k=4)[:, k % 4, :]
                    if g == A_:
                        pe.wait_ge(nT_ready, k + 1)
                    if g in (A_, G_):
                        for q in range(4):
                            mm = pe.matmul(Z[b + q // 2][:, (q % 2) * SEQ:(q % 2 + 1) * SEQ],
                                           w[:, q * P:(q + 1) * P], nT[:, k, 0:SEQ],
                                           start=(k == 0 and q % 2 == 0), stop=(k == KT - 1),
                                           skip_group_check=True)
                    else:
                        for t in range(TT):
                            mm = pe.matmul(ps[:, b + t, :], nT[:, k, t * P:(t + 1) * P], w,
                                           start=(k == 0), stop=(k == KT - 1))
                    if g == KV_:
                        pe.wait_ge(nC_ready, k + 1)
                        for t in range(TT):
                            mm = pe.matmul(C[t], nT[:, k, SEQ + t * P:SEQ + (t + 1) * P], w,
                                           start=(k == 0), stop=(k == KT - 1))
                    if k % 4 == 3:
                        mm.then_inc(slot_free, 1)
                elif kind == "convsum":
                    pe.wait_ge(conv_done, 1)
                    pe.wait_ge(modcol_saved, 8)
                    for q in range(4):
                        mm = pe.matmul(T[:, 0:SEQ], ones, acc[:, q, :], start=(q == 0), stop=(q == 3))
                    mm.then_inc(csum_done, 1)
                elif kind == "convsq":
                    pe.wait_ge(csq_saved, 1)
                    for q in range(4):
                        mm = pe.matmul(T[:, SEQ:2 * SEQ], ones, aT[:, q, :], start=(q == 0), stop=(q == 3))
                    mm.then_inc(csq_done, 1)
                elif kind == "kT":
                    pe.wait_ge(rope_done, 2)
                    pe.wait_ge(v_saved, 2)
                    for t in range(2 * TT):
                        for h in range(NKV):
                            mm = pe.transpose(C[t // 2][:, h * SEQ + (t % 2) * P:h * SEQ + (t % 2 + 1) * P],
                                              heads[:, t * SEQ + h * HD:t * SEQ + (h + 1) * HD], ident)
                    mm.then_inc(headT_done, 1)
                elif kind == "qT":
                    pe.wait_ge(rope_done, 3 if step[1] else 1)
                    for t in range(TT):
                        for h in range(4):
                            mm = pe.transpose(S[t][:, h * P:(h + 1) * P],
                                              heads[:, t * N + h * HD:t * N + (h + 1) * HD], ident)
                    mm.then_inc(headT_done, 1)
                elif kind == "head":
                    h, part = step[1:]
                    kv = h // (NH // NKV)
                    if part == 0:
                        if h == 0:
                            pe.wait_ge(headT_saved, 2)
                        if h == 4:
                            pe.wait_ge(headT_saved, 3)
                        for t in range(TT):
                            if h:
                                pe.wait_ge(pv_saved if t else pT1_saved, h)
                            pe.matmul(C[t], qT[:, h, t * P:(t + 1) * P], kT[:, kv, :], start=True, stop=True)
                            mm = pe.matmul(C[t][:, (1 - t) * P:(2 - t) * P], ident, k_(f"mask{t}"),
                                           start=False, stop=True, skip_group_check=True)
                        mm.then_inc(score_done, 1)
                    elif part == 1:
                        pe.wait_ge(probs_done, h + 1)
                        if h == 0:
                            pe.wait_ge(cnorm, 1)
                        if h:
                            pe.wait_ge(pT0_saved, h)
                        for t in range(TT):
                            for q in range(4):
                                mm = pe.transpose((C[0] if t else T)[:, q * P:(q + 1) * P],
                                                  probs[:, t, q * P:(q + 1) * P], ident)
                            mm.then_inc(pT_done, 1)
                    else:
                        pe.wait_ge(pT0_saved, h + 1)
                        pe.wait_ge(pT1_saved, h + 1)
                        for q in range(4):
                            mm = pe.matmul(C[1][:, 0:SEQ], vtok[:, q, kv * HD:(kv + 1) * HD], probsT[:, q, :],
                                           start=(q == 0), stop=(q == 3))
                        mm.then_inc(pv_done, 1)
                elif kind == "spatial":
                    pe.wait_ge(v_ready, 1)
                    pe.wait_ge(pT0_saved, NH)
                    pe.wait_ge(pT1_saved, NH)
                    for t in range(TT):
                        for h in range(4):
                            mm = pe.matmul((C[0] if t else T)[:, h * P:(h + 1) * P], w_sT[:, h, :],
                                           vbuf[:, t, h * HD:(h + 1) * HD], start=True, stop=True)
                    mm.then_inc(spatial_done, 1)
                elif kind == "gated":
                    pe.wait_ge(gated, 1)
                    for t in range(TT):
                        for h in range(4):
                            mm = pe.transpose((C[0] if t else T)[:, h * P:(h + 1) * P],
                                              ubuf[:, t, h * HD:(h + 1) * HD], ident)
                    mm.then_inc(gatedT_done, 1)
                elif kind == "wout":
                    g, c4 = step[1:]
                    b = 4 if g % 2 else 0
                    if c4 == 0:
                        if g == 0:
                            pe.wait_ge(gelu_v, 1)
                            pe.wait_ge(pv_saved, NH)
                        elif g == 1:
                            pe.wait_ge(gelu_u, 1)
                        else:
                            pe.wait_ge(h_ready, g - 1)
                    if g == 0 and c4 == 2:
                        pe.wait_ge(gatedT_saved, 1)
                    if g == 0 and c4 == 3:
                        pe.wait_ge(conv_saved, 1)
                    for i in range(4):
                        k = 4 * c4 + i
                        w = slot(n).rearrange("p (k n) -> p k n", k=4)[:, i, :]
                        for t in range(TT):
                            mm = pe.matmul(ps[:, b + t, :], mixT[:, k, t * P:(t + 1) * P], w,
                                           start=(k == 0), stop=(k == KT - 1))
                    mm.then_inc(slot_free, 1)
                elif kind == "hT":
                    g = step[1]
                    pe.wait_ge(h_ready, g + 1)
                    if g:
                        pe.wait_ge(hT_saved, g)
                    else:
                        pe.wait_ge(gatedT_saved, 1)
                    for t in range(TT):
                        for i in range(4):
                            k = 4 * g + i
                            mm = pe.transpose((T if t else C[0])[:, i * P:(i + 1) * P],
                                              tokens[:, t, k * P:(k + 1) * P], ident)
                    mm.then_inc(hT_done, 1)
                elif kind == "shift":
                    pe.wait_ge(wr_ready, 1)
                    pe.wait_ge(h_ready, 3)
                    for k in range(KT):
                        mm = pe.matmul(Z[0][0:1, 0:NE], modcol[:, 3, k, 0:1], wr[:, k, :],
                                       start=(k == 0), stop=(k == KT - 1))
                    mm.then_inc(shift_done, 1)
                elif kind == "shift_rows":
                    pe.wait_ge(rbias_row, 1)
                    pe.matmul(Z[1][:, 0:NE], ones[0:1, :], rrow[:], start=True, stop=True).then_inc(shift_done, 1)
                elif kind == "logits":
                    g = step[1]
                    pe.wait_ge(hT_saved, g + 1)
                    pe.wait_ge(half_saved, 6)
                    for k in range(4 * g, 4 * g + 4):
                        for t in range(TT):
                            mm = pe.matmul(M[:, t * NE:(t + 1) * NE], hrT[:, k, t * P:(t + 1) * P],
                                           wr_scaled[:, k, :], start=(k == 0 and t == 0), stop=(k == KT - 1),
                                           skip_group_check=True)
                    if g == 3:
                        mm.then_inc(logit_done, 1)
                elif kind == "route":
                    part = step[1]
                    if part == 1:
                        pe.wait_ge(mask_ready, 1)
                        mask = rt[:, 15]
                        pe.matmul(T[:, 0:NE], k_("before"), mask[:, 0, :], start=True, stop=True)
                        pe.matmul(T[:, NE:2 * NE], ones, mask[:, 0, :], start=True, stop=False)
                        pe.matmul(T[:, NE:2 * NE], k_("before"), mask[:, 1, :], start=False, stop=True)
                        for t in range(TT):
                            mm = pe.matmul(T[0:CAND, 128:129], cand[:, t, 0, :], ones[:, 0:1],
                                           start=(t == 0), stop=(t == TT - 1))
                        mm.then_inc(pos_done, 1)
                    elif part == 2:
                        pe.wait_ge(count_saved, 1)
                        pe.matmul(T[0:CAND, 0:2], k_("before")[0:CAND, 0:CAND], vcol[:, 0:2],
                                  start=True, stop=True)
                        pe.matmul(T[0:CAND, 2:4], ones[0:CAND, 0:CAND], vcol[:, 0:2], start=True, stop=True) \
                            .then_inc(order_done, 1)
                        pe.wait_ge(cand_ready, 1)
                        for t in range(TT):
                            for i in range(2):
                                mm = pe.transpose(C[0][0:CAND, (2 * t + i) * P:(2 * t + i + 1) * P],
                                                  cand[:, t, i, :], ident)
                        mm.then_inc(candT_done, 1)
                    else:
                        pe.wait_ge(table_oh, 2)
                        for i in range(2):
                            for t in range(TT):
                                at = (i * TT + t) * JOBS
                                pe.matmul(Z[0][:, at:at + JOBS], candT[:, t, i, :], onehot_j[:],
                                          start=True, stop=True)
                        pe.matmul(Z[0][0:1, 256:256 + JOBS], k_("expert")[0:CAND, :], onehot_j[:],
                                  start=True, stop=True)
                        pe.matmul(Z[0][0:1, 256 + JOBS:256 + 2 * JOBS], vcol[:, 1:2], onehot_j[:],
                                  start=True, stop=True).then_inc(table_done, 1)

            def gather(half):
                for k in range(8 * half, 8 * half + 8):
                    for t in range(TT):
                        mm = pe.matmul(Xb[:, k // 4, (k % 4) * BLK:(k % 4 + 1) * BLK],
                                       tokens[:, t, k * P:(k + 1) * P], oh_in[:, t, :],
                                       start=(t == 0), stop=(t == TT - 1))
                mm.then_inc(gathered, 1)

            def experts(j, wide):
                def arrived(i):
                    at = job_place(i)
                    before = sum(place(n) == at for n in range(NPRE))
                    pe.wait_ge(landed[at], j * (16 * JCH // SLOTS) + 16 * (before + i // SLOTS + 1))
                    return ring[:, at, :]

                pe.wait_ge(xg_ready, j + 1)
                for m, out_b in ((0, Gb), (1, Ub)):
                    if m == 1:
                        pe.wait_ge(bcast_saved, 8)
                    for i in range(8):
                        w = arrived(8 * m + i).rearrange("p (k f) -> p k f", k=2)
                        for kk in range(2):
                            k = 2 * i + kk
                            for f in range(2):
                                mm = pe.matmul(out_b[0][BASE * f:BASE * (f + 1), :], xg[:, k, 0:BASE],
                                               w[:, kk, f * N:(f + 1) * N], start=(k == 0), stop=(k == KT - 1))
                        for kk in range(2 * wide):
                            k = 2 * i + kk
                            for f in range(4):
                                mm = pe.matmul(out_b[1][REST * f:REST * (f + 1), :], xg[:, k, BASE:BLK],
                                               w[:, kk, f * 256:(f + 1) * 256], start=(k == 0), stop=(k == KT - 1))
                        mm.then_inc(slot_free, 1)
                pe.wait_ge(oh_ready, j + 2)
                pe.wait_ge(summed, j * 4 + 4)
                gather(0)
                pe.wait_ge(hidden_ready, j + 1)
                for i in range(1 + wide):
                    for q in range(4 // (i + 1)):
                        pe.transpose(Gb[i][:, q * P:(q + 1) * P], hidden[i][:, q * P:(q + 1) * P], ident)
                for t in range(TT):
                    mm = pe.transpose(Ub[0][0:BLK, t * P:(t + 1) * P], oh_out[:, t, :], ident)
                mm.then_inc(ehT_done, 1)
                gather(1)
                pe.wait_ge(ehT_saved, j + 1)
                pe.wait_ge(spread_saved, j + 1)
                for i in range(8):
                    w = arrived(16 + i)
                    for q in (0, 2, 1, 3):
                        mm = pe.matmul(Db[0][BASE * (q // 2):BASE * (q // 2 + 1), q % 2, :],
                                       hT[0][:, (i % 4) * P + BASE * (i // 4):(i % 4) * P + BASE * (i // 4 + 1)],
                                       w[:, q * N:(q + 1) * N], start=(i == 0), stop=(i == 7))
                    for q in range(4 * wide):
                        mm = pe.matmul(Db[1][REST * q:REST * (q + 1), :],
                                       hT[1][:, (i % 2) * P + REST * (i // 2):(i % 2) * P + REST * (i // 2 + 1)],
                                       w[:, q * N:(q + 1) * N], start=(i == 0), stop=(i == 7))
                    mm.then_inc(slot_free, 1)
                pe.wait_ge(xg_ready, j + 2)
                rows_used = BLK if wide else BASE
                for t in range(TT):
                    for q in range(4):
                        if t == 0:
                            pe.wait_ge(o_dve if q % 2 else o_act, j * 2 + (q // 2 + 1))
                        elif q % 2 == 0:
                            pe.wait_ge(summed, j * 4 + (5 + q // 2))
                        mm = pe.matmul(Yb[:, q, :], spread_T[0:rows_used, t, :],
                                       outs[0:rows_used, q * N:(q + 1) * N], start=True, stop=True)
                        if q % 2:
                            mm.then_inc(scattered, 1)

            pe.wait_ge(table_ready, 1)
            jobs = pe.value_load(n_i[0:1, 2 * JOBS:2 * JOBS + 1], min_val=1, max_val=JOBS - 1)
            pe.wait_ge(oh_ready, 1)
            gather(0)
            gather(1)
            for i in range(4):
                if i == 0:
                    pe.wait_ge(gate_saved, 1)
                elif i > 1:
                    pe.wait_ge(bcast_saved, 3 + i)
                pe.matmul(C[i % 2], k_("spread")[:, i * P:(i + 1) * P], modrow[:, 0, :], start=True, stop=True) \
                    .then_inc(bcast_done, 1)
            with pe.Fori(0, jobs) as j:
                wide = pe.value_load(n_i[0:1, bass.ds(j + JOBS, 1)], min_val=0, max_val=1)
                with pe.If(wide):
                    experts(j, True)
                with pe.Else():
                    experts(j, False)

        @block.scalar
        def _(act):
            copy = nc.scalar.copy

            for i, v in enumerate((c, c_ctx, norm_mix_g, norm_ffn_g)):
                act.dma_start(rows[KT * i:KT * (i + 1), :], v).then_inc(rows_in, 16)
            for t in range(2 * TT):
                act.dma_start(tokens[:, t, :], (x if t < TT else ctx)[(t % TT) * P:(t % TT + 1) * P, :]) \
                    .then_inc(tok_in if t < TT else ctx_in, 16)
            act.wait_ge(zeroed, 1)
            act.wait_ge(rowsT_done, 1)
            act.activation(silu_c[:, :, 0:2], S[0][:, 0:32].rearrange("p (r k) -> p k r", r=2), ACT.Silu) \
                .then_inc(silu_done, 1)
            for t in range(2 * TT):
                if t == TT:
                    act.wait_ge(setupT_done, 1)
                    copy(w_sT[:].rearrange("p h q -> p (h q)"), T).then_inc(wsT_saved, 1)
                if t % TT == 0:
                    act.wait_ge(ctx_in if t else tok_in, 16 * TT)
                nowhere = ring[:, PRE_SLOTS + t % TT, :] if t >= TT else nT_all[:, t * D:(t + 1) * D]
                act.activation(nowhere, tokens[:, t, :], ACT.Square,
                               accum_out=ss[:, t:t + 1]).then_inc(sumsq_done, 1)

            def save_tokT(t):
                for q in (1, 3):
                    act.wait_ge(tokT_done, 4 * t + q + 1)
                    copy(nT[:, 4 * q:4 * q + 4, t * P:(t + 1) * P], Z[q].rearrange("p (k t) -> p k t", k=4)) \
                        .then_inc(tokT_act, 1)

            def save_rows(b, p):
                act.wait_ge(slot_free, used_chunk(NUMBER["mod", b, p, 3]))
                copy(modrow[:, p, :], T if p else M).then_inc(row_saved, 1)

            save_tokT(0)
            save_tokT(1)
            save_rows(0, 0)
            save_tokT(2)
            save_tokT(3)
            save_rows(0, 1)
            for b in range(1, 4):
                for p in range(2):
                    act.wait_ge(ext_done, 2 * b - 1 + p)
                    save_rows(b, p)
            act.wait_ge(slot_free, used(A_))
            copy(bufA[:], ps[:, 0:2, :]).then_inc(a_saved, 1)
            act.wait_ge(slot_free, used(G_))
            act.activation(bufB[:], ps[:, 2:4, :], ACT.Sigmoid).then_inc(g_saved, 1)

            def squares(idx, bank):
                if idx:
                    act.wait_ge(rope_done, idx)
                act.activation(work[:].rearrange("p (t n) -> p t n", t=TT), ps[:, bank:bank + 2, :], ACT.Square) \
                    .then_inc(sq_saved, 1)

            def save_half(i):
                act.wait_ge(half_free, i + 3)
                if i < 2:
                    at = 64 * (i % 2)
                    copy(modrow[at:at + 64, 0, :], M[at:at + 64, :]).then_inc(half_saved, 1)
                else:
                    at = 8 * (i % 2)
                    copy(modcol[:, 2 + i // 2, at:at + 8, 0], M[:, 0:8]).then_inc(half_saved, 1)

            act.wait_ge(slot_free, used(Q0_))
            act.wait_ge(setupT_done, 1)
            squares(0, 4)
            for m in range(FIRST):
                act.wait_ge(half_in[m % HALF_SLOTS], 16 * (m // HALF_SLOTS + 1))
                rows_m = half_slots[:, m % HALF_SLOTS, :]
                act.activation(rows_m, rows_m, ACT.Copy, scale=silu_c[:, m % KT, 0:1]).then_inc(half_scaled, 1)

            def save_qT(g):
                act.wait_ge(headT_done, 3 if g else 1)
                for t in range(TT):
                    last = copy(qT[:, 4 * g:4 * g + 4, t * P:(t + 1) * P], S[t].rearrange("p (h t) -> p h t", h=4))
                last.then_inc(headT_saved, 1)

            save_qT(0)
            act.wait_ge(slot_free, used(KV_))
            act.wait_ge(rope_done, 1)
            w4 = work[:].rearrange("p (t n) -> p t n", t=2 * TT)
            act.activation(w4, ps[:, 0:4, 0:SEQ], ACT.Square).then_inc(sq_saved, 1)
            copy(vtok[:, 0:2], ps[:, 0:2, SEQ:N]).then_inc(v_saved, 1)
            copy(vtok[:, 2:4], ps[:, 2:4, SEQ:N]).then_inc(v_saved, 1)
            act.wait_ge(centred, 1)
            act.activation(bufA[:], bufB[:], ACT.Square).then_inc(csq_saved, 1)
            save_half(0)
            act.wait_ge(headT_done, 2)
            copy(kT[:, :, 0:SEQ], C[0].rearrange("p (h t) -> p h t", h=NKV))
            copy(kT[:, :, SEQ:N], C[1].rearrange("p (h t) -> p h t", h=NKV)).then_inc(headT_saved, 1)
            act.wait_ge(cnorm, 1)
            for q in range(4):
                last = act.activation(mixT[:, 12 + q, :], acc[:, q, :], ACT.Silu, bias=cv_b[:, q:q + 1],
                                      scale=cv_g[:, q:q + 1])
            last.then_inc(conv_saved, 1)
            def exps(h):
                act.wait_ge(neg_max, h + 1)
                if h:
                    act.wait_ge(pT_done, 2 * h)
                for t in range(TT):
                    act.activation(probs[:, t, :], C[t], ACT.Exp, bias=small[:, 2 + t:3 + t], scale=HD ** -0.5,
                                   accum_out=small[:, 4 + t:5 + t]).then_inc(exp_done, 1)
                for t in range(TT):
                    act.activation(small[:, 6 + t:7 + t], sink[:, h:h + 1], ACT.Exp, bias=small[:, 2 + t:3 + t]) \
                        .then_inc(exp_done, 1)

            def save_pT(h):
                if h:
                    act.wait_ge(pv_done, h)
                for t in range(TT):
                    act.wait_ge(pT_done, 2 * h + t + 1)
                    copy(probsT[:, :, t * P:(t + 1) * P], (C[0] if t else T).rearrange("p (k t) -> p k t", k=4)) \
                        .then_inc(pT1_saved if t else pT0_saved, 1)

            def save_pv(h):
                act.wait_ge(pv_done, h + 1)
                copy(mixT[:, h, :], C[1][:, 0:SEQ]).then_inc(pv_saved, 1)

            for h in range(NH):
                exps(h)
                if h == 1:
                    act.wait_ge(slot_free, used(Q1_))
                    squares(2, 4)
                if h == 3:
                    save_qT(1)
                if h == 5:
                    act.wait_ge(slot_free, used(V_))
                    act.activation(bufA[:], ps[:, 0:2, :], ACT.Gelu_apprx_tanh).then_inc(gelu_v, 1)
                if h in (2, 5):
                    save_half(h // 3 + 1)
                save_pT(h)
                save_pv(h)
            act.wait_ge(slot_free, used(U_))
            act.activation(bufB[:], ps[:, 4:6, :], ACT.Gelu_apprx_tanh).then_inc(gelu_u, 1)
            for i in range(4):
                act.wait_ge(bcast_done, i + 1)
                copy(gate_b[:, i * N:(i + 1) * N], M).then_inc(bcast_saved, 1)
            act.wait_ge(gatedT_done, 1)
            for t in range(TT):
                last = copy(mixT[:, 8:12, t * P:(t + 1) * P], (C[0] if t else T).rearrange("p (h t) -> p h t", h=4))
            last.then_inc(gatedT_saved, 1)
            save_half(3)
            for g in range(4):
                act.wait_ge(h_ready, g + 1)
                if g:
                    act.wait_ge(hsq_done, 2 * g)
                for t in range(TT):
                    act.activation(probs[:, t, :], tokens[:, t, g * N:(g + 1) * N], ACT.Square,
                                   accum_out=hsq[:, t, g:g + 1]).then_inc(hsq_done, 1)
                act.wait_ge(hT_done, g + 1)
                for t in range(TT):
                    last = copy(hrT[:, 4 * g:4 * g + 4, t * P:(t + 1) * P],
                                (T if t else C[0]).rearrange("p (k t) -> p k t", k=4))
                last.then_inc(hT_saved, 1)
                if g in (0, 2):
                    save_half(4 + g // 2)
            act.wait_ge(logit_saved, 1)
            act.activation(rt[:, 1], rt[:, 0], ACT.Sigmoid).then_inc(score_saved, 1)
            act.wait_ge(table_ready, 1)
            jobs = act.value_load(n_i[0:1, 2 * JOBS:2 * JOBS + 1], min_val=1, max_val=JOBS - 1)

            def save_tokens(half):
                for k in range(8 * half, 8 * half + 8):
                    last = act.activation(xg[:, k, :], Xb[:, k // 4, (k % 4) * BLK:(k % 4 + 1) * BLK], ACT.Identity,
                                          bias=modcol[:, 3, k, 0:1], scale=scale_ffn[:, k:k + 1])
                return last

            def job_evac(j, wide):
                act.wait_ge(slot_free, j * JCH + used_job(7))
                for i in range(1 + wide):
                    last = act.activation(silu_g[i], Gb[i], ACT.Silu)
                last.then_inc(silu_saved, 1)
                act.wait_ge(ehT_done, j + 1)
                for i in range(1 + wide):
                    last = copy(hT[i], Gb[i])
                last.then_inc(ehT_saved, 1)
                act.wait_ge(gathered, j * 2 + 3)
                save_tokens(0)
                act.wait_ge(gathered, j * 2 + 4)
                save_tokens(1).then_inc(xg_ready, 1)
                act.wait_ge(slot_free, j * JCH + used_job(23))
                save_outputs(act, copy, 0, wide)

            act.wait_ge(gate_done, 1)
            copy(modrow[:, 0, :], C[1]).then_inc(gate_saved, 1)
            act.wait_ge(gathered, 2)
            save_tokens(0)

            def save_gate(i):
                act.wait_ge(bcast_done, 5 + i)
                copy(gate_b[:, i * N:(i + 1) * N], C[i % 2]).then_inc(bcast_saved, 1)

            save_gate(0)
            save_gate(1)
            save_tokens(1).then_inc(xg_ready, 1)
            save_gate(2)
            save_gate(3)
            with act.Fori(0, jobs) as j:
                wide = act.value_load(n_i[0:1, bass.ds(j + JOBS, 1)], min_val=0, max_val=1)
                with act.If(wide):
                    job_evac(j, True)
                with act.Else():
                    job_evac(j, False)

        @block.vector
        def _(dve):
            tt, ts, stt = nc.vector.tensor_tensor, nc.vector.tensor_scalar, nc.vector.scalar_tensor_tensor

            def rsqrt(y, v, tmp):
                link(ts(y.bitcast(I32), v.bitcast(I32), 1, None, ALU.logical_shift_right))
                link(ts(y.bitcast(I32), y.bitcast(I32), -1.0, float(0x5F3759DF), ALU.mult, ALU.add))
                for _ in range(3):
                    link(tt(tmp, y, y, ALU.mult))
                    link(tt(tmp, tmp, v, ALU.mult))
                    link(ts(tmp, tmp, -0.5, 1.5, ALU.mult, ALU.add))
                    link(tt(y, y, tmp, ALU.mult))

            def save_tokT(t):
                for q in (0, 2):
                    dve.wait_ge(tokT_done, 4 * t + q + 1)
                    nc.vector.tensor_copy(nT[:, 4 * q:4 * q + 4, t * P:(t + 1) * P],
                                          Z[q].rearrange("p (k t) -> p k t", k=4)).then_inc(tokT_dve, 1)

            def save_modcol(b, p):
                at = slice(4 * b, 4 * b + 4)
                dve.wait_ge(ext_done, 2 * b + p + 1)
                tt(modcol[:, p, at], (T if p else M)[:, 0:8].rearrange("p (k r) -> p k r", r=2),
                   b_mix[:, p, at].unsqueeze(2).broadcast_to([P, 4, 2]), ALU.add).then_inc(modcol_saved, 1)

            half_count = [FIRST]

            def sum_rows(n):
                for m in range(half_count[0], half_count[0] + n):
                    if m % KT == 0:
                        dve.wait_ge(bias_in, 16 * (m // KT + 1))
                    dve.wait_ge(half_in[m % HALF_SLOTS], 16 * (m // HALF_SLOTS + 1))
                    dve.wait_ge(half_step, HALF_SLOTS + m)
                    total = halves[:, m // KT % 2, :]
                    stt(total, half_slots[:, m % HALF_SLOTS, :], silu_c[:, m % KT, 0:1], total, ALU.mult, ALU.add) \
                        .then_inc(half_step, 1)
                half_count[0] += n

            dve.wait_ge(silu_done, 1)
            nc.vector.tensor_copy(cols[:], S[0][:, 32:108]).then_inc(cols_saved, 1)
            for t in range(2 * TT):
                if t % TT == 0:
                    dve.wait_ge(sumsq_done, t + TT)
                    link(ts(stat[:, 0:2], ss[:, t:t + 2], 1.0 / D, EPS, ALU.mult, ALU.add))
                    rsqrt(rs_tok[:, t:t + 2], stat[:, 0:2], stat[:, 4:6])
                if t >= 2:
                    dve.wait_ge(tokT_done, 4 * (t - 1))
                ts(early[:, t % 2, :], tokens[:, t, :], rs_tok[:, t:t + 1], None, ALU.mult).then_inc(scaled, 1)
                if t:
                    save_tokT(t - 1)
            save_tokT(3)
            dve.wait_ge(setupT_done, 1)
            nc.vector.tensor_copy(conv_cols[:], S[1][:, 0:P].rearrange("p (q n) -> p q n", q=4)) \
                .then_inc(convc_saved, 1)
            save_modcol(0, 0)
            save_modcol(0, 1)
            for b in range(4):
                at = slice(4 * b, 4 * b + 4)
                dve.wait_ge(modcol_saved, 2 * b + 2)
                stt(scale_mix[:, at], modcol[:, 1, at], 1.0, mix_g[:, at].unsqueeze(2).broadcast_to([P, 4, 2]),
                    ALU.add, ALU.mult).then_inc(scale_done, 1)
                dve.wait_ge(scale_done, b + 1)
                if b == 0:
                    dve.wait_ge(tokT_act, 8)
                    dve.wait_ge(tokT_dve, 8)
                for k in range(4 * b, 4 * b + 4):
                    ts(nT[:, k, 0:SEQ], nT[:, k, 0:SEQ], scale_mix[:, k, 0:1], modcol[:, 0, k, 0:1],
                       ALU.mult, ALU.add).then_inc(nT_ready, 1)
                if b == 0:
                    dve.wait_ge(misc_in, 16 * 4)
                    link(ts(neg_sink[:], sink[:], -1.0, None, ALU.mult))
                    for i in range(2):
                        for t in range(TT):
                            g = qk_gain[:, i, :]
                            cs, sn = (k_(n)[:, t * HD:(t + 1) * HD] for n in ("cos", "sin"))
                            link(tt(rope[:, 2 * i, t, :], cs, g, ALU.mult))
                            for a, b in ((0, 64), (64, 0)):
                                link(tt(rope[:, 2 * i + 1, t, a:a + 64], sn[:, a:a + 64], g[:, b:b + 64], ALU.mult))
                if b < 3:
                    save_modcol(b + 1, 0)
                    save_modcol(b + 1, 1)
            def head_norm(idx):
                dve.wait_ge(sq_saved, idx + 1)
                link(nc.vector.tensor_reduce(ss[:], work[:].rearrange("p (h d) -> p h d", h=8), AX.X, ALU.add))
                link(ts(ss[:], ss[:], 1.0 / HD, EPS, ALU.mult, ALU.add))
                rsqrt(stat[:], ss[:], small[:, 8:16])

            def rotate(z, at, n_heads, table, t):
                shape = [P, n_heads, 64]
                zh = z.rearrange("p (h d) -> p h d", d=HD)
                o = heads[:, at:at + n_heads * HD].rearrange("p (h d) -> p h d", d=HD)
                w = work[:, at:at + n_heads * HD].rearrange("p (h d) -> p h d", d=HD)
                last = tt(o, zh, rope[:, table, t:t + 1, :].broadcast_to([P, n_heads, HD]), ALU.mult)
                for a, b in ((0, 64), (64, 0)):
                    last = tt(w[:, :, a:a + 64], zh[:, :, b:b + 64],
                              rope[:, table + 1, t:t + 1, a:a + 64].broadcast_to(shape), ALU.mult)
                return last

            def finish_heads(n):
                link(tt(heads[:, 0:n], heads[:, 0:n], work[:, 0:n], ALU.add))
                tt(heads[:].rearrange("p (h d) -> p h d", d=HD), heads[:].rearrange("p (h d) -> p h d", d=HD),
                   stat[:].unsqueeze(2).broadcast_to([P, 8, HD]), ALU.mult).then_inc(rope_done, 1)

            def rotate_q(idx, bank):
                if idx:
                    dve.wait_ge(headT_done, idx)
                for t in range(TT):
                    last = rotate(ps[:, bank + t, :], t * N, 4, 0, t)
                    if t == 0:
                        link(last)
                last.then_inc(qk_read, 1)
                dve.wait_ge(qk_read, idx + 1)
                finish_heads(1024)

            dve.wait_ge(g_saved, 1)
            dve.wait_ge(a_saved, 1)
            dve.wait_ge(zeroed, 2)
            link(tt(yT[:, :, PAD:PAD + SEQ], aT, acc, ALU.mult))
            for tap in range(CW):
                for q in range(4):
                    if tap:
                        dve.wait_ge(dve_step, dve_count[0] - 3)
                        ins = stt(acc[:, q, :], yT[:, q, tap:tap + SEQ], conv_cols[:, q, tap:tap + 1],
                                  acc[:, q, :], ALU.mult, ALU.add)
                    else:
                        ins = ts(acc[:, q, :], yT[:, q, 0:SEQ], conv_cols[:, q, 0:1],
                                 conv_cols[:, q, CW:CW + 1], ALU.mult, ALU.add)
                    ins.then_inc(dve_step, 1)
                    dve_count[0] += 1
            dve.wait_ge(dve_step, dve_count[0])
            ts(small[:, 32:33], small[:, 63:64], 1.0, None, ALU.mult).then_inc(conv_done, 1)
            head_norm(0)
            rotate_q(0, 4)
            sum_rows(6)
            dve.wait_ge(csum_done, 1)
            link(ts(bc[:, 0, :], T[:, 0:SEQ], 1.0 / N, None, ALU.mult))
            tt(acc, acc, bc[:, 0:1, :].broadcast_to([P, 4, SEQ]), ALU.subtract).then_inc(centred, 1)
            dve.wait_ge(centred, 1)

            head_norm(1)
            dve.wait_ge(headT_done, 1)
            dve.wait_ge(v_saved, 2)
            for t in range(TT):
                link(rotate(ps[:, t, 0:SEQ], t * SEQ, NKV, 2, t))
            for t in range(TT):
                last = tt(heads[:, N + t * SEQ:N + (t + 1) * SEQ].rearrange("p (h d) -> p h d", d=HD),
                          C[t][:, 0:SEQ].rearrange("p (h d) -> p h d", d=HD),
                          qk_gain[:, 1:2, :].broadcast_to([P, NKV, HD]), ALU.mult)
            last.then_inc(qk_read, 1)
            dve.wait_ge(qk_read, 2)
            finish_heads(N)
            dve.wait_ge(csq_done, 1)
            link(ts(bc[:, 0, :], T[:, SEQ:N], 1.0 / N, EPS, ALU.mult, ALU.add))
            rsqrt(bc[:, 1, :], bc[:, 0, :], bc[:, 2, :])
            tt(acc, acc, bc[:, 1:2, :].broadcast_to([P, 4, SEQ]), ALU.mult).then_inc(cnorm, 1)

            sum_rows(4)
            for h in range(NH):
                dve.wait_ge(score_done, h + 1)
                link(nc.vector.tensor_reduce(small[:, 0:2], ps[:, 2:4, :], AX.X, ALU.max))
                ts(small[:, 2:4], small[:, 0:2], -(HD ** -0.5), neg_sink[:, h:h + 1], ALU.mult, ALU.min) \
                    .then_inc(neg_max, 1)
                sum_rows(1)
                dve.wait_ge(exp_done, 4 * h + 4)
                link(tt(small[:, 4:6], small[:, 4:6], small[:, 6:8], ALU.add))
                link(nc.vector.reciprocal(small[:, 4:6], small[:, 4:6]))
                for t in range(TT):
                    last = ts(probs[:, t, :], probs[:, t, :], small[:, 4 + t:5 + t], None, ALU.mult)
                last.then_inc(probs_done, 1)
                if h == 1:
                    head_norm(2)
                elif h == 2:
                    rotate_q(2, 4)
                elif h == 6:
                    dve.wait_ge(wr_in, 16 * 4)
                    dve.wait_ge(gelu_v, 1)
                    for t in range(TT):
                        link(nc.vector.bn_stats(small[:, 16 + 6 * t:22 + 6 * t], vbuf[:, t, :]))
                        link(nc.vector.bn_aggr(small[:, 28 + 2 * t:30 + 2 * t], small[:, 16 + 6 * t:22 + 6 * t]))
                        link(ts(stat[:, t:t + 1], small[:, 29 + 2 * t:30 + 2 * t], EPS, None, ALU.add))
                    rsqrt(stat[:, 2:4], stat[:, 0:2], stat[:, 4:6])
                    for t in range(TT):
                        link(ts(vbuf[:, t, :], vbuf[:, t, :], small[:, 28 + 2 * t:29 + 2 * t], stat[:, 2 + t:3 + t],
                                ALU.subtract, ALU.mult))
                    link(tt(vbuf, vbuf, gm_gb[:, 0:1, :].broadcast_to([P, TT, N]), ALU.mult))
                    tt(vbuf, vbuf, gm_gb[:, 1:2, :].broadcast_to([P, TT, N]), ALU.add).then_inc(v_ready, 1)
                sum_rows((5, 3, 1, 5, 5, 5, 1, 5)[h])
                dve.wait_ge(probs_done, h + 1)
            dve.wait_ge(spatial_done, 1)
            for t in range(TT):
                last = tt(vbuf[:, t, :].rearrange("p (h d) -> p h d", h=4),
                          (C[0] if t else T).rearrange("p (h d) -> p h d", h=4),
                          b_s.unsqueeze(2).broadcast_to([P, 4, HD]), ALU.add)
            last.then_inc(mixed_saved, 1)
            dve.wait_ge(mixed_saved, 1)
            dve.wait_ge(gelu_u, 1)
            tt(bufB[:], bufB[:], bufA[:], ALU.mult).then_inc(gated, 1)
            for g in range(4):
                sum_rows((12, 12, 10, 0)[g])
                if g == 0:
                    dve.wait_ge(bcast_saved, 4)
                if g == 3:
                    dve.wait_ge(half_saved, 6)
                    link(stt(scale_ffn[:], modcol[:, 4, :, 0], 1.0, ffn_g, ALU.add, ALU.mult))
                    tt(wr_scaled[:], wr[:], scale_ffn[:].unsqueeze(2).broadcast_to([P, KT, NE]), ALU.mult) \
                        .then_inc(wr_ready, 1)
                    dve.wait_ge(shift_done, 1)
                    nc.vector.tensor_copy(rrow[:], Z[0][0:1, 0:NE]).then_inc(rbias_row, 1)
                dve.wait_ge(slot_free, used_out(g))
                b = 4 if g % 2 else 0
                for t in range(TT):
                    last = tt(work[:, t * N:(t + 1) * N], ps[:, b + t, :], gate_b[:, g * N:(g + 1) * N], ALU.mult)
                link(last)
                h_g = tokens[:, 0:TT, g * N:(g + 1) * N]
                tt(h_g, h_g, work[:].rearrange("p (t n) -> p t n", t=TT), ALU.add).then_inc(h_ready, 1)
            dve.wait_ge(shift_done, 2)
            link(nc.vector.tensor_copy(rt[:, 2, 0, :], Z[1][:, 0:NE]))
            dve.wait_ge(hsq_done, 8)
            link(nc.vector.tensor_reduce(stat[:, 0:2], hsq[:], AX.X, ALU.add))
            link(ts(stat[:, 0:2], stat[:, 0:2], 1.0 / D, EPS, ALU.mult, ALU.add))
            rsqrt(rs_tok[:, 0:2], stat[:, 0:2], stat[:, 2:4])
            rs2 = rs_tok[:, 0:2].unsqueeze(2).broadcast_to([P, TT, NE])
            dve.wait_ge(logit_done, 1)
            link(tt(rt[:, 0], M[:, 0:2 * NE].rearrange("p (t e) -> p t e", t=TT), rs2, ALU.mult))
            rb = rt[:, 2, 0:1, :]
            tt(rt[:, 0], rt[:, 0], rb.broadcast_to([P, TT, NE]), ALU.add).then_inc(logit_saved, 1)
            dve.wait_ge(score_saved, 1)
            scores, sel = rt[:, 1], rt[:, 3]
            link(tt(sel, scores, rbias[:].unsqueeze(1).broadcast_to([P, TT, NE]), ALU.add))
            v = sel.rearrange("p t (g a b) -> p (t g) a b", g=NG, a=2)

            def g8(i):
                return rt[:, i].rearrange("p t e -> p (t e)")[:, 0:16].rearrange("p (g a) -> p g a", a=2)

            def g1(i):
                return rt[:, i].rearrange("p t e -> p (t e)")[:, 0:8]

            hi, lo = g8(4), g8(5)
            link(tt(hi, v[:, :, :, 0], v[:, :, :, 1], ALU.max))
            link(tt(lo, v[:, :, :, 0], v[:, :, :, 1], ALU.min))
            link(tt(g1(6), hi[:, :, 0], hi[:, :, 1], ALU.max))
            link(tt(g1(7), hi[:, :, 0], hi[:, :, 1], ALU.min))
            link(tt(g1(8), lo[:, :, 0], lo[:, :, 1], ALU.max))
            link(tt(g1(7), g1(7), g1(8), ALU.max))
            link(tt(g1(6), g1(6), g1(7), ALU.add))

            def first_max(values, numbers, n, mx, eq, low, hot):
                shape = [P, TT, n]
                link(nc.vector.tensor_reduce(mx, values, AX.X, ALU.max))
                link(tt(eq, values, mx.unsqueeze(2).broadcast_to(shape), ALU.is_equal))
                link(tt(eq, eq, numbers.unsqueeze(1).broadcast_to(shape), ALU.mult))
                link(nc.vector.tensor_reduce(low, eq, AX.X, ALU.min))
                link(tt(hot, numbers.unsqueeze(1).broadcast_to(shape), low.unsqueeze(2).broadcast_to(shape),
                        ALU.is_equal))

            gsc = g1(6).rearrange("p (t g) -> p t g", t=TT)
            geq = g1(8).rearrange("p (t g) -> p t g", t=TT)
            ghot = g1(9).rearrange("p (t g) -> p t g", t=TT)
            first_max(gsc, k_("g4"), NG, small[:, 0:2], geq, small[:, 2:4], ghot)
            masked = rt[:, 10]
            link(ts(geq, ghot, BIG, -BIG, ALU.mult, ALU.add))
            m4 = masked.rearrange("p t (g e) -> p (t g) e", e=EPG)
            link(tt(m4, sel.rearrange("p t (g e) -> p (t g) e", e=EPG),
                    g1(9).unsqueeze(2).broadcast_to([P, 2 * NG, EPG]), ALU.mult))
            link(tt(m4, m4, g1(8).unsqueeze(2).broadcast_to([P, 2 * NG, EPG]), ALU.add))
            first_max(masked, k_("e16"), NE, small[:, 0:2], rt[:, 11], small[:, 2:4], rt[:, 12])
            link(ts(rt[:, 11], rt[:, 12], -3 * BIG, None, ALU.mult))
            link(tt(masked, masked, rt[:, 11], ALU.add))
            first_max(masked, k_("e16"), NE, small[:, 0:2], rt[:, 11], small[:, 2:4], rt[:, 13])
            mask, gates = rt[:, 15], rt[:, 14]
            link(tt(mask, rt[:, 12], rt[:, 13], ALU.add))
            for t in range(TT):
                last = nc.vector.tensor_copy(cand[:, t, 0, :].rearrange("p (b e) -> p b e", b=NBLK),
                                             rt[:, 15, t:t + 1, :].broadcast_to([P, NBLK, NE]))
            last.then_inc(mask_ready, 1)
            link(tt(gates, scores, mask, ALU.mult))
            link(nc.vector.tensor_reduce(small[:, 0:2], gates, AX.X, ALU.add))
            link(nc.vector.reciprocal(small[:, 2:4], small[:, 0:2]))
            link(tt(gates, gates, small[:, 2:4].unsqueeze(2).broadcast_to([P, TT, NE]), ALU.mult))
            dve.wait_ge(pos_done, 1)
            pos = rt[:, 16]
            link(ts(pos, T[:, 0:2 * NE].rearrange("p (t e) -> p t e", t=TT), 1.0, None, ALU.add))
            link(ts(vcol[:, 1:2], T[0:CAND, 128:129], k_("blk_lo")[0:CAND, :], float(BASE),
                    ALU.subtract, ALU.is_gt))
            ts(vcol[:, 0:1], T[0:CAND, 128:129], k_("blk_lo")[0:CAND, :], None, ALU.is_gt).then_inc(count_saved, 1)
            link(tt(pos, pos, mask, ALU.mult))
            link(ts(pos, pos, -1.0, None, ALU.add))
            lows = k_("cand_lo").rearrange("p (b e) -> p b e", b=NBLK)
            for t in range(TT):
                tt(cand[:, t, 0, :].rearrange("p (b e) -> p b e", b=NBLK),
                   rt[:, 16, t:t + 1, :].broadcast_to([P, NBLK, NE]), lows, ALU.subtract)
                last = nc.vector.tensor_copy(cand[:, t, 1, :].rearrange("p (b e) -> p b e", b=NBLK),
                                             rt[:, 14, t:t + 1, :].broadcast_to([P, NBLK, NE]))
            last.then_inc(cand_ready, 1)
            dve.wait_ge(order_done, 1)
            col = [vcol[:, i:i + 1] for i in range(8)]
            link(nc.vector.tensor_copy(vcol[:, 2:6], T[0:CAND, 0:4]))
            tt(col[6], col[2], col[3], ALU.subtract)
            link(tt(col[7], col[4], col[5], ALU.subtract))
            ts(col[2], col[3], 2.0, float(EARLY), ALU.mult, ALU.add)
            link(ts(col[4], col[6], 2.0 - EARLY, 0.0, ALU.add, ALU.max))
            tt(col[2], col[2], col[7], ALU.min)
            link(ts(col[4], col[4], 0.5, -0.25, ALU.mult, ALU.add))
            tt(col[2], col[2], col[3], ALU.add)
            link(ts(col[4], col[4], 2.0 ** 23, None, ALU.add))
            link(ts(col[4], col[4], 2.0 ** 23, col[5], ALU.subtract, ALU.min))
            link(tt(col[6], col[6], col[4], ALU.add))
            link(tt(col[7], col[2], col[6], ALU.subtract))
            link(ts(col[2], col[7], col[1], col[6], ALU.mult, ALU.add))
            link(nc.vector.tensor_copy(n_i[:, 2 * JOBS:2 * JOBS + 1], T[0:1, 2:3]))
            dve.wait_ge(count_saved, 1)
            ts(onehot_j[:], k_("jobno")[0:CAND, :], col[2], col[0], ALU.is_equal, ALU.mult) \
                .then_inc(table_oh, 1)
            dve.wait_ge(candT_done, 1)
            nc.vector.tensor_copy(candT.rearrange("c t i p -> c (t i p)"), C[0][0:CAND, :]).then_inc(table_oh, 1)
            dve.wait_ge(table_done, 1)
            link(nc.vector.tensor_copy(job.rearrange("p i t j -> p (i t j)"), Z[0][:, 0:4 * JOBS]))
            nc.vector.tensor_copy(n_i[:, 0:2 * JOBS], Z[0][0:1, 256:256 + 2 * JOBS]).then_inc(table_ready, 1)
            dve.wait_ge(table_ready, 1)

            def gather_matrix(j):
                for t in range(TT):
                    last = ts(oh_in[:, t, :], k_("slots"), job[:, 0, t, bass.ds(j, 1)], rs_tok[:, t:t + 1],
                              ALU.is_equal, ALU.mult)
                last.then_inc(oh_ready, 1)

            def spread_matrix(j):
                for t in range(TT):
                    last = ts(oh_out[:, t, :], k_("slots"), job[:, 0, t, bass.ds(j, 1)],
                              job[:, 1, t, bass.ds(j, 1)], ALU.is_equal, ALU.mult)
                return last

            def hidden_product(j, wide):
                dve.wait_ge(silu_saved, j + 1)
                dve.wait_ge(slot_free, j * JCH + used_job(15))
                for i in range(1 + wide):
                    last = tt(hidden[i], silu_g[i], Ub[i], ALU.mult)
                last.then_inc(hidden_ready, 1)
                dve.wait_ge(ehT_done, j + 1)
                nc.vector.tensor_copy(spread_T[0:BLK].rearrange("p t n -> p (t n)"), Ub[0][0:BLK, 0:SEQ]) \
                    .then_inc(spread_saved, 1)
                dve.wait_ge(slot_free, j * JCH + used_job(23))
                save_outputs(dve, nc.vector.tensor_copy, 1, wide)

            jobs = dve.value_load(n_i[0:1, 2 * JOBS:2 * JOBS + 1], min_val=1, max_val=JOBS - 1)
            gather_matrix(0)
            dve.wait_ge(y_zeroed, 1)
            with dve.Fori(0, jobs) as j:
                wide = dve.value_load(n_i[0:1, bass.ds(j + JOBS, 1)], min_val=0, max_val=1)
                dve.wait_ge(gathered, j * 2 + 2)
                gather_matrix(j + 1)
                spread_matrix(j)
                with dve.If(wide):
                    hidden_product(j, True)
                with dve.Else():
                    hidden_product(j, False)
                for t in range(TT):
                    for h in range(2):
                        dve.wait_ge(scattered, j * 4 + (2 * t + h + 1))
                        y = yacc[:, t, h, :]
                        tt(y, Yb[:, 2 * h:2 * h + 2, :].rearrange("p a n -> p (a n)"), y, ALU.add) \
                            .then_inc(summed, 1)
            dve.wait_ge(summed, jobs * 4 + 4)
            dve.wait_ge(bcast_saved, 8)
            ts(small[:, 33:34], small[:, 63:64], 1.0, None, ALU.mult).then_inc(y_done, 1)
            for q in range(3):
                t, h = q // 2, q % 2
                y = yacc[:, t, h, :]
                link(tt(y, y, gate_b[:, h * 1024:(h + 1) * 1024], ALU.mult))
                o = tokens[:, t, h * 1024:(h + 1) * 1024]
                tt(o, o, y, ALU.add).then_inc(out_ready, 1)


INPUTS = ["x", "c", "ctx", "c_ctx", "w_mod", "b_mod", "norm_mix_g", "norm_ffn_g", "w_in", "w_out",
          "q_norm_g", "k_norm_g", "attn_sink", "gmlp_ln_g", "gmlp_ln_b", "gmlp_w_s", "gmlp_b_s", "conv_w",
          "conv_b", "conv_ln_g", "conv_ln_b", "w_router", "router_bias", "w_gate", "w_up", "w_down"]
SHAPES = {"x": (SEQ, D), "ctx": (SEQ, D), "c": (16, P), "c_ctx": (16, P), "norm_mix_g": (16, P),
          "norm_ffn_g": (16, P), "gmlp_b_s": (4, P), "conv_ln_g": (4, P), "conv_ln_b": (4, P),
          "w_mod": (D, 6 * D), "b_mod": (1, 6 * D), "w_in": (D, 3584), "w_out": (D, D),
          "q_norm_g": (1, HD), "k_norm_g": (1, HD), "attn_sink": (1, NH), "gmlp_ln_g": (1, N),
          "gmlp_ln_b": (1, N), "gmlp_w_s": (4, P, P), "conv_w": (CW, N), "conv_b": (1, N),
          "w_router": (D, NE), "router_bias": (1, NE), "w_gate": (NE, D, FE), "w_up": (NE, D, FE),
          "w_down": (NE, FE, D)}


def kernel(**inputs):
    import concourse.bacc as bacc
    from concourse.bass_utils import run_bass_kernel_spmd

    nc = bacc.Bacc("TRN2", target_bir_lowering=False, num_devices=1)
    arrays, args = {}, []
    for name in INPUTS:
        a = np.ascontiguousarray(inputs[name]).reshape(SHAPES[name])
        arrays[name + "_dram"] = a
        args.append(nc.dram_tensor(name + "_dram", a.shape, F32, kind="ExternalInput").ap())
    _, _, tables = constants()
    table = np.concatenate([np.broadcast_to(v, (P, v.shape[1])) for v in tables.values()], 1).astype(np.float32)
    arrays["tables_dram"] = np.ascontiguousarray(table)
    args.append(nc.dram_tensor("tables_dram", table.shape, F32, kind="ExternalInput").ap())
    out = nc.dram_tensor("out_dram", (SEQ, D), F32, kind="ExternalOutput").ap()
    build(nc, *args, out)
    r = run_bass_kernel_spmd(nc, [arrays], core_ids=[0])
    return r.results[0]["out_dram"].reshape(1, SEQ, D)
```
